# Optimizing a Trainium2 kernel written in Bass

```python
import math
import jax, jax.numpy as jnp
from jax import lax
import numpy as np

D_MODEL = 1024
BATCH = 1
SEQ = 256
DEPTH = 2

GRID_W = 64
Q_BLOCK = 128
EPS = 1e-6

A_HEADS = 8
A_KV_HEADS = 2
A_GROUP = A_HEADS // A_KV_HEADS
A_HEAD_DIM = 64
AXIAL_THETA = 10000.0

B_HEADS = 8
B_QK_DIM = 32
B_V_DIM = 2 * B_QK_DIM
B_ROT_DIM = B_QK_DIM // 4
ROPE_THETA = 500000.0

C_HEADS = 8
C_Q_RANK = 384
C_KV_RANK = 256
C_NOPE_DIM = 64
C_ROPE_DIM = 32
C_V_DIM = 64
MLA_THETA = 10000.0

N_BRANCH = 3
BRANCH_W = 512
D_FF = 4 * D_MODEL

A_Q_W = A_HEADS * A_HEAD_DIM
A_KV_W = A_KV_HEADS * A_HEAD_DIM
B_QK_W = B_HEADS * 2 * B_QK_DIM
B_V_W = B_HEADS * B_V_DIM
GATE_W = N_BRANCH * D_MODEL
IN_SIZES = (A_Q_W, A_KV_W, A_KV_W, B_QK_W, B_QK_W, B_V_W, C_Q_RANK, C_KV_RANK, C_ROPE_DIM, GATE_W)
IN_COLS = A_Q_W + 2 * A_KV_W + 2 * B_QK_W + B_V_W + C_Q_RANK + C_KV_RANK + C_ROPE_DIM + GATE_W


def _rms_norm(x, g):
    xf = x.astype(jnp.float32)
    y = xf * lax.rsqrt(jnp.mean(xf * xf, axis=-1, keepdims=True) + EPS)
    return (y * g.astype(jnp.float32)).astype(x.dtype)

def _angles(pos, dim, theta):
    inv_freq = theta ** (-jnp.arange(0, dim, 2, dtype=jnp.float32) / dim)
    return pos.astype(jnp.float32)[:, None] * inv_freq[None, :]

def _rotate(x, ang):
    cos = jnp.cos(ang)[:, None, :].astype(x.dtype)
    sin = jnp.sin(ang)[:, None, :].astype(x.dtype)
    x1, x2 = jnp.split(x, 2, axis=-1)
    return jnp.concatenate([x1 * cos - x2 * sin, x2 * cos + x1 * sin], axis=-1)

def _softmax_f32(s):
    return jax.nn.softmax(s.astype(jnp.float32), axis=-1)

def _sweep_query_blocks(block_fn, *qs):
    b, s = qs[0].shape[:2]
    nb = s // Q_BLOCK
    blocked = tuple(jnp.swapaxes(q.reshape((b, nb, Q_BLOCK) + q.shape[2:]), 0, 1) for q in qs)
    out = lax.map(lambda qb: block_fn(*qb), blocked)
    out = jnp.swapaxes(out, 0, 1)
    return out.reshape((b, s) + out.shape[3:])

def _split_columns(p):
    out, start = [], 0
    for n in IN_SIZES:
        out.append(p[..., start:start + n])
        start += n
    return out

def _gqa_axial(q, k, v, q_g, k_g, row_ang, col_ang):
    b, s = q.shape[:2]
    half = A_HEAD_DIM // 2

    def axial(t):
        return jnp.concatenate([_rotate(t[..., :half], row_ang), _rotate(t[..., half:], col_ang)], axis=-1)

    q = axial(_rms_norm(q, q_g)) * (A_HEAD_DIM ** -0.5)
    k = axial(_rms_norm(k, k_g))
    q = q.reshape(b, s, A_KV_HEADS, A_GROUP, A_HEAD_DIM)

    def block(qb):
        sc = jnp.einsum('bqkgd,bskd->bkgqs', qb, k)
        p = _softmax_f32(sc).astype(v.dtype)
        return jnp.einsum('bkgqs,bskd->bqkgd', p, v)

    o = _sweep_query_blocks(block, q)
    return o.reshape(b, s, A_HEADS * A_HEAD_DIM)

def _diff_attention(q, k, v, lam_p, sub_g, lambda_init, rot_ang):
    b, s = q.shape[:2]

    def partial_rot(t):
        t = t.reshape(b, s, B_HEADS * 2, B_QK_DIM)
        t = jnp.concatenate([_rotate(t[..., :B_ROT_DIM], rot_ang), t[..., B_ROT_DIM:]], axis=-1)
        return t.reshape(b, s, B_HEADS, 2, B_QK_DIM)

    q = partial_rot(q) * (B_QK_DIM ** -0.5)
    k = partial_rot(k)
    v = v.reshape(b, s, B_HEADS, B_V_DIM)
    lf = lam_p.astype(jnp.float32)
    lam = jnp.exp(jnp.sum(lf[0] * lf[1])) - jnp.exp(jnp.sum(lf[2] * lf[3])) + lambda_init

    def block(qb):
        sc = jnp.einsum('bqhcd,bshcd->bhcqs', qb, k)
        p = _softmax_f32(sc)
        p = (p[:, :, 0] - lam * p[:, :, 1]).astype(v.dtype)
        return jnp.einsum('bhqs,bshe->bqhe', p, v)

    o = _sweep_query_blocks(block, q)
    o = _rms_norm(o, sub_g) * (1.0 - lambda_init)
    return o.reshape(b, s, B_HEADS * B_V_DIM)

def _mla(c_q, c_kv, k_r, q_g, kv_g, w_uq, w_ukv, ang):
    b, s = c_q.shape[:2]
    q = jnp.einsum('bsr,rn->bsn', _rms_norm(c_q, q_g), w_uq).reshape(b, s, C_HEADS, C_NOPE_DIM + C_ROPE_DIM)
    kv = jnp.einsum('bsr,rn->bsn', _rms_norm(c_kv, kv_g), w_ukv).reshape(b, s, C_HEADS, C_NOPE_DIM + C_V_DIM)
    scale = (C_NOPE_DIM + C_ROPE_DIM) ** -0.5
    q_nope = q[..., :C_NOPE_DIM] * scale
    q_rope = _rotate(q[..., C_NOPE_DIM:], ang) * scale
    k_nope, v = kv[..., :C_NOPE_DIM], kv[..., C_NOPE_DIM:]
    k_rope = _rotate(k_r[:, :, None, :], ang)[:, :, 0]

    def block(qn, qr):
        sc = jnp.einsum('bqhd,bshd->bhqs', qn, k_nope) + jnp.einsum('bqhr,bsr->bhqs', qr, k_rope)
        p = _softmax_f32(sc).astype(v.dtype)
        return jnp.einsum('bhqs,bshe->bqhe', p, v)

    o = _sweep_query_blocks(block, q_nope, q_rope)
    return o.reshape(b, s, C_HEADS * C_V_DIM)

def first_inputs(seed: int = 0) -> dict:
    key = jax.random.key(seed)
    ks = jax.random.split(key, 20)
    f32 = jnp.float32

    def nrm(k, shape, scale):
        return jax.random.normal(k, shape, f32) * scale

    def gain(k, shape):
        return 1.0 + 0.02 * jax.random.normal(k, shape, f32)

    return {
        'x': jax.random.normal(ks[0], (BATCH, SEQ, D_MODEL), f32),
        'ln1_g': gain(ks[1], (DEPTH, D_MODEL)),
        'w_in': nrm(ks[2], (DEPTH, D_MODEL, IN_COLS), D_MODEL ** -0.5),
        'a_q_norm': gain(ks[3], (DEPTH, A_HEAD_DIM)),
        'a_k_norm': gain(ks[4], (DEPTH, A_HEAD_DIM)),
        'b_lambda': nrm(ks[5], (DEPTH, 4, B_QK_DIM), 0.1),
        'b_subln': gain(ks[6], (DEPTH, B_V_DIM)),
        'c_q_norm': gain(ks[7], (DEPTH, C_Q_RANK)),
        'c_kv_norm': gain(ks[8], (DEPTH, C_KV_RANK)),
        'c_w_uq': nrm(ks[9], (DEPTH, C_Q_RANK, C_HEADS * (C_NOPE_DIM + C_ROPE_DIM)), C_Q_RANK ** -0.5),
        'c_w_ukv': nrm(ks[10], (DEPTH, C_KV_RANK, C_HEADS * (C_NOPE_DIM + C_V_DIM)), C_KV_RANK ** -0.5),
        'w_branch': nrm(ks[11], (DEPTH, N_BRANCH, BRANCH_W, D_MODEL), BRANCH_W ** -0.5),
        'w_out': nrm(ks[12], (DEPTH, D_MODEL, D_MODEL), D_MODEL ** -0.5),
        'ln2_g': gain(ks[13], (DEPTH, D_MODEL)),
        'w_ff1': nrm(ks[14], (DEPTH, D_MODEL, D_FF), D_MODEL ** -0.5),
        'w_ff2': nrm(ks[15], (DEPTH, D_FF, D_MODEL), D_FF ** -0.5),
        'final_g': gain(ks[16], (D_MODEL,)),
    }

def first_block(x, ln1_g, w_in, a_q_norm, a_k_norm, b_lambda, b_subln, c_q_norm, c_kv_norm,
              c_w_uq, c_w_ukv, w_branch, w_out, ln2_g, w_ff1, w_ff2, final_g):
    b, s, d = x.shape
    n_rows = s // GRID_W
    t = jnp.arange(s)
    row_idx = jnp.repeat(jnp.arange(n_rows), GRID_W)
    col_idx = jnp.tile(jnp.arange(GRID_W), n_rows)
    half = A_HEAD_DIM // 2
    row_ang = _angles(row_idx, half, AXIAL_THETA)
    col_ang = _angles(col_idx, half, AXIAL_THETA)
    b_ang = _angles(t, B_ROT_DIM, ROPE_THETA)
    c_ang = _angles(t, C_ROPE_DIM, MLA_THETA)

    for l in range(DEPTH):
        h = _rms_norm(x, ln1_g[l])
        proj = jnp.einsum('bsd,dn->bsn', h, w_in[l])
        (a_q, a_k, a_v, b_q, b_k, b_v, c_cq, c_ckv, c_kr, gate_logits) = _split_columns(proj)

        y_a = _gqa_axial(a_q.reshape(b, s, A_HEADS, A_HEAD_DIM),
                         a_k.reshape(b, s, A_KV_HEADS, A_HEAD_DIM),
                         a_v.reshape(b, s, A_KV_HEADS, A_HEAD_DIM),
                         a_q_norm[l], a_k_norm[l], row_ang, col_ang)
        lambda_init = 0.8 - 0.6 * math.exp(-0.3 * l)
        y_b = _diff_attention(b_q, b_k, b_v, b_lambda[l], b_subln[l], lambda_init, b_ang)
        y_c = _mla(c_cq, c_ckv, c_kr, c_q_norm[l], c_kv_norm[l], c_w_uq[l], c_w_ukv[l], c_ang)

        y = jnp.stack([y_a, y_b, y_c], axis=2)
        gates = jax.nn.sigmoid(gate_logits.reshape(b, s, N_BRANCH, d))
        merged = jnp.sum(gates * jnp.einsum('bsne,ned->bsnd', y, w_branch[l]), axis=2)
        x = x + jnp.einsum('bsd,de->bse', merged, w_out[l])

        h2 = _rms_norm(x, ln2_g[l])
        ff = jnp.square(jax.nn.relu(jnp.einsum('bsd,df->bsf', h2, w_ff1[l])))
        x = x + jnp.einsum('bsf,fd->bsd', ff, w_ff2[l])

    return _rms_norm(x, final_g)


HEAD_DIM = 64
POOL_WIDTH = D_MODEL // 4
POOL_WINDOWS = (2, 4, 8, 16)
N_POOL_GROUPS = len(POOL_WINDOWS)
POOL_GROUP_DIM = POOL_WIDTH // N_POOL_GROUPS
CONV_WIDTH = (3 * D_MODEL) // 8
CONV_KERNEL = 31
SGU_WIDTH = D_MODEL - POOL_WIDTH - CONV_WIDTH
SGU_HEADS = SGU_WIDTH // HEAD_DIM
CHUNK = 128
D_MIX = POOL_WIDTH + CONV_WIDTH + SGU_WIDTH
D_IN = POOL_WIDTH + 2 * CONV_WIDTH + 2 * SGU_WIDTH
D_FF_2 = ((8 * D_MODEL // 3 + 127) // 128) * 128
N_EXPERTS = 8
TOP_K = 2
D_FF_EXPERT = 7 * D_MODEL // 2
N_MOD = 6


def rms_norm(x, g):
    xf = x.astype(jnp.float32)
    y = xf * lax.rsqrt(jnp.mean(xf * xf, axis=-1, keepdims=True) + EPS)
    return (y * g.astype(jnp.float32)).astype(x.dtype)

def layer_norm(x, g, b):
    xf = x.astype(jnp.float32)
    mu = jnp.mean(xf, axis=-1, keepdims=True)
    var = jnp.mean(jnp.square(xf - mu), axis=-1, keepdims=True)
    y = (xf - mu) * lax.rsqrt(var + EPS) * g.astype(jnp.float32) + b.astype(jnp.float32)
    return y.astype(x.dtype)

def multiscale_pool(a, pool_w, pool_scale):
    S = a.shape[1]
    af = a.astype(jnp.float32)
    cs = jnp.pad(jnp.cumsum(af, axis=1), ((0, 0), (1, 0), (0, 0)))
    t = jnp.arange(S)
    outs = []
    for g, w in enumerate(POOL_WINDOWS):
        half = w // 2
        hi = jnp.clip(t + half, 0, S)
        lo = jnp.clip(t - half, 0, S)
        sl = slice(g * POOL_GROUP_DIM, (g + 1) * POOL_GROUP_DIM)
        cs_g = cs[:, :, sl]
        win_sum = jnp.take(cs_g, hi, axis=1) - jnp.take(cs_g, lo, axis=1)
        count = (hi - lo).astype(jnp.float32)[None, :, None]
        diff = (win_sum / count - af[:, :, sl]).astype(a.dtype)
        outs.append(jnp.einsum('bsc,cd->bsd', diff, pool_w[g]))
    return jnp.concatenate(outs, axis=-1) * pool_scale

def conformer_conv(p, conv_w, conv_b, ln_g, ln_b):
    val, gate = jnp.split(p, 2, axis=-1)
    glu = val * jax.nn.sigmoid(gate)
    y = lax.conv_general_dilated(
        glu, conv_w[:, None, :], window_strides=(1,),
        padding=[(CONV_KERNEL // 2, CONV_KERNEL // 2)],
        dimension_numbers=('NWC', 'WIO', 'NWC'),
        feature_group_count=CONV_WIDTH) + conv_b
    return jax.nn.silu(layer_norm(y, ln_g, ln_b))

def spatial_gating(p, ln_g, ln_b, sgu_w, sgu_b):
    B, S, _ = p.shape
    u, v = jnp.split(p, 2, axis=-1)
    v = layer_norm(v, ln_g, ln_b).reshape(B, S // CHUNK, CHUNK, SGU_HEADS, HEAD_DIM)
    mixed = jnp.einsum('hpq,bnqhd->bnphd', sgu_w, v) + sgu_b.T[:, :, None]
    return u * mixed.reshape(B, S, SGU_WIDTH)

def swiglu(h, w_gate, w_up, w_down):
    return (jax.nn.silu(h @ w_gate) * (h @ w_up)) @ w_down

def moe_swiglu(h, router_w, router_b, w_gate, w_up, w_down):
    logits = jnp.einsum('bsd,de->bse', h.astype(jnp.float32), router_w.astype(jnp.float32)) \
        + router_b.astype(jnp.float32)
    top_vals, top_idx = lax.top_k(logits, TOP_K)
    top_w = jax.nn.softmax(top_vals, axis=-1)
    combine = jnp.sum(jax.nn.one_hot(top_idx, N_EXPERTS, dtype=jnp.float32) * top_w[..., None], axis=-2)
    combine = combine.astype(h.dtype)
    y = jnp.zeros_like(h)
    for e in range(N_EXPERTS):
        y = y + combine[..., e:e + 1] * swiglu(h, w_gate[e], w_up[e], w_down[e])
    return y

def second_inputs(seed: int = 0) -> dict:
    key = jax.random.key(seed)
    ks = jax.random.split(key, 32)
    n_dense = (DEPTH + 1) // 2
    n_moe = DEPTH // 2

    def nrm(k, shape, fan_in):
        return jax.random.normal(k, shape, jnp.float32) * (fan_in ** -0.5)

    def near_one(k, shape):
        return 1.0 + 0.1 * jax.random.normal(k, shape, jnp.float32)

    def small(k, shape):
        return 0.02 * jax.random.normal(k, shape, jnp.float32)

    return {
        "x": jax.random.normal(ks[0], (BATCH, SEQ, D_MODEL), jnp.float32),
        "c": jax.random.normal(ks[1], (BATCH, D_MODEL), jnp.float32),
        "ada_w": nrm(ks[2], (DEPTH, D_MODEL, N_MOD * D_MODEL), D_MODEL),
        "ada_b": small(ks[3], (DEPTH, N_MOD * D_MODEL)),
        "mix_norm_g": near_one(ks[4], (DEPTH, D_MODEL)),
        "ffn_norm_g": near_one(ks[5], (DEPTH, D_MODEL)),
        "w_in": nrm(ks[6], (DEPTH, D_MODEL, D_IN), D_MODEL),
        "pool_w": nrm(ks[7], (DEPTH, N_POOL_GROUPS, POOL_GROUP_DIM, POOL_GROUP_DIM), POOL_GROUP_DIM),
        "pool_scale": near_one(ks[8], (DEPTH, POOL_WIDTH)),
        "conv_w": nrm(ks[9], (DEPTH, CONV_KERNEL, CONV_WIDTH), CONV_KERNEL),
        "conv_b": small(ks[10], (DEPTH, CONV_WIDTH)),
        "conv_ln_g": near_one(ks[11], (DEPTH, CONV_WIDTH)),
        "conv_ln_b": small(ks[12], (DEPTH, CONV_WIDTH)),
        "sgu_ln_g": near_one(ks[13], (DEPTH, SGU_WIDTH)),
        "sgu_ln_b": small(ks[14], (DEPTH, SGU_WIDTH)),
        "sgu_w": nrm(ks[15], (DEPTH, SGU_HEADS, CHUNK, CHUNK), CHUNK),
        "sgu_b": near_one(ks[16], (DEPTH, SGU_HEADS, CHUNK)),
        "w_out": nrm(ks[17], (DEPTH, D_MIX, D_MODEL), D_MIX),
        "ffn_w_gate": nrm(ks[18], (n_dense, D_MODEL, D_FF_2), D_MODEL),
        "ffn_w_up": nrm(ks[19], (n_dense, D_MODEL, D_FF_2), D_MODEL),
        "ffn_w_down": nrm(ks[20], (n_dense, D_FF_2, D_MODEL), D_FF_2),
        "router_w": nrm(ks[21], (n_moe, D_MODEL, N_EXPERTS), D_MODEL),
        "router_b": 0.01 * jax.random.normal(ks[22], (n_moe, N_EXPERTS), jnp.float32),
        "moe_w_gate": nrm(ks[23], (n_moe, N_EXPERTS, D_MODEL, D_FF_EXPERT), D_MODEL),
        "moe_w_up": nrm(ks[24], (n_moe, N_EXPERTS, D_MODEL, D_FF_EXPERT), D_MODEL),
        "moe_w_down": nrm(ks[25], (n_moe, N_EXPERTS, D_FF_EXPERT, D_MODEL), D_FF_EXPERT),
        "final_norm_g": near_one(ks[26], (D_MODEL,)),
    }

def second_block(x, c, ada_w, ada_b, mix_norm_g, ffn_norm_g, w_in, pool_w, pool_scale,
              conv_w, conv_b, conv_ln_g, conv_ln_b, sgu_ln_g, sgu_ln_b, sgu_w, sgu_b, w_out,
              ffn_w_gate, ffn_w_up, ffn_w_down, router_w, router_b,
              moe_w_gate, moe_w_up, moe_w_down, final_norm_g):
    cond = jax.nn.silu(c)
    for l in range(DEPTH):
        mod = cond @ ada_w[l] + ada_b[l]
        mods = jnp.split(mod[:, None, :], N_MOD, axis=-1)
        shift_m, scale_m, gate_m, shift_f, scale_f, gate_f = mods

        h = rms_norm(x, mix_norm_g[l]) * (1.0 + scale_m) + shift_m
        proj = h @ w_in[l]
        p_pool, p_conv, p_sgu = jnp.split(proj, [POOL_WIDTH, POOL_WIDTH + 2 * CONV_WIDTH], axis=-1)
        out_a = multiscale_pool(p_pool, pool_w[l], pool_scale[l])
        out_b = conformer_conv(p_conv, conv_w[l], conv_b[l], conv_ln_g[l], conv_ln_b[l])
        out_c = spatial_gating(p_sgu, sgu_ln_g[l], sgu_ln_b[l], sgu_w[l], sgu_b[l])
        mixed = jnp.concatenate([out_a, out_b, out_c], axis=-1)
        x = x + gate_m * (mixed @ w_out[l])

        h = rms_norm(x, ffn_norm_g[l]) * (1.0 + scale_f) + shift_f
        i = l // 2
        if l % 2 == 0:
            y = swiglu(h, ffn_w_gate[i], ffn_w_up[i], ffn_w_down[i])
        else:
            y = moe_swiglu(h, router_w[i], router_b[i], moe_w_gate[i], moe_w_up[i], moe_w_down[i])
        x = x + gate_f * y
    return rms_norm(x, final_norm_g)


def setup_inputs(seed=0):
    out = dict(first_inputs(seed))
    for name, value in second_inputs(seed + 1).items():
        if name != "x":
            out[name + "_2"] = value
    return out


def reference(
    x, ln1_g, w_in, a_q_norm, a_k_norm, b_lambda, b_subln, c_q_norm, c_kv_norm, c_w_uq, c_w_ukv,
    w_branch, w_out, ln2_g, w_ff1, w_ff2, final_g, c_2, ada_w_2, ada_b_2, mix_norm_g_2,
    ffn_norm_g_2, w_in_2, pool_w_2, pool_scale_2, conv_w_2, conv_b_2, conv_ln_g_2, conv_ln_b_2,
    sgu_ln_g_2, sgu_ln_b_2, sgu_w_2, sgu_b_2, w_out_2, ffn_w_gate_2, ffn_w_up_2, ffn_w_down_2,
    router_w_2, router_b_2, moe_w_gate_2, moe_w_up_2, moe_w_down_2, final_norm_g_2,
):
    x = first_block(
        x, ln1_g, w_in, a_q_norm, a_k_norm, b_lambda, b_subln, c_q_norm, c_kv_norm, c_w_uq,
        c_w_ukv, w_branch, w_out, ln2_g, w_ff1, w_ff2, final_g,
    )
    return second_block(
        x, c_2, ada_w_2, ada_b_2, mix_norm_g_2, ffn_norm_g_2, w_in_2, pool_w_2, pool_scale_2,
        conv_w_2, conv_b_2, conv_ln_g_2, conv_ln_b_2, sgu_ln_g_2, sgu_ln_b_2, sgu_w_2, sgu_b_2,
        w_out_2, ffn_w_gate_2, ffn_w_up_2, ffn_w_down_2, router_w_2, router_b_2, moe_w_gate_2,
        moe_w_up_2, moe_w_down_2, final_norm_g_2,
    )


_drawn_inputs = setup_inputs


def setup_inputs(seed=0):
    import zlib

    import numpy as np

    out = dict(_drawn_inputs(seed))
    spreads = {}
    factors = {'a_q_norm': 8.0,
     'a_k_norm': 7.877,
     'b_subln': 2.738,
     'c_q_norm': 7.818,
     'c_kv_norm': 6.77,
     'conv_b_2': 3.827,
     'conv_ln_b_2': 5.391,
     'sgu_ln_b_2': 3.083,
     'router_b_2': 4.785}
    for name, (base, spread) in spreads.items():
        noise = np.random.default_rng([zlib.crc32(name.encode()), seed]).standard_normal(out[name].shape)
        drawn = base * np.exp(spread * noise) if base else spread * noise
        out[name] = __import__('jax').numpy.asarray(drawn.astype(out[name].dtype))
    for name, factor in factors.items():
        out[name] = (out[name] * factor).astype(out[name].dtype)
    return out
```

```python
import math
from contextlib import ExitStack

import numpy as np
import concourse.bass as bass
from concourse import mybir

F32 = mybir.dt.float32
U32 = mybir.dt.uint32
ALU = mybir.AluOpType
ACT = mybir.ActivationFunctionType
AX = mybir.AxisListType.X

P = 128
SEQ = 256
NB = SEQ // P
D = 1024
KD = D // P
DEPTH = 2
EPS = 1e-6
GRID_W = 64

A_HEADS, A_KV, A_DIM = 8, 2, 64
B_HEADS, B_DIM, B_ROT = 8, 32, 8
C_HEADS, C_NOPE, C_ROPE, C_V = 8, 64, 32, 64
C_QK = C_NOPE + C_ROPE
CQ_RANK, CKV_RANK = 384, 256
KCQ, KCKV = CQ_RANK // P, CKV_RANK // P
BR_W = 512
FF = 4 * D
O_AK = A_HEADS * A_DIM
O_AV = O_AK + A_KV * A_DIM
O_BQ = O_AV + A_KV * A_DIM
O_BK = O_BQ + B_HEADS * 2 * B_DIM
O_BV = O_BK + B_HEADS * 2 * B_DIM
O_CQ = O_BV + B_HEADS * 2 * B_DIM
O_CKV = O_CQ + CQ_RANK
O_KR = O_CKV + CKV_RANK
PROJ_W = O_KR + C_ROPE
GATE_W = 3 * D
PROJ_N = PROJ_W // 8
GATE_N = GATE_W // 8

POOL_W, CONV_W, SGU_W = 256, 384, 384
KCONV = CONV_W // P
TAPS = 31
HALO = TAPS // 2
SGU_HEADS, SGU_D = 6, 64
WINDOWS = (2, 4, 8, 16)
FF2 = 2816
EXPERTS = 8
FFE = 3584
MODS = 6
WIDTHS = (64, 112, 144, SEQ)
ESTEPS = FFE // 256

NSLOT = 4
SLOT = 4096
SUB = 2048
L1_CHUNKS = 40
L2_CHUNKS = 20
FT = 2

ROW_L1 = 2 * KD + KCQ + KCKV
R_C = DEPTH * ROW_L1
R2_MIXG, R2_FFNG = 0, DEPTH * KD
R2_PS = 2 * DEPTH * KD
R2_CB = R2_PS + DEPTH * 2
R2_CG = R2_CB + DEPTH * KCONV
R2_CLB = R2_CG + DEPTH * KCONV
R2_SB = R2_CLB + DEPTH * KCONV
R2_N = R2_SB + DEPTH * SGU_HEADS
B_AQ, B_AK, B_SUB, B_LAM, B_INIT = 0, 64, 128, 192, 320
B_N = 322


class Signal:

    def __init__(self, sem, per):
        self.sem, self.per = sem, per

    def at(self, u, k):
        return u * self.per + k


class Steps:

    def __init__(self, eng, sem):
        self.eng, self.sem, self.base, self.n = eng, sem, 0, 0

    def did(self, ins):
        ins.then_inc(self.sem, 1)
        self.n += 1

    def settle(self):
        self.eng.wait_ge(self.sem, self.base + self.n)

    def do(self, ins):
        self.did(ins)
        self.settle()


DVE_STEPS, POOL_STEPS = 156, 12
N_CONST = 3 + 5 * DEPTH
N_ROWS = 4 * DEPTH + 2 + 6 + 2
N_MIX = 7
N_MIXL = 7


def build(nc, t):
    ctx = ExitStack()
    with ctx:
        def sb(name, shape, dt=F32):
            return ctx.enter_context(nc.sbuf_tensor(name, shape, dt))

        def sig(name, per=0):
            return Signal(ctx.enter_context(nc.semaphore(name)), per)

        ring = sb("ring", [P, NSLOT * SLOT])
        x = sb("x", [P, NB, D])
        hT = sb("hT", [P, KD, SEQ])
        rot = sb("rot", [P, 4096])
        arena = sb("arena", [P, 12288])
        qk = sb("qk", [P, 4096])
        yT = sb("yT", [P, 13, SEQ])
        probs = sb("probs", [P, 4, NB * SEQ])
        pT = sb("pT", [P, 2, 2 * SEQ])
        o = sb("o", [P, NB, BR_W])
        ident = sb("ident", [P, P])
        rows = sb("rows", [P, 3, P])
        cols = sb("cols", [P, 3, P])
        bc = sb("bc", [P, DEPTH, B_N])
        cur = sb("cur", [P, ROW_L1])
        curb = sb("curb", [P, B_N])
        cwr = sb("cwr", [TAPS, DEPTH, CONV_W])
        cwc = sb("cwc", [P, DEPTH, KCONV, TAPS])
        ropeA = sb("ropeA", [P, NB, 2, A_DIM])
        ropeB = sb("ropeB", [P, NB, 2, B_ROT])
        ropeC = sb("ropeC", [P, NB, 2, C_ROPE])
        small = sb("small", [P, 512])
        mhalf = sb("mhalf", [P, SEQ])
        epsc = sb("epsc", [P, 20])
        inverse = {n: sb(f"inverse{n}", [P, 20]) for n in (D, A_DIM, CQ_RANK, CKV_RANK)}
        zcol = sb("zcol", [P, 2])
        idx = sb("idx", [P, NB, 8], U32)
        counts = sb("counts", [P, EXPERTS], mybir.dt.int32)

        xn = rot[:, 0:NB * D].rearrange("p (b d) -> p b d", b=NB)
        aqr = rot[:, 0:NB * 512].rearrange("p (b d) -> p b d", b=NB)
        akr = rot[:, 1024:1280].rearrange("p (b d) -> p b d", b=NB)
        t1 = rot[:, 1280:2560].rearrange("p (b d) -> p b d", b=NB)
        t2 = rot[:, 2560:3840].rearrange("p (b d) -> p b d", b=NB)
        qC = rot[:, 0:1536].rearrange("p (b d) -> p b d", b=NB)
        kC = rot[:, 1536:3072].rearrange("p (b d) -> p b d", b=NB)
        vC = rot[:, 3072:4096].rearrange("p (b d) -> p b d", b=NB)
        proj = arena[:, 0:NB * PROJ_W].rearrange("p (b n) -> p b n", b=NB)
        merged = arena[:, 0:NB * D].rearrange("p (b d) -> p b d", b=NB)
        gated = arena[:, 2048:3072].rearrange("p (i d) -> p i d", i=2)
        gates = arena[:, 6144:12288].rearrange("p (b n) -> p b n", b=NB)
        hid = arena[:, 0:2048].rearrange("p (i f s) -> p i f s", i=2, f=4)
        aqT = qk[:, 0:1024].rearrange("p (k s) -> p k s", s=SEQ)
        akT = qk[:, 1024:1280]
        bqT = qk[:, 1280:2304].rearrange("p (k s) -> p k s", s=SEQ)
        bkT = qk[:, 2304:3328].rearrange("p (k s) -> p k s", s=SEQ)
        cqT = qk[0:C_QK, 0:2048].rearrange("p (k s) -> p k s", s=SEQ)
        ckT = qk[0:C_QK, 2048:4096].rearrange("p (k s) -> p k s", s=SEQ)
        cnT = yT[:, 8:13, :]

        gateB = arena[:, 0:2048].rearrange("p (g d) -> p g d", g=2)
        band = arena[:, 2048:4096].rearrange("p (k g s) -> p k g s", k=NB, g=4)
        poolA = arena[:, 4096:4608].rearrange("p (b c) -> p b c", b=NB)
        diffT = arena[:, 4608:5120].rearrange("p (j s) -> p j s", j=2)
        glu = arena[:, 5120:5120 + KCONV * (SEQ + 2 * HALO)].rearrange("p (c s) -> p c s", c=KCONV)
        sg = arena[:, 6144:6912].rearrange("p (c s) -> p c s", c=KCONV)
        cacc = arena[:, 6912:7680].rearrange("p (c s) -> p c s", c=KCONV)
        csq = arena[:, 7680:8448].rearrange("p (c s) -> p c s", c=KCONV)
        cmean = arena[:, 8448:8704]
        crstd = arena[:, 8704:8960]
        us = arena[:, 8960:9728].rearrange("p (b c) -> p b c", b=NB)
        vs = arena[:, 9728:10496].rearrange("p (b c) -> p b c", b=NB)
        swr = arena[:, 10496:11264].rearrange("p (h q) -> p h q", h=SGU_HEADS)
        swT = arena[:, 11264:12032].rearrange("p (h q) -> p h q", h=SGU_HEADS)
        condB = qk[:, 0:1024].rearrange("p (k m) -> p k m", k=KD)
        finB = qk[:, 1024:2048]
        sguG = qk[:, 2048:2432]
        sguB = qk[:, 2432:2816]
        outc = qk[:, 2816:3584].rearrange("p (b c) -> p b c", b=NB)
        pw = qk[:, 3584:3712].rearrange("p (j d) -> p j d", j=2)
        rw = qk[:, 3712:3776].rearrange("p (k e) -> p k e", k=KD)
        rb = qk[:, 3776:3784]
        io8 = qk[:, 3784:3792]
        ones = probs[:, 0, 0:P]
        mixT = yT[:, 0:8, :]
        modc = probs[:, 1, 0:32]
        mulc = probs[:, 1, 32:48]
        condc = probs[:, 1, 48:56]
        comb = probs[:, 1, 64:80].rearrange("p (b e) -> p b e", b=NB)
        cmb = probs[:, 1, 80:82]
        ffsg = probs[:, 2, :].rearrange("p (f s) -> p f s", f=FT)
        ffhid = pT[:, :, :].rearrange("p i (f s) -> p i f s", f=FT)
        yacc = arena[:, 4096:6144].rearrange("p (b d) -> p b d", b=NB)
        sel = arena[:, 6144:6656].rearrange("p (b c) -> p b c", b=NB)
        selw = arena[:, 6656:7168].rearrange("p (b c) -> p b c", b=NB)
        selT = arena[:, 7168:7680].rearrange("p (i s) -> p i s", i=2)
        ye = arena[:, 7680:7680 + 2 * D].rearrange("p (i d) -> p i d", i=2)
        hTe = hT
        tri = rot[:, 2048:2048 + P]
        slots = rot[:, 2176:2176 + SEQ]
        place = small[:, 240:240 + NB * (EXPERTS + 1)].rearrange("p (b e) -> p b e", b=NB)
        weight = small[:, 260:260 + NB * (EXPERTS + 1)].rearrange("p (b e) -> p b e", b=NB)
        chosen = small[:, 280:296].rearrange("p (b e) -> p b e", b=NB)
        curp, curw = small[:, 300:302], small[:, 302:304]
        emsg = probs[:, 2:4, :]
        ehid = pT[:, :, :]

        G = [ctx.enter_context(nc.psum_tensor(f"G{i}", [P, 512], F32)) for i in range(4)]
        T = [ctx.enter_context(nc.psum_tensor(f"T{i}", [P, 512], F32)) for i in range(2)]
        S = [ctx.enter_context(nc.psum_tensor(f"S{i}", [P, 512], F32)) for i in range(2)]
        H4 = [S[0], S[1], T[0], T[1]]

        loaded = [sig(f"loaded{i}", 16 * L1_CHUNKS // NSLOT) for i in range(NSLOT)]
        used = [sig(f"used{i}", L1_CHUNKS // NSLOT) for i in range(NSLOT)]
        x_in = sig("x_in")
        consts_in = sig("consts_in")
        rows_in = sig("rows_in")
        mix_in = sig("mix_in")
        mixl_in = [sig(f"mixl_in{i}") for i in range(DEPTH)]
        ident_ok = sig("ident_ok")
        half_ok = sig("half_ok")
        rows_turned = sig("rows_turned")
        cols_ok = sig("cols_ok")
        cur_ok = sig("cur_ok", 1)
        dve_step = sig("dve_step")
        pool_step = sig("pool_step")
        x_new = sig("x_new", 4)
        ss_ok = sig("ss_ok", 2)
        rstd_ok = sig("rstd_ok", 1)
        xn_ok = sig("xn_ok", 2)
        xn_turned = sig("xn_turned", 4)
        hT_act = sig("hT_act", 2)
        hT_dve = sig("hT_dve", 2)
        proj_mm = sig("proj_mm", 8)
        proj_act = sig("proj_act", 8)
        proj_dve = sig("proj_dve", 8)
        gate_mm = sig("gate_mm", 8)
        gate_ev = sig("gate_ev", 16)
        asq_ok = sig("asq_ok", 1)
        ars_ok = sig("ars_ok", 1)
        csq_ok = sig("csq_ok", 4)
        crs_ok = sig("crs_ok", 1)
        lam_in = sig("lam_in", 1)
        lam_exp = sig("lam_exp", 1)
        cn_ok = sig("cn_ok", 1)
        rope_ok = sig("rope_ok", 1)
        cn_turned = sig("cn_turned", 3)
        cn_ev = sig("cn_ev", 3)
        up_mm = sig("up_mm", 6)
        up_ev = sig("up_ev", 8)
        qk_turned = sig("qk_turned", 15)
        qk_act = sig("qk_act", 8)
        qk_dve = sig("qk_dve", 7)
        ropeC_ok = sig("ropeC_ok", 1)
        sc_mm = sig("sc_mm", 32)
        negmax_ok = sig("negmax_ok", 32)
        exp_ok = sig("exp_ok", 32)
        pcomb_ok = sig("pcomb_ok", 8)
        p_turned = sig("p_turned", 24)
        pT_ok = sig("pT_ok", 24)
        pv_mm = sig("pv_mm", 24)
        o_ev = sig("o_ev", 24)
        subsq_ok = sig("subsq_ok", 1)
        subrs_ok = sig("subrs_ok", 1)
        o_ok = sig("o_ok", 3)
        o_turned = sig("o_turned", 6)
        y_act = sig("y_act", 3)
        y_dve = sig("y_dve", 3)
        br_mm = sig("br_mm", 9)
        br_ev = sig("br_ev", 12)
        mg_turned = sig("mg_turned", 4)
        mg_act = sig("mg_act", 2)
        mg_dve = sig("mg_dve", 2)
        ff_mm = sig("ff_mm", 24)
        ff_ev = sig("ff_ev", 32)
        ff2_mm = sig("ff2_mm", 1)
        blk1_done = sig("blk1_done")
        cond_ok = sig("cond_ok")
        condB_ok = sig("condB_ok")
        mods_ok = sig("mods_ok", 1)
        w2_mm = sig("w2_mm", 7)
        pool_ev = sig("pool_ev", 1)
        conv_sg = sig("conv_sg", 3)
        glu_ok = sig("glu_ok", 3)
        uv_ev = sig("uv_ev", 4)
        diff_mm = sig("diff_mm", 2)
        diff_ev = sig("diff_ev", 2)
        poolo_mm = sig("poolo_mm", 2)
        poolo_ev = sig("poolo_ev", 2)
        cacc_ok = sig("cacc_ok", 1)
        cmean_mm = sig("cmean_mm", 1)
        cdev_ok = sig("cdev_ok", 1)
        cvar_mm = sig("cvar_mm", 1)
        cvar_ok = sig("cvar_ok", 1)
        crstd_ok = sig("crstd_ok", 1)
        cln_ok = sig("cln_ok", 3)
        csig_ok = sig("csig_ok", 3)
        conv_ok = sig("conv_ok", 3)
        sw_turned = sig("sw_turned", 2)
        sw_ev = sig("sw_ev", 2)
        vvar_ok = sig("vvar_ok", 1)
        vrs_ok = sig("vrs_ok", 1)
        vn_ok = sig("vn_ok", 1)
        sgu_mm = sig("sgu_mm", 2)
        outc_ok = sig("outc_ok", 1)
        outc_turned = sig("outc_turned", 2)
        outc_ev = sig("outc_ev", 2)
        sub_in = [[sig(f"sub_in{i}{n}") for n in "gud"] for i in range(2)]
        sub_used = [[sig(f"sub_used{i}{n}") for n in "gud"] for i in range(2)]
        fg_mm = sig("fg_mm")
        fu_mm = sig("fu_mm")
        fsg_ok = sig("fsg_ok")
        fhid_ok = sig("fhid_ok")
        chosen_ok = sig("chosen_ok")
        rank_mm = sig("rank_mm")
        counts_ok = sig("counts_ok")
        cur_loaded = sig("cur_loaded")
        sel_ok = sig("sel_ok")
        selw_ok = sig("selw_ok")
        gath_mm = sig("gath_mm")
        hTe_act = sig("hTe_act")
        hTe_dve = sig("hTe_dve")
        esg_ok = sig("esg_ok")
        et_ok = sig("et_ok")
        ehid_ok = sig("ehid_ok")
        edn_done = sig("edn_done")
        selT_mm = sig("selT_mm")
        selT_ok = sig("selT_ok")
        ye_act = sig("ye_act")
        ye_dve = sig("ye_dve")
        scat_mm = sig("scat_mm")
        scat_ev = sig("scat_ev")
        rt_mm = sig("rt_mm")
        rt_max = sig("rt_max")
        rt_exp = sig("rt_exp")
        stored = sig("stored")
        out_ok = sig("out_ok")
        merged_ok = sig("merged_ok", 1)
        ff_relu = sig("ff_relu", 32)
        zero_ok = sig("zero_ok")
        fin_in = sig("fin_in")
        ft_ok = sig("ft_ok")
        fdn_done = sig("fdn_done")
        adaG_ev = sig("adaG_ev", 1)

        block = ctx.enter_context(nc.Block())

        def slot(pos):
            return ring[:, (pos % NSLOT) * SLOT:(pos % NSLOT + 1) * SLOT]

        def sub(i, piece):
            at = (i * 3 + piece) * SUB
            return ring[:, at:at + SUB]

        U_FIN1, U_MIX, U_FFN, U_FIN2 = 4, 5, 6, 9

        def used_at(l, pos):
            return l * (L1_CHUNKS // NSLOT) + pos // NSLOT + 2

        def used2_at(l, pos):
            return DEPTH * L1_CHUNKS // NSLOT + l * L2_CHUNKS // NSLOT + pos // NSLOT + 2
        X1 = DEPTH * 4 * 2

        def each_expert(eng, body):
            with eng.Fori(0, EXPERTS) as e:
                n = eng.value_load(counts[0:1, bass.ds(e, 1)], min_val=0, max_val=SEQ)
                for lo, w in zip((-1, *WIDTHS), WIDTHS):
                    with eng.If(n > lo):
                        with eng.If(n <= w):
                            body(e, w)

        def blocks(w):
            return [(i, i * P, min(P, w - i * P)) for i in range(-(-w // P))]

        def gather_bank(k, w):
            per = min(4, 512 // w)
            return k // per, k % per * w

        @block.sync
        def _(sp):
            sp.dma_start(x[:], t["x"][0].rearrange("(b p) d -> p b d", p=P)).then_inc(x_in.sem, 16)

            def load(l, pos, dst, src, per=L1_CHUNKS, first=0):
                i = pos % NSLOT
                sp.wait_ge(used[i].sem, first + l * (per // NSLOT) + pos // NSLOT + 1)
                sp.dma_start(dst, src).then_inc(loaded[i].sem, 16)

            with sp.Fori(0, DEPTH) as l:
                w_in = t["w_in"][l].rearrange("(k p) n -> p k n", p=P)
                for part, n, c0 in ((0, PROJ_N, 0), (1, GATE_N, PROJ_W)):
                    with sp.Fori(0, 2) as it:
                        for c in range(NSLOT):
                            i = c
                            sp.wait_ge(used[i].sem, l * (L1_CHUNKS // NSLOT) + (2 * part) + it + 1)
                            sp.dma_start(slot(c)[:, 0:KD * n].rearrange("p (k n) -> p k n", k=KD),
                                         w_in[:, :, bass.ds(it * (NSLOT * n) + c0 + c * n, n)]).then_inc(loaded[i].sem, 16)
                load(l, 16, slot(16)[:, 0:KCQ * 768].rearrange("p (k n) -> p k n", k=KCQ),
                     t["c_w_uq"][l].rearrange("(k p) n -> p k n", p=P))
                load(l, 17, slot(17)[:, 0:KCKV * 1024].rearrange("p (k n) -> p k n", k=KCKV),
                     t["c_w_ukv"][l].rearrange("(k p) n -> p k n", p=P))
                for n in range(3):
                    load(l, 18 + n, slot(18 + n).rearrange("p (k n) -> p k n", k=4),
                         t["w_branch"][l, n].rearrange("(k p) n -> p k n", p=P))
                for n, (k0, k1) in enumerate(((0, 3), (3, 6), (6, 8))):
                    load(l, 21 + n, slot(21 + n)[:, 0:(k1 - k0) * D].rearrange("p (k n) -> p k n", n=D),
                         t["w_out"][l].rearrange("(k p) n -> p k n", p=P)[:, k0:k1, :])
                f1 = t["w_ff1"][l].rearrange("(k p) n -> p k n", p=P)
                f2 = t["w_ff2"][l].rearrange("(k p) n -> p k n", p=P)
                with sp.Fori(0, 4) as it:
                    for c in range(NSLOT):
                        sp.wait_ge(used[c].sem, l * (L1_CHUNKS // NSLOT) + it + 6 + 1)
                        if c % 2 == 0:
                            sp.dma_start(slot(c).rearrange("p (k n) -> p k n", k=KD),
                                         f1[:, :, bass.ds(it * 1024 + (c // 2) * 512, 512)]).then_inc(loaded[c].sem, 16)
                        else:
                            sp.dma_start(slot(c).rearrange("p (k n) -> p k n", k=4),
                                         f2[:, bass.ds(it * 8 + (c // 2) * 4, 4), :]).then_inc(loaded[c].sem, 16)
            base = DEPTH * L1_CHUNKS // NSLOT
            subn = [0, 0]

            def load_sub(i, g, u, d, wait):
                for piece, src in enumerate((g, u, d)):
                    sp.wait_ge(sub_used[i][piece].sem, wait)
                    dst = sub(i, piece).rearrange("p (k n) -> p k n", n=src.shape[2])
                    sp.dma_start(dst, src).then_inc(sub_in[i][piece].sem, 16)

            for l in range(DEPTH):
                b2 = base + l * L2_CHUNKS // NSLOT
                if l > 0:
                    for i in range(2):
                        for piece in range(3):
                            sp.wait_ge(sub_used[i][piece].sem, 1 + subn[i])
                ada = t["ada_w_2"][l].rearrange("(k p) n -> p k n", p=P)
                with sp.Fori(0, 2) as it:
                    for c in range(NSLOT):
                        sp.wait_ge(used[c].sem, it + b2 + 1)
                        sp.dma_start(slot(c).rearrange("p (k n) -> p k n", k=KD),
                                     ada[:, :, bass.ds(it * (3 * D) + c * 512, 512)]).then_inc(loaded[c].sem, 16)
                w2 = t["w_in_2"][l].rearrange("(k p) n -> p k n", p=P)
                at = 0
                for c, n in enumerate((POOL_W, CONV_W, CONV_W, SGU_W, SGU_W)):
                    load(0, 8 + c, slot(8 + c)[:, 0:KD * n].rearrange("p (k n) -> p k n", k=KD),
                         w2[:, :, at:at + n], first=b2)
                    at += n
                for c in range(4):
                    c0 = (2 + 3 * (c // 2)) * D + (c % 2) * 512
                    load(0, 13 + c, slot(13 + c).rearrange("p (k n) -> p k n", k=KD), ada[:, :, c0:c0 + 512], first=b2)
                for n, (k0, k1) in enumerate(((0, 3), (3, 6), (6, 8))):
                    load(0, 17 + n, slot(17 + n)[:, 0:(k1 - k0) * D].rearrange("p (k n) -> p k n", n=D),
                         t["w_out_2"][l].rearrange("(k p) n -> p k n", p=P)[:, k0:k1, :], first=b2)
                for i in range(NSLOT):
                    sp.wait_ge(used[i].sem, b2 + L2_CHUNKS // NSLOT + 1)
                if l == 0:
                    g = t["ffn_w_gate_2"][0].rearrange("(k p) n -> p k n", p=P)
                    u = t["ffn_w_up_2"][0].rearrange("(k p) n -> p k n", p=P)
                    d = t["ffn_w_down_2"][0].rearrange("(k p) n -> p k n", p=P)
                    with sp.Fori(0, 5) as it:
                        for i in range(2):
                            n0 = it * (2 * FT * P) + i * FT * P
                            load_sub(i, g[:, :, bass.ds(n0, FT * P)], u[:, :, bass.ds(n0, FT * P)],
                                     d[:, bass.ds(it * (2 * FT) + i * FT, FT), :], it + 1)
                    load_sub(0, g[:, :, 10 * FT * P:], u[:, :, 10 * FT * P:], d[:, 10 * FT:, :], 6)
                    subn = [6, 5]
                else:
                    with sp.Fori(0, EXPERTS) as e:
                        g = t["moe_w_gate_2"][0, e].rearrange("(k p) n -> p k n", p=P)
                        u = t["moe_w_up_2"][0, e].rearrange("(k p) n -> p k n", p=P)
                        d = t["moe_w_down_2"][0, e].rearrange("(k p) n -> p k n", p=P)
                        with sp.Fori(0, 7) as it:
                            for i in range(2):
                                n0 = it * (2 * FT * P) + i * FT * P
                                load_sub(i, g[:, :, bass.ds(n0, FT * P)], u[:, :, bass.ds(n0, FT * P)],
                                         d[:, bass.ds(it * (2 * FT) + i * FT, FT), :],
                                         e * 7 + it + subn[i] + 1)
            sp.wait_ge(out_ok.sem, NB)
            sp.dma_start(t["out"][0].rearrange("(b p) d -> p b d", p=P), x[:]).then_inc(stored.sem, 16)
            sp.wait_ge(stored.sem, 16)

        @block.gpsimd
        def _(pool):
            step = Steps(pool, pool_step.sem)
            pool.memset(ident[:], 0.0).then_inc(ident_ok.sem, 1)
            pool.memset(mhalf[:], -0.5)
            pool.memset(epsc[:], EPS)
            for n, tile in inverse.items():
                last = pool.memset(tile[:], 1.0 / n)
            last.then_inc(half_ok.sem, 1)
            pool.memset(zcol[:], 0.0).then_inc(zero_ok.sem, 1)
            for i in range(2):
                for piece in range(3):
                    pool.sem_inc(sub_used[i][piece].sem, 1)
            for i in range(NSLOT):
                pool.sem_inc(used[i].sem, 1)
            n = 0
            for l in range(DEPTH):
                at = l * ROW_L1
                for name, r in (("ln1_g", KD), ("ln2_g", KD), ("c_q_norm", KCQ), ("c_kv_norm", KCKV)):
                    pool.dma_start(rows[at:at + r, 0, :], t[name][l].rearrange("(r p) -> r p", p=P)).then_inc(rows_in.sem, 16)
                    at += r
                    n += 1
            pool.dma_start(rows[R_C:R_C + KD, 0, :], t["c_2"][0].rearrange("(r p) -> r p", p=P)).then_inc(rows_in.sem, 16)
            pool.dma_start(rows[0:DEPTH * MODS * KD, 1, :], t["ada_b_2"].rearrange("l (r p) -> (l r) p", p=P)).then_inc(rows_in.sem, 16)
            for at, name in ((R2_MIXG, "mix_norm_g_2"), (R2_FFNG, "ffn_norm_g_2"), (R2_PS, "pool_scale_2"),
                             (R2_CB, "conv_b_2"), (R2_CG, "conv_ln_g_2"), (R2_CLB, "conv_ln_b_2")):
                v = t[name].rearrange("l (r p) -> (l r) p", p=P)
                pool.dma_start(rows[at:at + v.shape[0], 2, :], v).then_inc(rows_in.sem, 16)
            pool.dma_start(rows[R2_SB:R2_SB + DEPTH * SGU_HEADS, 2, :], t["sgu_b_2"].rearrange("l h p -> (l h) p")).then_inc(rows_in.sem, 16)
            pool.dma_start(cwr[:], t["conv_w_2"].rearrange("l t c -> t l c")).then_inc(rows_in.sem, 16)
            pool.wait_ge(ident_ok.sem, 1)
            pool.affine_select(out=ident[:], in_=ident[:], compare_op=ALU.not_equal, fill=1.0, base=0,
                               pattern=[[-1, P]], channel_multiplier=1).then_inc(ident_ok.sem, 1)
            pool.wait_ge(half_ok.sem, 1)

            def inv_root(v, out, count, u_wait, done):
                n = v.shape[1]
                step.do(pool.tensor_tensor(v, v, inverse[count][:, 0:n], ALU.mult))
                step.do(pool.tensor_tensor(v, v, epsc[:, 0:n], ALU.add))
                pool.tensor_tensor(out, v, mhalf[:, 0:n], ALU.pow).then_inc(done.sem, 1)

            def norm_root(u):
                pool.wait_ge(ss_ok.sem, ss_ok.at(u, 2))
                inv_root(small[:, 0:2], small[:, 2:4], D, u, rstd_ok)

            pool.wait_ge(cols_ok.sem, 1)
            pool.wait_ge(consts_in.sem, 16 * N_CONST)
            with pool.Fori(0, DEPTH) as l:
                step.base, step.n = l * POOL_STEPS, 0
                step.do(pool.tensor_copy(cur[:], cols[:, 0, bass.ds(l * ROW_L1, ROW_L1)]))
                pool.tensor_copy(curb[:], bc[:, bass.ds(l, 1), :].rearrange("p a n -> p (a n)")).then_inc(cur_ok.sem, 1)
                norm_root(l * 2)
                pool.wait_ge(asq_ok.sem, asq_ok.at(l, 1))
                inv_root(small[:, 8:28], small[:, 32:52], A_DIM, l, ars_ok)
                pool.wait_ge(csq_ok.sem, csq_ok.at(l, 4))
                step.did(pool.tensor_tensor(small[:, 56:58], small[:, 56:58], inverse[CQ_RANK][:, 0:2], ALU.mult))
                step.do(pool.tensor_tensor(small[:, 58:60], small[:, 58:60], inverse[CKV_RANK][:, 0:2], ALU.mult))
                step.do(pool.tensor_tensor(small[:, 56:60], small[:, 56:60], epsc[:, 0:4], ALU.add))
                pool.tensor_tensor(small[:, 60:64], small[:, 56:60], mhalf[:, 0:4], ALU.pow).then_inc(crs_ok.sem, 1)
                pool.wait_ge(subsq_ok.sem, subsq_ok.at(l, 1))
                inv_root(small[:, 64:80], small[:, 80:96], 2 * B_DIM, l, subrs_ok)
                norm_root(l * 2 + 1)
                pool.wait_ge(x_new.sem, l * 8 + 8 + 1)
            assert step.n == POOL_STEPS, step.n
            step.base, step.n = DEPTH * POOL_STEPS, 0
            norm_root(U_FIN1)
            pool.wait_ge(blk1_done.sem, 1)
            pool.dma_start(finB, t["final_norm_g_2"].partition_broadcast(P)).then_inc(mix_in.sem, 16)
            pool.dma_start(rw, t["router_w_2"][0].rearrange("(k p) e -> p k e", p=P)).then_inc(mix_in.sem, 16)
            pool.dma_start(rb, t["router_b_2"][0].partition_broadcast(P)).then_inc(mix_in.sem, 16)
            pool.dma_start(tri, t["before"]).then_inc(mix_in.sem, 16)
            pool.dma_start(slots, t["slots"].partition_broadcast(P)).then_inc(mix_in.sem, 16)
            pool.dma_start(io8, t["iota8"].partition_broadcast(P)).then_inc(mix_in.sem, 16)
            pool.dma_start(band.rearrange("p k g s -> p k (g s)"), t["band"].rearrange("(k p) g s -> p k (g s)", p=P)).then_inc(mix_in.sem, 16)
            pool.memset(ones, 1.0).then_inc(half_ok.sem, 1)
            for c in range(KCONV):
                pool.memset(glu[:, c, 0:HALO], 0.0)
                pool.memset(glu[:, c, HALO + SEQ:], 0.0).then_inc(half_ok.sem, 1)
            for l in range(DEPTH):
                if l:
                    pool.wait_ge(x_new.sem, X1 + 1 + 8)
                q = mixl_in[l].sem
                for g in range(2):
                    pool.dma_start(gateB[:, g, :], t["ada_b_2"][l, (2 + 3 * g) * D:(3 + 3 * g) * D].partition_broadcast(P)).then_inc(q, 16)
                pool.dma_start(sguG, t["sgu_ln_g_2"][l].partition_broadcast(P)).then_inc(q, 16)
                pool.dma_start(sguB, t["sgu_ln_b_2"][l].partition_broadcast(P)).then_inc(q, 16)
                pool.dma_start(swr, t["sgu_w_2"][l].rearrange("h p q -> p h q")).then_inc(q, 16)
                pw_v = t["pool_w_2"][l].rearrange("(j i) c d -> i c j d", i=2)
                for i in range(2):
                    pool.dma_start(pw[64 * i:64 * i + 64], pw_v[i]).then_inc(q, 16)
                norm_root(U_MIX + 2 * l)
                pool.wait_ge(vvar_ok.sem, l + 1)
                pool.tensor_tensor(small[:, 100:102], small[:, 98:100], mhalf[:, 0:2], ALU.pow).then_inc(vrs_ok.sem, 1)
                pool.wait_ge(cvar_ok.sem, l + 1)
                pool.tensor_tensor(crstd, crstd, mhalf[:], ALU.pow).then_inc(crstd_ok.sem, 1)
                norm_root(U_FFN + 2 * l)
            norm_root(U_FIN2)

        @block.scalar
        def _(act):
            q = consts_in.sem
            act.dma_start(ropeA[:], t["rope_a"].rearrange("(b p) c d -> p b c d", p=P)).then_inc(q, 16)
            act.dma_start(ropeB[:], t["rope_b"].rearrange("(b p) c d -> p b c d", p=P)).then_inc(q, 16)
            act.dma_start(ropeC[:], t["rope_c"].rearrange("(b p) c d -> p b c d", p=P)).then_inc(q, 16)
            for l in range(DEPTH):
                for at, name in ((B_AQ, "a_q_norm"), (B_AK, "a_k_norm"), (B_SUB, "b_subln")):
                    act.dma_start(bc[:, l, at:at + 64], t[name][l].partition_broadcast(P)).then_inc(q, 16)
                act.dma_start(bc[:, l, B_LAM:B_LAM + 128], t["b_lambda"][l].rearrange("a d -> (a d)").partition_broadcast(P)).then_inc(q, 16)
                act.dma_start(bc[:, l, B_INIT:B_INIT + 2], t["lam_init"][l].partition_broadcast(P)).then_inc(q, 16)
            act.wait_ge(x_in.sem, 16)
            act.sem_inc(proj_act.sem, 2)
            act.sem_inc(gate_ev.sem, 4)
            act.sem_inc(ff_relu.sem, 4)

            def norm_squares(u):
                for b in range(NB):
                    act.activation(xn[:, b, :], x[:, b, :], ACT.Square, accum_out=small[:, b:b + 1]).then_inc(ss_ok.sem, 1)

            def turned_evac(u, turned, done, mul, add=None):
                for i in (0, 2):
                    act.wait_ge(turned.sem, turned.at(u, i + 1))
                    for kk in range(2):
                        k = 2 * i + kk
                        src = T[0][:, kk * SEQ:(kk + 1) * SEQ]
                        if mul is None:
                            ins = act.activation(hT[:, k, :], src, ACT.Copy)
                        elif add is None:
                            ins = act.activation(hT[:, k, :], src, ACT.Copy, scale=mul[:, k:k + 1])
                        else:
                            ins = act.activation(hT[:, k, :], src, ACT.Identity, scale=mul[:, k:k + 1], bias=add[:, k:k + 1])
                    ins.then_inc(done.sem, 1)

            act.wait_ge(rows_turned.sem, 1)
            for i, n in enumerate((R_C + KD, DEPTH * MODS * KD, R2_N)):
                ins = act.activation(cols[:, i, 0:n], T[0][:, i * P:i * P + n], ACT.Copy)
            ins.then_inc(cols_ok.sem, 1)
            act.wait_ge(rows_turned.sem, 2)
            for l in range(DEPTH):
                ins = act.activation(cwc[:, l], T[1][:, l * 128:l * 128 + KCONV * TAPS].rearrange("p (c t) -> p c t", c=KCONV), ACT.Copy)
            ins.then_inc(cols_ok.sem, 1)

            with act.Fori(0, DEPTH) as l:
                act.wait_ge(x_new.sem, l * 8 + 1)
                norm_squares(l * 2)
                act.wait_ge(cur_ok.sem, cur_ok.at(l, 1))
                turned_evac(l * 2, xn_turned, hT_act, cur[:, 0:KD])
                with act.Fori(0, 2) as it:
                    for c in range(NSLOT):
                        act.wait_ge(proj_mm.sem, l * 8 + it * 4 + (c + 1))
                        act.activation(proj[:, 0, bass.ds(it * (NSLOT * PROJ_N) + c * PROJ_N, PROJ_N)],
                                       G[2 * (c % 2)][:, 0:PROJ_N], ACT.Copy).then_inc(proj_act.sem, 1)
                act.wait_ge(proj_act.sem, proj_act.at(l, 8) + 2)
                act.wait_ge(proj_dve.sem, proj_dve.at(l, 8) + 2)
                for i, (c0, w) in enumerate(((O_CQ, CQ_RANK), (O_CKV, CKV_RANK))):
                    for b in range(NB):
                        act.activation(probs[:, 2 * i + b, 0:w], proj[:, b, c0:c0 + w], ACT.Square,
                                       accum_out=small[:, 56 + 2 * i + b:57 + 2 * i + b]).then_inc(csq_ok.sem, 1)
                act.wait_ge(lam_in.sem, lam_in.at(l, 1))
                act.activation(small[:, 104:106], small[:, 102:104], ACT.Exp).then_inc(lam_exp.sem, 1)
                with act.Fori(0, 2) as it:
                    for c in range(NSLOT):
                        for b in range(NB):
                            if b == 0:
                                act.wait_ge(gate_mm.sem, l * 8 + it * 4 + (c + 1))
                            else:
                                act.wait_ge(used[c].sem, used_at(l, 8) + it)
                            act.activation(gates[:, b, bass.ds(it * (NSLOT * GATE_N) + c * GATE_N, GATE_N)],
                                           G[2 * (c % 2) + b][:, 0:GATE_N], ACT.Sigmoid).then_inc(gate_ev.sem, 1)
                for i in range(3):
                    act.wait_ge(cn_turned.sem, cn_turned.at(l, i + 1))
                    for kk in range(2 if i < 2 else 1):
                        k = 2 * i + kk
                        ins = act.activation(cnT[:, k, :], T[i % 2][:, kk * SEQ:(kk + 1) * SEQ], ACT.Copy,
                                             scale=cur[:, 2 * KD + k:2 * KD + k + 1])
                    ins.then_inc(cn_ev.sem, 1)
                for i in range(0, 7, 2):
                    act.wait_ge(qk_turned.sem, qk_turned.at(l, i + 1))
                    dst = (qk[:, 0:512], None, akT, None, qk[:, 1280 + 512:1280 + 1024], None, qk[:, 2304 + 512:2304 + 1024])[i]
                    act.activation(dst, T[0][:, 0:dst.shape[1]], ACT.Copy).then_inc(qk_act.sem, 1)

                def attend(s0, ns, u0, nu, scale):
                    def exps(s):
                        act.wait_ge(negmax_ok.sem, negmax_ok.at(l, s + 1))
                        for b in range(NB):
                            ins = act.activation(probs[:, s % 4, b * SEQ:(b + 1) * SEQ], S[s % 2][:, b * SEQ:(b + 1) * SEQ], ACT.Exp,
                                                 scale=scale, bias=small[:, 120 + 2 * (s % 4) + b:121 + 2 * (s % 4) + b],
                                                 accum_out=small[:, 128 + 2 * (s % 4) + b:129 + 2 * (s % 4) + b])
                        ins.then_inc(exp_ok.sem, 1)

                    lead = ns // nu
                    for s in range(lead):
                        exps(s0 + s)
                    for i in range(nu):
                        if i + 1 < nu:
                            for s in range(lead):
                                exps(s0 + (i + 1) * lead + s)
                        u = u0 + i
                        act.wait_ge(p_turned.sem, p_turned.at(l, u + 1))
                        act.activation(pT[:, u % 2, :], T[u % 2][:, :], ACT.Copy).then_inc(pT_ok.sem, 1)

                def y_evac(br):
                    act.wait_ge(o_turned.sem, o_turned.at(l, 2 * br + 1))
                    act.activation(yT[:, 4 * br:4 * br + 2, :], T[0][:, :].rearrange("p (k s) -> p k s", k=2), ACT.Copy).then_inc(y_act.sem, 1)

                attend(0, 8, 0, 8, A_DIM ** -0.5)
                y_evac(0)
                attend(8, 16, 8, 8, B_DIM ** -0.5)
                y_evac(1)
                for i in range(8):
                    if i % 2 == 0:
                        act.wait_ge(qk_turned.sem, qk_turned.at(l, 7 + i + 1))
                        dst = (cqT if i < 4 else ckT)[:, 2 * (i % 4):2 * (i % 4) + 2, :]
                        act.activation(dst, T[(7 + i) % 2][0:C_QK, :].rearrange("p (k s) -> p k s", k=2), ACT.Copy).then_inc(qk_act.sem, 1)
                attend(24, 8, 16, 8, C_QK ** -0.5)
                y_evac(2)
                turned_evac(l, mg_turned, mg_act, None)
                act.wait_ge(x_new.sem, l * 8 + 4 + 1)
                norm_squares(l * 2 + 1)
                turned_evac(l * 2 + 1, xn_turned, hT_act, cur[:, KD:2 * KD])
                with act.Fori(0, 4) as it:
                    for j in range(2):
                        for f in range(4):
                            if f < 3:
                                act.wait_ge(ff_mm.sem, l * 24 + it * 6 + (3 * j + f + 1))
                            else:
                                act.wait_ge(used[2 * j].sem, used_at(l, 24) + it)
                            act.activation(hid[:, j, f, :], H4[f][:, 0:SEQ], ACT.Relu).then_inc(ff_relu.sem, 1)
            act.wait_ge(x_new.sem, X1 + 1)
            act.dma_start(arena[:, 0:D], t["final_g"].partition_broadcast(P)).then_inc(fin_in.sem, 16)
            norm_squares(U_FIN1)
            act.wait_ge(blk1_done.sem, 1)
            act.activation(condc, cols[:, 0, R_C:R_C + KD], ACT.Sigmoid).then_inc(cond_ok.sem, 1)
            for l in range(DEPTH):
                u = U_MIX + 2 * l
                if l:
                    act.wait_ge(x_new.sem, X1 + 1 + 8 * l)
                norm_squares(u)
                act.wait_ge(mods_ok.sem, l + 1)
                turned_evac(u - 1, xn_turned, hT_act, mulc[:, 0:KD], modc[:, 0:KD])
                for c in range(KCONV):
                    if c < 2:
                        act.wait_ge(w2_mm.sem, w2_mm.at(l, 4 + c))
                    else:
                        act.wait_ge(used[10 % NSLOT].sem, used2_at(l, 10))
                    act.activation(sg[:, c, :], H4[1 + c][:, 0:SEQ], ACT.Sigmoid).then_inc(conv_sg.sem, 1)
                for i, dst in enumerate((us, vs)):
                    for b in range(NB):
                        if b == 0:
                            act.wait_ge(w2_mm.sem, w2_mm.at(l, 6 + i))
                        else:
                            act.wait_ge(used[(11 + i) % NSLOT].sem, used2_at(l, 11 + i))
                        act.activation(dst[:, b, :], G[2 * i + b][:, 0:SGU_W], ACT.Copy).then_inc(uv_ev.sem, 1)
                for i in range(2):
                    act.wait_ge(outc_turned.sem, outc_turned.at(l, i + 1))
                    k = 2 - i
                    act.activation(mixT[:, 5 + 2 * i:5 + 2 * i + k, :], G[2 + i][:, 0:k * SEQ].rearrange("p (k s) -> p k s", k=k),
                                   ACT.Copy).then_inc(outc_ev.sem, 1)
                for c in range(KCONV):
                    act.wait_ge(cln_ok.sem, cln_ok.at(l, c + 1))
                    act.activation(sg[:, c, :], cacc[:, c, :], ACT.Sigmoid).then_inc(csig_ok.sem, 1)
                act.wait_ge(x_new.sem, X1 + 1 + 8 * l + 4)
                norm_squares(u + 1)
                turned_evac(u, xn_turned, hT_act, mulc[:, KD:2 * KD], modc[:, 16:16 + KD])

                def silu_gate(n, i, count):
                    for f in range(FT):
                        act.wait_ge(fhid_ok.sem, n * FT + (f + 1))
                        if f == 0:
                            act.wait_ge(fg_mm.sem, n + 1)
                        else:
                            act.wait_ge(sub_used[i][0].sem, count)
                        act.activation(ffsg[:, f, :], H4[2 * f][:, 0:SEQ], ACT.Sigmoid).then_inc(fsg_ok.sem, 1)

                if l == 0:
                    with act.Fori(0, 5) as it:
                        for i in range(2):
                            silu_gate(it * 2 + i, i, it + 2)
                    silu_gate(10, 0, 7)
                else:
                    act.wait_ge(rt_max.sem, 1)
                    act.activation(small[:, 200:202], small[:, 196:198], ACT.Exp).then_inc(rt_exp.sem, 1)

                    def expert(e, w):
                        act.wait_ge(gath_mm.sem, e + 1)
                        for k in range(KD):
                            bank, c0 = gather_bank(k, w)
                            if bank % 2 == 0:
                                ins = act.activation(hTe[:, k, 0:w], H4[bank][:, c0:c0 + w], ACT.Identity, scale=mulc[:, KD + k:KD + k + 1], bias=modc[:, 16 + k:17 + k])
                        ins.then_inc(hTe_act.sem, 1)
                        with act.Fori(0, ESTEPS // 2) as it:
                            for i in range(2):
                                act.wait_ge(ehid_ok.sem, e * ESTEPS + it * 2 + (i + 1))
                                act.wait_ge(sub_used[i][0].sem, e * (ESTEPS // 2) + it + (8 - i))
                                act.activation(emsg[:, i, 0:FT * w], H4[2 * i][:, 0:FT * w], ACT.Sigmoid).then_inc(esg_ok.sem, 1)
                        act.wait_ge(selT_mm.sem, e + 1)
                        for i, s0, n in blocks(w):
                            ins = act.activation(selT[0:n, i, :], H4[0][0:n, i * SEQ:(i + 1) * SEQ], ACT.Copy)
                        ins.then_inc(selT_ok.sem, 1)
                        act.wait_ge(edn_done.sem, e + 1)
                        for i, s0, n in blocks(w):
                            ins = act.activation(ye[0:n, i, 512:1024], G[2 + i][0:n, :], ACT.Copy)
                        ins.then_inc(ye_act.sem, 1)

                    act.wait_ge(counts_ok.sem, 1)
                    each_expert(act, expert)
            act.wait_ge(x_new.sem, X1 + 1 + 16)
            norm_squares(U_FIN2)

        @block.vector
        def _(dve):
            step = Steps(dve, dve_step.sem)
            dve.sem_inc(x_new.sem, 1)
            dve.sem_inc(proj_dve.sem, 2)
            dve.sem_inc(fhid_ok.sem, FT)
            dve.sem_inc(scat_ev.sem, 1)
            dve.sem_inc(ehid_ok.sem, 2)
            dve.wait_ge(x_in.sem, 16)
            dve.wait_ge(consts_in.sem, 16 * N_CONST)

            def normalise(u, v):
                dve.wait_ge(rstd_ok.sem, rstd_ok.at(u, 1))
                for b in range(NB):
                    dve.tensor_scalar(xn[:, b, :], x[:, b, :], small[:, 2 + b:3 + b], None, ALU.mult).then_inc(xn_ok.sem, 1)

            def turned_evac(v, turned, done, mul, add=None):
                for i in (1, 3):
                    dve.wait_ge(turned.sem, turned.at(v, i + 1))
                    for kk in range(2):
                        k = 2 * i + kk
                        src = T[1][:, kk * SEQ:(kk + 1) * SEQ]
                        if mul is None:
                            ins = dve.tensor_copy(hT[:, k, :], src)
                        elif add is None:
                            ins = dve.tensor_scalar(hT[:, k, :], src, mul[:, k:k + 1], None, ALU.mult)
                        else:
                            ins = dve.tensor_scalar(hT[:, k, :], src, mul[:, k:k + 1], add[:, k:k + 1], ALU.mult, ALU.add)
                    ins.then_inc(done.sem, 1)

            def add_to_x(g=None, count=0):
                for half in range(2):
                    for b in range(NB):
                        xs = x[:, b, half * 512:(half + 1) * 512]
                        if g is None:
                            dve.tensor_tensor(xs, G[2 * half + b][:, :], xs, ALU.add).then_inc(x_new.sem, 1)
                        else:
                            tmp = csq.rearrange("p c s -> p (c s)")[:, 0:512]
                            dve.wait_ge(x_new.sem, count + 2 * half + b)
                            step.do(dve.tensor_tensor(tmp, G[2 * half + b][:, :], gateB[:, g, half * 512:(half + 1) * 512], ALU.mult))
                            dve.tensor_tensor(xs, xs, tmp, ALU.add).then_inc(x_new.sem, 1)

            def bcast(ap, shape):
                return ap.broadcast_to(shape)

            with dve.Fori(0, DEPTH) as l:
                step.base, step.n = l * DVE_STEPS, 0
                dve.wait_ge(cur_ok.sem, cur_ok.at(l, 1))
                normalise(l * 2, l * 2)
                turned_evac(l * 2, xn_turned, hT_dve, cur[:, 0:KD])
                lp = curb[:, B_LAM:B_LAM + 128].rearrange("p (a c d) -> p a c d", a=2, c=2)
                lt = small[:, 400:464].rearrange("p (a d) -> p a d", a=2)
                step.do(dve.tensor_tensor(lt, lp[:, :, 0, :], lp[:, :, 1, :], ALU.mult))
                dve.tensor_reduce(small[:, 102:104], lt, AX, ALU.add).then_inc(lam_in.sem, 1)
                step.did(dve.tensor_scalar(curb[:, B_SUB:B_SUB + 64], curb[:, B_SUB:B_SUB + 64], curb[:, B_INIT + 1:B_INIT + 2], None, ALU.mult))
                with dve.Fori(0, 2) as it:
                    for c in range(NSLOT):
                        dve.wait_ge(used[c].sem, used_at(l, 0) + it)
                        dve.tensor_copy(proj[:, 1, bass.ds(it * (NSLOT * PROJ_N) + c * PROJ_N, PROJ_N)],
                                        G[2 * (c % 2) + 1][:, 0:PROJ_N]).then_inc(proj_dve.sem, 1)
                dve.wait_ge(proj_act.sem, proj_act.at(l, 8) + 2)
                dve.wait_ge(proj_dve.sem, proj_dve.at(l, 8) + 2)
                nqk = A_HEADS + A_KV
                for b in range(NB):
                    step.did(dve.tensor_tensor(t1[:, b, :], proj[:, b, 0:nqk * A_DIM], proj[:, b, 0:nqk * A_DIM], ALU.mult))
                step.settle()
                dve.tensor_reduce(small[:, 8:28], rot[:, 1280:2560].rearrange("p (h d) -> p h d", d=A_DIM), AX, ALU.add).then_inc(asq_ok.sem, 1)
                dve.wait_ge(crs_ok.sem, crs_ok.at(l, 1))
                for i, (c0, w) in enumerate(((O_CQ, CQ_RANK), (O_CKV, CKV_RANK))):
                    for b in range(NB):
                        r = small[:, 60 + 2 * i + b:61 + 2 * i + b]
                        ins = dve.tensor_scalar(proj[:, b, c0:c0 + w], proj[:, b, c0:c0 + w], r, None, ALU.mult)
                        if (i, b) == (1, 1):
                            ins.then_inc(cn_ok.sem, 1)
                        else:
                            step.did(ins)
                dve.wait_ge(ars_ok.sem, ars_ok.at(l, 1))
                for b in range(NB):
                    v = proj[:, b, 0:nqk * A_DIM].rearrange("p (h d) -> p h d", d=A_DIM)
                    r = small[:, 32 + 10 * b:42 + 10 * b].unsqueeze(2)
                    step.did(dve.tensor_tensor(t1[:, b].rearrange("p (h d) -> p h d", d=A_DIM), v, bcast(r, [P, nqk, A_DIM]), ALU.mult))
                step.settle()
                for b in range(NB):
                    v = t1[:, b].rearrange("p (h d) -> p h d", d=A_DIM)
                    for h0, h1, at in ((0, A_HEADS, B_AQ), (A_HEADS, nqk, B_AK)):
                        gn = curb[:, at:at + A_DIM].unsqueeze(1)
                        step.did(dve.tensor_tensor(v[:, h0:h1], v[:, h0:h1], bcast(gn, [P, h1 - h0, A_DIM]), ALU.mult))
                step.settle()
                for b in range(NB):
                    v = t1[:, b].rearrange("p (h d) -> p h d", d=A_DIM)
                    w = t2[:, b].rearrange("p (h d) -> p h d", d=A_DIM)
                    for e in range(2):
                        vo = t1[:, b].rearrange("p (h a e d) -> p h a e d", h=nqk, a=2, e=2)[:, :, :, 1 - e, :]
                        wo = t2[:, b].rearrange("p (h a e d) -> p h a e d", h=nqk, a=2, e=2)[:, :, :, e, :]
                        sn = ropeA[:, b, 1, :].rearrange("p (a e d) -> p a e d", a=2, e=2)[:, :, e, :].unsqueeze(1)
                        step.did(dve.tensor_tensor(wo, vo, bcast(sn, [P, nqk, 2, 16]), ALU.mult))
                step.settle()
                for b in range(NB):
                    v = t1[:, b].rearrange("p (h d) -> p h d", d=A_DIM)
                    cs = ropeA[:, b, 0, :].unsqueeze(1)
                    step.did(dve.tensor_tensor(v, v, bcast(cs, [P, nqk, A_DIM]), ALU.mult))
                step.settle()
                for b in range(NB):
                    v = t1[:, b].rearrange("p (h d) -> p h d", d=A_DIM)
                    w = t2[:, b].rearrange("p (h d) -> p h d", d=A_DIM)
                    q_out = aqr[:, b].rearrange("p (i g d) -> p g i d", i=4, g=2)
                    for g in range(A_KV):
                        step.did(dve.tensor_tensor(q_out[:, g], v[:, 4 * g:4 * g + 4], w[:, 4 * g:4 * g + 4], ALU.add))
                    step.did(dve.tensor_tensor(akr[:, b].rearrange("p (h d) -> p h d", d=A_DIM), v[:, A_HEADS:], w[:, A_HEADS:], ALU.add))
                for b in range(NB):
                    v = proj[:, b, O_BQ:O_BV].rearrange("p (u d) -> p u d", d=B_DIM)
                    a = probs[:, b, 0:256].rearrange("p (u d) -> p u d", d=B_ROT)
                    c = probs[:, b, 256:512].rearrange("p (u d) -> p u d", d=B_ROT)
                    step.did(dve.tensor_tensor(a, v[:, :, 0:B_ROT], bcast(ropeB[:, b, 0, :].unsqueeze(1), [P, 32, B_ROT]), ALU.mult))
                    for e in range(2):
                        sn = ropeB[:, b, 1, 4 * e:4 * e + 4].unsqueeze(1)
                        step.did(dve.tensor_tensor(c[:, :, 4 * e:4 * e + 4], v[:, :, 4 - 4 * e:8 - 4 * e], bcast(sn, [P, 32, 4]), ALU.mult))
                for b in range(NB):
                    v = proj[:, b, O_KR:O_KR + C_ROPE]
                    a, c = probs[:, 2 + b, 0:C_ROPE], probs[:, 2 + b, C_ROPE:2 * C_ROPE]
                    step.did(dve.tensor_tensor(a, v, ropeC[:, b, 0, :], ALU.mult))
                    for e in range(2):
                        step.did(dve.tensor_tensor(c[:, 16 * e:16 * e + 16], v[:, 16 - 16 * e:32 - 16 * e], ropeC[:, b, 1, 16 * e:16 * e + 16], ALU.mult))
                step.settle()
                for b in range(NB):
                    a, c = probs[:, 2 + b, 0:C_ROPE], probs[:, 2 + b, C_ROPE:2 * C_ROPE]
                    step.did(dve.tensor_tensor(proj[:, b, O_KR:O_KR + C_ROPE], a, c, ALU.add))
                for b in range(NB):
                    v = proj[:, b, O_BQ:O_BV].rearrange("p (u d) -> p u d", d=B_DIM)
                    a = probs[:, b, 0:256].rearrange("p (u d) -> p u d", d=B_ROT)
                    c = probs[:, b, 256:512].rearrange("p (u d) -> p u d", d=B_ROT)
                    ins = dve.tensor_tensor(v[:, :, 0:B_ROT], a, c, ALU.add)
                    if b == 0:
                        step.did(ins)
                    else:
                        ins.then_inc(rope_ok.sem, 1)
                dve.wait_ge(lam_exp.sem, lam_exp.at(l, 1))
                step.do(dve.tensor_tensor(small[:, 107:108], small[:, 105:106], small[:, 104:105], ALU.subtract))
                step.did(dve.tensor_tensor(small[:, 106:107], small[:, 107:108], curb[:, B_INIT:B_INIT + 1], ALU.subtract))
                for i in (1, 3, 5):
                    dve.wait_ge(qk_turned.sem, qk_turned.at(l, i + 1))
                    dst = {1: qk[:, 512:1024], 3: qk[:, 1280:1792], 5: qk[:, 2304:2816]}[i]
                    dve.tensor_copy(dst, T[1][:, :]).then_inc(qk_dve.sem, 1)
                for half in range(2):
                    for b in range(NB):
                        j = 2 * half + b
                        if j < 3:
                            dve.wait_ge(up_mm.sem, up_mm.at(l, j + 1))
                        else:
                            dve.wait_ge(used[0].sem, used_at(l, 16))
                        dve.tensor_copy(qC[:, b, half * 384:(half + 1) * 384], G[j][:, 0:384]).then_inc(up_ev.sem, 1)
                for half in range(2):
                    for b in range(NB):
                        j = 2 * half + b
                        if j < 3:
                            dve.wait_ge(up_mm.sem, up_mm.at(l, 3 + j + 1))
                        else:
                            dve.wait_ge(used[1].sem, used_at(l, 17))
                        kv = G[j][:, :].rearrange("p (h d) -> p h d", d=C_NOPE + C_V)
                        kh = kC[:, b, half * 384:(half + 1) * 384].rearrange("p (h d) -> p h d", d=C_QK)
                        vh = vC[:, b, half * 256:(half + 1) * 256].rearrange("p (h d) -> p h d", d=C_V)
                        dve.tensor_copy(kh[:, :, 0:C_NOPE], kv[:, :, 0:C_NOPE])
                        dve.tensor_copy(vh, kv[:, :, C_NOPE:]).then_inc(up_ev.sem, 1)
                dve.wait_ge(up_ev.sem, up_ev.at(l, 8))
                for b in range(NB):
                    kh = kC[:, b].rearrange("p (h d) -> p h d", d=C_QK)[:, :, C_NOPE:]
                    step.did(dve.tensor_copy(kh, bcast(proj[:, b, O_KR:O_KR + C_ROPE].unsqueeze(1), [P, C_HEADS, C_ROPE])))
                    v = qC[:, b].rearrange("p (h d) -> p h d", d=C_QK)[:, :, C_NOPE:]
                    a = pT[:, b, 0:256].rearrange("p (h d) -> p h d", d=C_ROPE)
                    c = pT[:, b, 256:512].rearrange("p (h d) -> p h d", d=C_ROPE)
                    step.did(dve.tensor_tensor(a, v, bcast(ropeC[:, b, 0, :].unsqueeze(1), [P, C_HEADS, C_ROPE]), ALU.mult))
                    for e in range(2):
                        sn = ropeC[:, b, 1, 16 * e:16 * e + 16].unsqueeze(1)
                        step.did(dve.tensor_tensor(c[:, :, 16 * e:16 * e + 16], v[:, :, 16 - 16 * e:32 - 16 * e], bcast(sn, [P, C_HEADS, 16]), ALU.mult))
                step.settle()
                for b in range(NB):
                    v = qC[:, b].rearrange("p (h d) -> p h d", d=C_QK)[:, :, C_NOPE:]
                    a = pT[:, b, 0:256].rearrange("p (h d) -> p h d", d=C_ROPE)
                    c = pT[:, b, 256:512].rearrange("p (h d) -> p h d", d=C_ROPE)
                    ins = dve.tensor_tensor(v, a, c, ALU.add)
                    if b == 0:
                        step.did(ins)
                    else:
                        ins.then_inc(ropeC_ok.sem, 1)

                def attend(s0, ns, u0, nu, scale, br):
                    lead = ns // nu

                    def maxima(s):
                        dve.wait_ge(sc_mm.sem, sc_mm.at(l, s + 1))
                        m = small[:, 112 + 2 * (s % 4):114 + 2 * (s % 4)]
                        step.do(dve.tensor_reduce(m, S[s % 2][:, :].rearrange("p (b k) -> p b k", b=NB), AX, ALU.max))
                        dve.tensor_scalar(small[:, 120 + 2 * (s % 4):122 + 2 * (s % 4)], m, -scale, None, ALU.mult).then_inc(negmax_ok.sem, 1)

                    def inverse(s):
                        dve.wait_ge(exp_ok.sem, exp_ok.at(l, s + 1))
                        step.do(dve.reciprocal(small[:, 136 + 2 * (s % 4):138 + 2 * (s % 4)], small[:, 128 + 2 * (s % 4):130 + 2 * (s % 4)]))

                    for s in range(lead):
                        maxima(s0 + s)
                    for i in range(nu):
                        u, s = u0 + i, s0 + i * lead
                        for j in range(lead):
                            inverse(s + j)
                        if lead == 2:
                            r0, r1 = (small[:, 136 + 2 * ((s + j) % 4):138 + 2 * ((s + j) % 4)] for j in range(2))
                            p0, p1 = (probs[:, (s + j) % 4, :].rearrange("p (b k) -> p b k", b=NB) for j in range(2))
                            step.do(dve.tensor_scalar(r1, r1, small[:, 106:107], None, ALU.mult))
                            for b in range(NB):
                                step.did(dve.tensor_scalar(p1[:, b], p1[:, b], r1[:, b:b + 1], None, ALU.mult))
                            step.settle()
                            for b in range(NB):
                                ins = dve.scalar_tensor_tensor(out=p0[:, b], in0=p0[:, b], scalar=r0[:, b:b + 1], in1=p1[:, b], op0=ALU.mult, op1=ALU.add)
                                if b == 0:
                                    step.did(ins)
                                else:
                                    ins.then_inc(pcomb_ok.sem, 1)
                        if i + 1 < nu:
                            for j in range(lead):
                                maxima(s + lead + j)
                        dve.wait_ge(pv_mm.sem, pv_mm.at(l, u + 1))
                        dst = o[:, :, 64 * i:64 * i + 64]
                        src = G[u % 2][:, 0:NB * 64].rearrange("p (b d) -> p b d", b=NB)
                        if lead == 2:
                            dve.tensor_copy(dst, src).then_inc(o_ev.sem, 1)
                        else:
                            r = small[:, 136 + 2 * (s % 4):138 + 2 * (s % 4)].unsqueeze(2)
                            dve.tensor_tensor(dst, src, bcast(r, [P, NB, 64]), ALU.mult).then_inc(o_ev.sem, 1)
                    dve.wait_ge(o_ev.sem, o_ev.at(l, u0 + nu))
                    if lead == 2:
                        of = o[:, :, :].rearrange("p b (h d) -> p (b h) d", d=64)
                        tf = qk[:, 0:1024].rearrange("p (h d) -> p h d", d=64)
                        step.do(dve.tensor_tensor(tf, of, of, ALU.mult))
                        dve.tensor_reduce(small[:, 64:80], tf, AX, ALU.add).then_inc(subsq_ok.sem, 1)
                        dve.wait_ge(subrs_ok.sem, subrs_ok.at(l, 1))
                        step.do(dve.tensor_tensor(of, of, bcast(small[:, 80:96].unsqueeze(2), [P, 16, 64]), ALU.mult))
                        dve.tensor_tensor(of, of, bcast(curb[:, B_SUB:B_SUB + 64].unsqueeze(1), [P, 16, 64]), ALU.mult).then_inc(o_ok.sem, 1)
                    else:
                        dve.tensor_copy(small[:, 470:471], o[:, 0, 0:1]).then_inc(o_ok.sem, 1)
                    dve.wait_ge(o_turned.sem, o_turned.at(l, 2 * br + 2))
                    dve.tensor_copy(yT[:, 4 * br + 2:4 * br + 4, :], T[1][:, :].rearrange("p (k s) -> p k s", k=2)).then_inc(y_dve.sem, 1)

                attend(0, 8, 0, 8, A_DIM ** -0.5, 0)
                attend(8, 16, 8, 8, B_DIM ** -0.5, 1)
                for i in range(1, 8, 2):
                    dve.wait_ge(qk_turned.sem, qk_turned.at(l, 7 + i + 1))
                    dst = (cqT if i < 4 else ckT)[:, 2 * (i % 4):2 * (i % 4) + 2, :]
                    dve.tensor_copy(dst, T[(7 + i) % 2][0:C_QK, :].rearrange("p (k s) -> p k s", k=2)).then_inc(qk_dve.sem, 1)
                attend(24, 8, 16, 8, C_QK ** -0.5, 2)
                dve.wait_ge(gate_ev.sem, gate_ev.at(l, 16) + 4)
                for n in range(3):
                    for half in range(2):
                        for b in range(NB):
                            j = 2 * half + b
                            if j < 3:
                                dve.wait_ge(br_mm.sem, br_mm.at(l, 3 * n + j + 1))
                            else:
                                dve.wait_ge(used[(18 + n) % NSLOT].sem, used_at(l, 18 + n))
                            gt = gates[:, b, n * D + half * 512:n * D + (half + 1) * 512]
                            m = merged[:, b, half * 512:(half + 1) * 512]
                            if n == 0:
                                dve.tensor_tensor(m, G[j][:, :], gt, ALU.mult).then_inc(br_ev.sem, 1)
                            else:
                                dve.tensor_tensor(gated[:, j % 2], G[j][:, :], gt, ALU.mult).then_inc(br_ev.sem, 1)
                                dve.wait_ge(br_ev.sem, br_ev.at(l, 4 * n + j + 1))
                                ins = dve.tensor_tensor(m, m, gated[:, j % 2], ALU.add)
                                if (n, j) == (2, 3):
                                    ins.then_inc(merged_ok.sem, 1)
                                else:
                                    step.did(ins)
                    if n:
                        step.settle()
                turned_evac(l, mg_turned, mg_dve, None)
                dve.wait_ge(used[23 % NSLOT].sem, used_at(l, 23))
                add_to_x()
                normalise(l * 2 + 1, l * 2 + 1)
                turned_evac(l * 2 + 1, xn_turned, hT_dve, cur[:, KD:2 * KD])
                with dve.Fori(0, 4) as it:
                    for j in range(2):
                        for f in range(4):
                            dve.wait_ge(ff_relu.sem, l * 32 + it * 8 + (j * 4 + f + 1 + 4))
                            dve.tensor_tensor(hid[:, j, f, :], hid[:, j, f, :], hid[:, j, f, :], ALU.mult).then_inc(ff_ev.sem, 1)
                dve.wait_ge(ff2_mm.sem, ff2_mm.at(l, 1))
                add_to_x()
            assert step.n == DVE_STEPS, step.n
            step.base, step.n = DEPTH * DVE_STEPS, 0

            gF = arena[:, 0:D]
            dve.wait_ge(fin_in.sem, 16)
            dve.wait_ge(rstd_ok.sem, rstd_ok.at(U_FIN1, 1))
            for b in range(NB):
                ins = dve.scalar_tensor_tensor(out=x[:, b, :], in0=x[:, b, :], scalar=small[:, 2 + b:3 + b], in1=gF, op0=ALU.mult, op1=ALU.mult)
                if b == 0:
                    step.did(ins)
                else:
                    ins.then_inc(blk1_done.sem, 1)
            dve.wait_ge(cond_ok.sem, 1)
            step.do(dve.tensor_tensor(condc, condc, cols[:, 0, R_C:R_C + KD], ALU.mult))
            dve.tensor_copy(condB, bcast(condc.unsqueeze(2), [P, KD, P])).then_inc(condB_ok.sem, 1)
            dve.wait_ge(mix_in.sem, 16 * N_MIX)
            dve.wait_ge(half_ok.sem, 2 + KCONV)
            for l in range(DEPTH):
                u = U_MIX + 2 * l
                dve.wait_ge(mixl_in[l].sem, 16 * N_MIXL)
                dve.wait_ge(used[3].sem, used2_at(l, 7))
                for i in range(2):
                    ab = l * MODS * KD + i * 3 * KD
                    step.did(dve.tensor_tensor(modc[:, 16 * i:16 * i + 16], S[0][:, 16 * i:16 * i + 16], cols[:, 1, ab:ab + 16], ALU.add))
                step.settle()
                for i, r in enumerate((R2_MIXG, R2_FFNG)):
                    ins = dve.scalar_tensor_tensor(out=mulc[:, KD * i:KD * i + KD], in0=modc[:, 16 * i + KD:16 * i + 2 * KD], scalar=1.0,
                                                   in1=cols[:, 2, r + l * KD:r + l * KD + KD], op0=ALU.add, op1=ALU.mult)
                    if i == 0:
                        step.do(ins)
                    else:
                        ins.then_inc(mods_ok.sem, 1)
                normalise(u, u - 1)
                dve.wait_ge(mods_ok.sem, l + 1)
                turned_evac(u - 1, xn_turned, hT_dve, mulc[:, 0:KD], modc[:, 0:KD])
                for b in range(NB):
                    if b == 0:
                        dve.wait_ge(w2_mm.sem, w2_mm.at(l, 1))
                        step.did(dve.tensor_copy(poolA[:, b, :], G[b][:, 0:POOL_W]))
                    else:
                        dve.wait_ge(used[8 % NSLOT].sem, used2_at(l, 8))
                        dve.tensor_copy(poolA[:, b, :], G[b][:, 0:POOL_W]).then_inc(pool_ev.sem, 1)
                dve.wait_ge(used[9 % NSLOT].sem, used2_at(l, 9))
                for c in range(KCONV):
                    dve.wait_ge(conv_sg.sem, conv_sg.at(l, c + 1))
                    dve.tensor_tensor(glu[:, c, HALO:HALO + SEQ], (G[2], G[3], S[0])[c][:, 0:SEQ], sg[:, c, :], ALU.mult).then_inc(glu_ok.sem, 1)
                for j in range(2):
                    dve.wait_ge(diff_mm.sem, diff_mm.at(l, j + 1))
                    dve.tensor_copy(diffT[:, j, :], T[j][:, 0:SEQ]).then_inc(diff_ev.sem, 1)
                for j in range(2):
                    dve.wait_ge(sw_turned.sem, sw_turned.at(l, j + 1))
                    dve.tensor_copy(swT[:, 3 * j:3 * j + 3, :], T[j][:, 0:3 * P].rearrange("p (h q) -> p h q", h=3)).then_inc(sw_ev.sem, 1)
                for j in range(2):
                    dve.wait_ge(poolo_mm.sem, poolo_mm.at(l, j + 1))
                    dve.tensor_scalar(mixT[:, j, :], S[j][:, 0:SEQ], cols[:, 2, R2_PS + 2 * l + j:R2_PS + 2 * l + j + 1], None, ALU.mult).then_inc(poolo_ev.sem, 1)
                dve.wait_ge(uv_ev.sem, uv_ev.at(l, 4))
                for b in range(NB):
                    step.did(dve.bn_stats(small[:, 150 + 6 * b:156 + 6 * b], vs[:, b, :]))
                step.settle()
                for b in range(NB):
                    step.did(dve.bn_aggr(small[:, 162 + 2 * b:164 + 2 * b], small[:, 150 + 6 * b:156 + 6 * b]))
                step.settle()
                for b in range(NB):
                    ins = dve.tensor_scalar(small[:, 98 + b:99 + b], small[:, 163 + 2 * b:164 + 2 * b], EPS, None, ALU.add)
                    if b == 0:
                        step.do(ins)
                    else:
                        ins.then_inc(vvar_ok.sem, 1)
                dve.wait_ge(vrs_ok.sem, l + 1)
                for b in range(NB):
                    step.did(dve.tensor_scalar(vs[:, b, :], vs[:, b, :], small[:, 162 + 2 * b:163 + 2 * b], small[:, 100 + b:101 + b], ALU.subtract, ALU.mult))
                step.settle()
                step.do(dve.tensor_tensor(vs, vs, bcast(sguG.unsqueeze(1), [P, NB, SGU_W]), ALU.mult))
                dve.tensor_tensor(vs, vs, bcast(sguB.unsqueeze(1), [P, NB, SGU_W]), ALU.add).then_inc(vn_ok.sem, 1)
                for h in range(SGU_HEADS):
                    dve.wait_ge(sgu_mm.sem, sgu_mm.at(l, h // 4 + 1))
                    src = G[h // 4][:, (h % 4) * P:(h % 4 + 1) * P].rearrange("p (b d) -> p b d", b=NB)
                    ins = dve.scalar_tensor_tensor(out=outc[:, :, h * SGU_D:(h + 1) * SGU_D], in0=src,
                                                   scalar=cols[:, 2, R2_SB + l * SGU_HEADS + h:R2_SB + l * SGU_HEADS + h + 1],
                                                   in1=us[:, :, h * SGU_D:(h + 1) * SGU_D], op0=ALU.add, op1=ALU.mult)
                    if h < SGU_HEADS - 1:
                        step.did(ins)
                    else:
                        ins.then_inc(outc_ok.sem, 1)
                dve.wait_ge(glu_ok.sem, glu_ok.at(l, 3))
                for c in range(KCONV):
                    step.did(dve.tensor_scalar(cacc[:, c, :], glu[:, c, 0:SEQ], cwc[:, l, c, 0:1],
                                               cols[:, 2, R2_CB + l * KCONV + c:R2_CB + l * KCONV + c + 1], ALU.mult, ALU.add))
                step.settle()
                for tap in range(1, TAPS):
                    for c in range(KCONV):
                        ins = dve.scalar_tensor_tensor(out=cacc[:, c, :], in0=glu[:, c, tap:tap + SEQ], scalar=cwc[:, l, c, tap:tap + 1],
                                                       in1=cacc[:, c, :], op0=ALU.mult, op1=ALU.add)
                        if (tap, c) == (TAPS - 1, KCONV - 1):
                            ins.then_inc(cacc_ok.sem, 1)
                        else:
                            step.did(ins)
                    step.settle()
                for c in range(4):
                    dve.wait_ge(used[(13 + c) % NSLOT].sem, used2_at(l, 13 + c))
                    gb = gateB[:, c // 2, (c % 2) * 512:(c % 2 + 1) * 512]
                    ins = dve.tensor_tensor(gb, G[c][:, :], gb, ALU.add)
                    if c < 3:
                        step.did(ins)
                    else:
                        ins.then_inc(adaG_ev.sem, 1)
                dve.wait_ge(cmean_mm.sem, l + 1)
                for c in range(KCONV):
                    step.did(dve.scalar_tensor_tensor(out=cacc[:, c, :], in0=S[0][:, 0:SEQ], scalar=-1.0 / CONV_W, in1=cacc[:, c, :], op0=ALU.mult, op1=ALU.add))
                step.settle()
                for c in range(KCONV):
                    ins = dve.tensor_tensor(csq[:, c, :], cacc[:, c, :], cacc[:, c, :], ALU.mult)
                    if c < KCONV - 1:
                        step.did(ins)
                    else:
                        ins.then_inc(cdev_ok.sem, 1)
                dve.wait_ge(cvar_mm.sem, l + 1)
                dve.tensor_scalar(crstd, S[1][:, 0:SEQ], 1.0 / CONV_W, EPS, ALU.mult, ALU.add).then_inc(cvar_ok.sem, 1)
                dve.wait_ge(crstd_ok.sem, l + 1)
                for c in range(KCONV):
                    step.did(dve.tensor_tensor(cacc[:, c, :], cacc[:, c, :], crstd, ALU.mult))
                step.settle()
                for c in range(KCONV):
                    gc = cols[:, 2, R2_CG + l * KCONV + c:R2_CG + l * KCONV + c + 1]
                    bcc = cols[:, 2, R2_CLB + l * KCONV + c:R2_CLB + l * KCONV + c + 1]
                    dve.tensor_scalar(cacc[:, c, :], cacc[:, c, :], gc, bcc, ALU.mult, ALU.add).then_inc(cln_ok.sem, 1)
                dve.wait_ge(cln_ok.sem, cln_ok.at(l, 3))
                for c in range(KCONV):
                    dve.wait_ge(csig_ok.sem, csig_ok.at(l, c + 1))
                    dve.tensor_tensor(mixT[:, 2 + c, :], cacc[:, c, :], sg[:, c, :], ALU.mult).then_inc(conv_ok.sem, 1)
                dve.wait_ge(adaG_ev.sem, l + 1)
                dve.wait_ge(used[19 % NSLOT].sem, used2_at(l, 19))
                add_to_x(0, X1 + 1 + 8 * l)
                dve.wait_ge(x_new.sem, X1 + 1 + 8 * l + 4)
                normalise(u + 1, u)
                turned_evac(u, xn_turned, hT_dve, mulc[:, KD:2 * KD], modc[:, 16:16 + KD])

                def hidden(n, i, count):
                    for f in range(FT):
                        dve.wait_ge(fsg_ok.sem, n * FT + (f + 1))
                        dve.tensor_tensor(ffsg[:, f, :], H4[2 * f][:, 0:SEQ], ffsg[:, f, :], ALU.mult).then_inc(ft_ok.sem, 1)
                        if f == 0:
                            dve.wait_ge(fu_mm.sem, n + 1)
                        else:
                            dve.wait_ge(sub_used[i][1].sem, count)
                        dve.wait_ge(ft_ok.sem, n * FT + (f + 1))
                        dve.tensor_tensor(ffhid[:, i, f, :], H4[2 * f + 1][:, 0:SEQ], ffsg[:, f, :], ALU.mult).then_inc(fhid_ok.sem, 1)

                if l == 0:
                    with dve.Fori(0, 5) as it:
                        for i in range(2):
                            hidden(it * 2 + i, i, it + 2)
                    hidden(10, 0, 7)
                    dve.wait_ge(fdn_done.sem, 1)
                    add_to_x(1, X1 + 1 + 8 * l + 4)
                else:
                    dve.wait_ge(rt_mm.sem, 1)
                    lg = small[:, 160:176].rearrange("p (b e) -> p b e", b=NB)
                    step.do(dve.tensor_tensor(lg, S[0][:, 0:NB * EXPERTS].rearrange("p (b e) -> p b e", b=NB), bcast(rb.unsqueeze(1), [P, NB, EXPERTS]), ALU.add))
                    for b in range(NB):
                        step.did(dve.max(small[:, 176 + 8 * b:184 + 8 * b], lg[:, b, :]))
                    step.settle()
                    mx = small[:, 176:192].rearrange("p (b e) -> p b e", b=NB)
                    for b in range(NB):
                        step.did(dve.max_index(idx[:, b, :], mx[:, b, :], lg[:, b, :]))
                    dve.tensor_tensor(small[:, 196:198], mx[:, :, 1], mx[:, :, 0], ALU.subtract).then_inc(rt_max.sem, 1)
                    step.settle()
                    idf = small[:, 208:224].rearrange("p (b e) -> p b e", b=NB)
                    step.do(dve.tensor_copy(idf, idx[:, :, :]))
                    dve.wait_ge(rt_exp.sem, 1)
                    step.do(dve.tensor_scalar(small[:, 202:204], small[:, 200:202], 1.0, None, ALU.add))
                    step.do(dve.reciprocal(small[:, 204:206], small[:, 202:204]))
                    step.do(dve.tensor_tensor(small[:, 206:208], small[:, 200:202], small[:, 204:206], ALU.mult))
                    for b in range(NB):
                        first, second = small[:, 310 + 16 * b:318 + 16 * b], small[:, 318 + 16 * b:326 + 16 * b]
                        step.did(dve.tensor_scalar(first, io8, idf[:, b, 0:1], None, ALU.is_equal))
                        step.did(dve.tensor_scalar(second, io8, idf[:, b, 1:2], None, ALU.is_equal))
                    step.did(dve.memset(place, -1.0))
                    step.did(dve.memset(weight, 0.0))
                    step.did(dve.memset(yacc, 0.0))
                    step.settle()
                    for b in range(NB):
                        first, second = small[:, 310 + 16 * b:318 + 16 * b], small[:, 318 + 16 * b:326 + 16 * b]
                        step.do(dve.tensor_tensor(chosen[:, b, :], first, second, ALU.add))
                        step.did(dve.tensor_scalar(first, first, small[:, 204 + b:205 + b], None, ALU.mult))
                        step.do(dve.tensor_scalar(second, second, small[:, 206 + b:207 + b], None, ALU.mult))
                        ins = dve.tensor_tensor(weight[:, b, 0:EXPERTS], first, second, ALU.add)
                        if b == 0:
                            step.do(ins)
                        else:
                            ins.then_inc(chosen_ok.sem, 1)
                    dve.wait_ge(rank_mm.sem, 1)
                    step.did(dve.tensor_copy(counts[:], S[0][:, 32:40]))
                    step.do(dve.scalar_tensor_tensor(out=place[:, :, 0:EXPERTS], in0=S[0][:, 16:32].rearrange("p (b e) -> p b e", b=NB),
                                                     scalar=1.0, in1=chosen, op0=ALU.add, op1=ALU.mult))
                    dve.tensor_scalar(place[:, :, 0:EXPERTS], place[:, :, 0:EXPERTS], -1.0, None, ALU.add).then_inc(counts_ok.sem, 1)
                    dve.wait_ge(chosen_ok.sem, 1)
                    dve.wait_ge(counts_ok.sem, 1)

                    def select(e):
                        dve.tensor_copy(curp.unsqueeze(2), place[:, :, bass.ds(e, 1)])
                        dve.tensor_copy(curw.unsqueeze(2), weight[:, :, bass.ds(e, 1)]).then_inc(cur_loaded.sem, 1)
                        dve.wait_ge(cur_loaded.sem, e + 1)
                        for b in range(NB):
                            ins = dve.tensor_scalar(sel[:, b, :], slots, curp[:, b:b + 1], None, ALU.is_equal)
                        ins.then_inc(sel_ok.sem, 1)

                    def expert(e, w):
                        dve.wait_ge(gath_mm.sem, e + 1)
                        for k in range(KD):
                            bank, c0 = gather_bank(k, w)
                            if bank % 2 == 1:
                                ins = dve.tensor_scalar(hTe[:, k, 0:w], H4[bank][:, c0:c0 + w], mulc[:, KD + k:KD + k + 1], modc[:, 16 + k:17 + k], ALU.mult, ALU.add)
                        ins.then_inc(hTe_dve.sem, 1)
                        for b in range(NB):
                            ins = dve.tensor_scalar(selw[:, b, 0:P * len(blocks(w))], slots[:, 0:P * len(blocks(w))], curp[:, b:b + 1], curw[:, b:b + 1], ALU.is_equal, ALU.mult)
                        ins.then_inc(selw_ok.sem, 1)
                        dve.wait_ge(sel_ok.sem, e + 1)
                        dve.wait_ge(selw_ok.sem, e + 1)
                        select(e + 1)
                        with dve.Fori(0, ESTEPS // 2) as it:
                            for i in range(2):
                                n = e * ESTEPS + it * 2
                                dve.wait_ge(esg_ok.sem, n + (i + 1))
                                dve.tensor_tensor(emsg[:, i, 0:FT * w], H4[2 * i][:, 0:FT * w], emsg[:, i, 0:FT * w], ALU.mult).then_inc(et_ok.sem, 1)
                                dve.wait_ge(sub_used[i][1].sem, e * (ESTEPS // 2) + it + (8 - i))
                                dve.wait_ge(et_ok.sem, n + (i + 1))
                                dve.tensor_tensor(ehid[:, i, 0:FT * w], H4[2 * i + 1][:, 0:FT * w], emsg[:, i, 0:FT * w], ALU.mult).then_inc(ehid_ok.sem, 1)
                        dve.wait_ge(edn_done.sem, e + 1)
                        for i, s0, n in blocks(w):
                            ins = dve.tensor_copy(ye[0:n, i, 0:512], G[i][0:n, :])
                        ins.then_inc(ye_dve.sem, 1)
                        dve.wait_ge(scat_ev.sem, e * 4 + 1)
                        for half in range(2):
                            for b in range(NB):
                                j = 2 * half + b
                                ys = yacc[:, b, half * 512:(half + 1) * 512]
                                dve.wait_ge(scat_mm.sem, e * 4 + (j + 1))
                                dve.tensor_tensor(ys, G[j][:, :], ys, ALU.add).then_inc(scat_ev.sem, 1)

                    select(0)
                    each_expert(dve, expert)
                    dve.wait_ge(scat_ev.sem, EXPERTS * 4 + 1)
                    for half in range(2):
                        for b in range(NB):
                            hs = slice(half * 512, (half + 1) * 512)
                            step.do(dve.tensor_tensor(yacc[:, b, hs], yacc[:, b, hs], gateB[:, 1, hs], ALU.mult))
                            dve.tensor_tensor(x[:, b, hs], x[:, b, hs], yacc[:, b, hs], ALU.add).then_inc(x_new.sem, 1)
            dve.wait_ge(rstd_ok.sem, rstd_ok.at(U_FIN2, 1))
            for b in range(NB):
                dve.scalar_tensor_tensor(out=x[:, b, :], in0=x[:, b, :], scalar=small[:, 2 + b:3 + b], in1=finB, op0=ALU.mult, op1=ALU.mult).then_inc(out_ok.sem, 1)

        @block.tensor
        def _(pe):
            mm = pe.matmul

            def weights(l, pos, at=None):
                i = pos % NSLOT
                pe.wait_ge(loaded[i].sem, (l * (L1_CHUNKS // NSLOT) + pos // NSLOT + 1) * 16 if at is None else at)
                return slot(pos)

            def turn(v, src, ready, count, turned, done_a, done_d, whole=True):
                pe.wait_ge(ready.sem, count)
                for i in range(4):
                    if i == 2:
                        pe.wait_ge(done_a.sem, done_a.at(v, 1))
                    if i == 3:
                        pe.wait_ge(done_d.sem, done_d.at(v, 1))
                    for kk in range(2):
                        for b in range(NB):
                            k = 2 * i + kk
                            ins = pe.transpose(T[i % 2][:, kk * SEQ + b * P:kk * SEQ + (b + 1) * P], src[:, b, k * P:(k + 1) * P], ident[:])
                    ins.then_inc(turned.sem, 1)
                if whole:
                    pe.wait_ge(done_a.sem, done_a.at(v, 2))
                    pe.wait_ge(done_d.sem, done_d.at(v, 2))

            def open_banks():
                for j in range(4):
                    mm(G[j][:, 0:2], ident[:], zcol[:], start=True, stop=False, skip_group_check=True)

            def close_banks(done):
                for j in range(4):
                    ins = mm(G[j][:, 0:2], ident[:], zcol[:], start=False, stop=True, skip_group_check=True)
                ins.then_inc(done.sem, 1)

            pe.wait_ge(ident_ok.sem, 2)
            pe.wait_ge(zero_ok.sem, 1)
            pe.wait_ge(rows_in.sem, 16 * N_ROWS)
            for i, n in enumerate((R_C + KD, DEPTH * MODS * KD, R2_N)):
                ins = pe.transpose(T[0][:, i * P:i * P + n], rows[0:n, i, :], ident[0:n, 0:n])
            ins.then_inc(rows_turned.sem, 1)
            for l in range(DEPTH):
                for c in range(KCONV):
                    ins = pe.transpose(T[1][:, l * 128 + c * TAPS:l * 128 + (c + 1) * TAPS], cwr[:, l, c * P:(c + 1) * P], ident[0:TAPS, 0:TAPS])
            ins.then_inc(rows_turned.sem, 1)
            pe.wait_ge(cols_ok.sem, 2)

            with pe.Fori(0, DEPTH) as l:
                turn(l * 2, xn, xn_ok, xn_ok.at(l * 2, 2), xn_turned, hT_act, hT_dve, whole=False)
                for part, n in ((0, PROJ_N), (1, GATE_N)):
                    with pe.Fori(0, 2) as it:
                        if part == 0:
                            pe.wait_ge(hT_act.sem, hT_act.at(l * 2, 2))
                            pe.wait_ge(hT_dve.sem, hT_dve.at(l * 2, 2))
                        else:
                            pe.wait_ge(proj_act.sem, proj_act.at(l, 8) + 2)
                            pe.wait_ge(proj_dve.sem, proj_dve.at(l, 8) + 2)
                        for c in range(NSLOT):
                            w = weights(l, 8 * part + c, (l * 10 + it + (2 * part + 1)) * 16)[:, 0:KD * n].rearrange("p (k n) -> p k n", k=KD)
                            for b in range(NB):
                                if part == 0:
                                    pe.wait_ge((proj_act if b == 0 else proj_dve).sem, l * 8 + it * 4 + (c + 1))
                                else:
                                    pe.wait_ge(gate_ev.sem, l * 16 + it * 8 + (2 * c + b + 1))
                                for k in range(KD):
                                    ins = mm(G[2 * (c % 2) + b][:, 0:n], hT[:, k, b * P:(b + 1) * P], w[:, k, :], start=(k == 0), stop=(k == KD - 1))
                                ins.then_inc(((proj_mm, gate_mm)[part] if b == 0 else used[c]).sem, 1)
                pe.wait_ge(cn_ok.sem, cn_ok.at(l, 1))
                for i in range(3):
                    if i == 2:
                        pe.wait_ge(cn_ev.sem, cn_ev.at(l, 1))
                    for kk in range(2 if i < 2 else 1):
                        for b in range(NB):
                            c0 = O_CQ + (2 * i + kk) * P
                            ins = pe.transpose(T[i % 2][:, kk * SEQ + b * P:kk * SEQ + (b + 1) * P], proj[:, b, c0:c0 + P], ident[:])
                    ins.then_inc(cn_turned.sem, 1)
                pe.wait_ge(rope_ok.sem, rope_ok.at(l, 1))
                pe.wait_ge(cn_ev.sem, cn_ev.at(l, 3))
                src = ([(aqr, 256 * i) for i in range(2)] + [(akr, 0)] + [(proj, O_BQ + 256 * i) for i in range(4)])
                for i, (s, c0) in enumerate(src):
                    if i >= 2:
                        (pe.wait_ge(qk_act.sem, qk_act.at(l, i // 2)) if i % 2 == 0 else pe.wait_ge(qk_dve.sem, qk_dve.at(l, i // 2)))
                    for kk in range(1 if i == 2 else 2):
                        for b in range(NB):
                            ins = pe.transpose(T[i % 2][:, kk * SEQ + b * P:kk * SEQ + (b + 1) * P], s[:, b, c0 + kk * P:c0 + (kk + 1) * P], ident[:])
                    ins.then_inc(qk_turned.sem, 1)
                pe.wait_ge(gate_ev.sem, gate_ev.at(l, 16) + 4)
                w = weights(l, 16)[:, 0:KCQ * 768].rearrange("p (k n) -> p k n", k=KCQ)
                for half in range(2):
                    for b in range(NB):
                        j = 2 * half + b
                        for k in range(KCQ):
                            ins = mm(G[j][:, 0:384], cnT[:, k, b * P:(b + 1) * P], w[:, k, half * 384:(half + 1) * 384], start=(k == 0), stop=(k == KCQ - 1))
                        ins.then_inc((up_mm if j < 3 else used[0]).sem, 1)
                w = weights(l, 17)[:, 0:KCKV * 1024].rearrange("p (k n) -> p k n", k=KCKV)
                for half in range(2):
                    for b in range(NB):
                        j = 2 * half + b
                        pe.wait_ge(up_ev.sem, up_ev.at(l, j + 1))
                        for k in range(KCKV):
                            ins = mm(G[j][:, :], cnT[:, KCQ + k, b * P:(b + 1) * P], w[:, k, half * 512:(half + 1) * 512], start=(k == 0), stop=(k == KCKV - 1))
                        ins.then_inc((up_mm if j < 3 else used[1]).sem, 1)

                def attend(s0, ns, u0, nu, q_at, k_at, v_at, ready):
                    lead = ns // nu

                    def scores(s):
                        if s >= 2:
                            pe.wait_ge(exp_ok.sem, exp_ok.at(l, s - 1))
                        for b in range(NB):
                            ins = mm(S[s % 2][:, b * SEQ:(b + 1) * SEQ], q_at(s - s0, b), k_at(s - s0), start=True, stop=True)
                        ins.then_inc(sc_mm.sem, 1)

                    for s in range(lead):
                        scores(s0 + s)
                    for i in range(nu):
                        u, s = u0 + i, s0 + i * lead
                        if lead == 2:
                            pe.wait_ge(pcomb_ok.sem, pcomb_ok.at(l, i + 1))
                        else:
                            pe.wait_ge(exp_ok.sem, exp_ok.at(l, s + 1))
                        if u >= 2:
                            pe.wait_ge(pT_ok.sem, pT_ok.at(l, u - 1))
                        for kb in range(NB):
                            for b in range(NB):
                                ins = pe.transpose(T[u % 2][:, kb * SEQ + b * P:kb * SEQ + (b + 1) * P], probs[:, s % 4, b * SEQ + kb * P:b * SEQ + (kb + 1) * P], ident[:])
                        ins.then_inc(p_turned.sem, 1)
                        if i + 1 < nu:
                            for j in range(lead):
                                scores(s + lead + j)
                        pe.wait_ge(pT_ok.sem, pT_ok.at(l, u + 1))
                        if u >= 2:
                            pe.wait_ge(o_ev.sem, o_ev.at(l, u - 1))
                        for b in range(NB):
                            for kb in range(NB):
                                ins = mm(G[u % 2][:, b * 64:(b + 1) * 64], pT[:, u % 2, kb * SEQ + b * P:kb * SEQ + (b + 1) * P], v_at(i, kb), start=(kb == 0), stop=(kb == NB - 1))
                        ins.then_inc(pv_mm.sem, 1)

                def turn_o(br):
                    pe.wait_ge(o_ok.sem, o_ok.at(l, br + 1))
                    for i in range(2):
                        for kk in range(2):
                            for b in range(NB):
                                ins = pe.transpose(T[i][:, kk * SEQ + b * P:kk * SEQ + (b + 1) * P], o[:, b, (2 * i + kk) * P:(2 * i + kk + 1) * P], ident[:])
                        ins.then_inc(o_turned.sem, 1)
                    pe.wait_ge(y_act.sem, y_act.at(l, br + 1))
                    pe.wait_ge(y_dve.sem, y_dve.at(l, br + 1))

                pe.wait_ge(up_ev.sem, up_ev.at(l, 8))
                pe.wait_ge(qk_act.sem, qk_act.at(l, 4))
                pe.wait_ge(qk_dve.sem, qk_dve.at(l, 3))
                attend(0, 8, 0, 8,
                       lambda h, b: aqT[64 * (h // 4):64 * (h // 4) + 64, h % 4, b * P:(b + 1) * P],
                       lambda h: akT[64 * (h // 4):64 * (h // 4) + 64, :],
                       lambda h, kb: proj[:, kb, O_AV + 64 * (h // 4):O_AV + 64 * (h // 4) + 64], None)
                turn_o(0)
                attend(8, 16, 8, 8,
                       lambda j, b: bqT[32 * (j % 4):32 * (j % 4) + 32, j // 4, b * P:(b + 1) * P],
                       lambda j: bkT[32 * (j % 4):32 * (j % 4) + 32, j // 4, :],
                       lambda h, kb: proj[:, kb, O_BV + 64 * h:O_BV + 64 * h + 64], None)
                turn_o(1)
                pe.wait_ge(ropeC_ok.sem, ropeC_ok.at(l, 1))
                for i in range(8):
                    if i >= 2:
                        (pe.wait_ge(qk_act.sem, qk_act.at(l, 4 + i // 2)) if i % 2 == 0 else pe.wait_ge(qk_dve.sem, qk_dve.at(l, 3 + i // 2)))
                    for kk in range(2):
                        for b in range(NB):
                            h = 2 * (i % 4) + kk
                            s = qC if i < 4 else kC
                            ins = pe.transpose(T[(7 + i) % 2][0:C_QK, kk * SEQ + b * P:kk * SEQ + (b + 1) * P], s[:, b, h * C_QK:(h + 1) * C_QK], ident[:])
                    ins.then_inc(qk_turned.sem, 1)
                pe.wait_ge(qk_act.sem, qk_act.at(l, 8))
                pe.wait_ge(qk_dve.sem, qk_dve.at(l, 7))
                attend(24, 8, 16, 8,
                       lambda h, b: cqT[:, h, b * P:(b + 1) * P], lambda h: ckT[:, h, :],
                       lambda h, kb: vC[:, kb, 64 * h:64 * h + 64], None)
                turn_o(2)
                for n in range(3):
                    w = weights(l, 18 + n).rearrange("p (k n) -> p k n", k=4)
                    for half in range(2):
                        for b in range(NB):
                            j = 2 * half + b
                            if n:
                                pe.wait_ge(br_ev.sem, br_ev.at(l, 4 * (n - 1) + j + 1))
                            for k in range(4):
                                ins = mm(G[j][:, :], yT[:, 4 * n + k, b * P:(b + 1) * P], w[:, k, half * 512:(half + 1) * 512], start=(k == 0), stop=(k == 3))
                            ins.then_inc((br_mm if j < 3 else used[(18 + n) % NSLOT]).sem, 1)
                turn(l, merged, merged_ok, merged_ok.at(l, 1), mg_turned, mg_act, mg_dve)
                k = 0
                for n, kn in enumerate((3, 3, 2)):
                    w = weights(l, 21 + n)[:, 0:kn * D].rearrange("p (k n) -> p k n", n=D)
                    for kk in range(kn):
                        for half in range(2):
                            for b in range(NB):
                                ins = mm(G[2 * half + b][:, :], hT[:, k, b * P:(b + 1) * P], w[:, kk, half * 512:(half + 1) * 512], start=(k == 0), stop=(k == KD - 1))
                        k += 1
                    ins.then_inc(used[(21 + n) % NSLOT].sem, 1)
                turn(l * 2 + 1, xn, xn_ok, xn_ok.at(l * 2 + 1, 2), xn_turned, hT_act, hT_dve)
                open_banks()
                with pe.Fori(0, 4) as it:
                    for j in range(2):
                        w = weights(l, 2 * j, (l * 10 + it + 7) * 16).rearrange("p (k n) -> p k n", k=KD)
                        for f in range(4):
                            pe.wait_ge(ff_relu.sem, l * 32 + it * 8 + (4 * j + f + 1))
                            for k in range(KD):
                                ins = mm(H4[f][:, 0:SEQ], w[:, k, f * P:(f + 1) * P], hT[:, k, :], start=(k == 0), stop=(k == KD - 1))
                            ins.then_inc((ff_mm if f < 3 else used[2 * j]).sem, 1)
                        w = weights(l, 2 * j + 1, (l * 10 + it + 7) * 16).rearrange("p (k n) -> p k n", k=4)
                        for f in range(4):
                            pe.wait_ge(ff_ev.sem, l * 32 + it * 8 + (4 * j + f + 1))
                            for half in range(2):
                                for b in range(NB):
                                    ins = mm(G[2 * half + b][:, :], hid[:, j, f, b * P:(b + 1) * P], w[:, f, half * 512:(half + 1) * 512], start=False, stop=False, skip_group_check=True)
                        ins.then_inc(used[2 * j + 1].sem, 1)
                close_banks(ff2_mm)

            pe.wait_ge(condB_ok.sem, 1)
            pe.wait_ge(mix_in.sem, 16 * N_MIX)
            pe.wait_ge(half_ok.sem, 2 + KCONV)
            for l in range(DEPTH):
                v = U_MIX + 2 * l - 1
                b2 = (DEPTH * L1_CHUNKS + l * L2_CHUNKS) // NSLOT
                pe.wait_ge(mixl_in[l].sem, 16 * N_MIXL)
                if l:
                    pe.wait_ge(x_new.sem, X1 + 1 + 8)
                with pe.Fori(0, 2) as it:
                    for c in range(NSLOT):
                        w = weights(0, c, (it + b2 + 1) * 16).rearrange("p (k n) -> p k n", k=KD)
                        for f in range(4):
                            for k in range(KD):
                                ins = mm(S[0][:, bass.ds(it * 16 + 4 * c + f, 1)], w[:, k, f * P:(f + 1) * P], condc[:, k:k + 1], start=(k == 0), stop=(k == KD - 1))
                        ins.then_inc(used[c].sem, 1)
                turn(v, xn, xn_ok, xn_ok.at(v, 2), xn_turned, hT_act, hT_dve)

                def chunk(pos, n=512):
                    return weights(0, pos, (b2 + pos // NSLOT + 1) * 16)[:, 0:KD * n].rearrange("p (k n) -> p k n", k=KD)

                def tokens(pos, n, banks, sem):
                    w = chunk(pos, n)
                    for b in range(NB):
                        for k in range(KD):
                            ins = mm(banks[b][:, 0:n], hT[:, k, b * P:(b + 1) * P], w[:, k, :], start=(k == 0), stop=(k == KD - 1))
                        ins.then_inc((sem if b == 0 else used[pos % NSLOT]).sem, 1)

                def features(pos, n, banks, sem):
                    w = chunk(pos, n)
                    for f in range(n // P):
                        for k in range(KD):
                            ins = mm(banks[f][:, 0:SEQ], w[:, k, f * P:(f + 1) * P], hT[:, k, :], start=(k == 0), stop=(k == KD - 1))
                        ins.then_inc((sem if f < n // P - 1 else used[pos % NSLOT]).sem, 1)

                tokens(8, POOL_W, (G[0], G[1]), w2_mm)
                features(9, CONV_W, (G[2], G[3], S[0]), w2_mm)
                features(10, CONV_W, (S[1], T[0], T[1]), w2_mm)
                pe.wait_ge(pool_ev.sem, l + 1)
                tokens(11, SGU_W, (G[0], G[1]), w2_mm)
                pe.wait_ge(glu_ok.sem, glu_ok.at(l, 3))
                tokens(12, SGU_W, (G[2], G[3]), w2_mm)
                for g in range(4):
                    j, r = g // 2, 64 * (g % 2)
                    for b in range(NB):
                        ins = mm(T[j][r:r + 64, 0:SEQ], poolA[:, b, g * 64:(g + 1) * 64], band[:, b, g, :], start=(b == 0), stop=(b == NB - 1))
                    if g % 2:
                        ins.then_inc(diff_mm.sem, 1)
                for j in range(2):
                    pe.wait_ge(diff_ev.sem, diff_ev.at(l, j + 1))
                    for h in range(3):
                        ins = pe.transpose(T[j][:, h * P:(h + 1) * P], swr[:, 3 * j + h, :], ident[:])
                    ins.then_inc(sw_turned.sem, 1)
                for g in range(4):
                    j, r = g // 2, 64 * (g % 2)
                    ins = mm(S[j][r:r + 64, 0:SEQ], pw[r:r + 64, j, :], diffT[r:r + 64, j, :], start=True, stop=True)
                    if g % 2:
                        ins.then_inc(poolo_mm.sem, 1)
                pe.wait_ge(sw_ev.sem, sw_ev.at(l, 2))
                pe.wait_ge(vn_ok.sem, l + 1)
                for h in range(SGU_HEADS):
                    ins = mm(G[h // 4][:, (h % 4) * P:(h % 4 + 1) * P], swT[:, h, :], vs[:, :, h * SGU_D:(h + 1) * SGU_D], start=True, stop=True)
                    if h in (3, SGU_HEADS - 1):
                        ins.then_inc(sgu_mm.sem, 1)
                pe.wait_ge(outc_ok.sem, l + 1)
                for i in range(2):
                    for kk in range(2 - i):
                        for b in range(NB):
                            k = 2 * i + kk
                            ins = pe.transpose(G[2 + i][:, kk * SEQ + b * P:kk * SEQ + (b + 1) * P], outc[:, b, k * P:(k + 1) * P], ident[:])
                    ins.then_inc(outc_turned.sem, 1)
                pe.wait_ge(outc_ev.sem, outc_ev.at(l, 2))
                for c in range(4):
                    w = chunk(13 + c)
                    for k in range(KD):
                        ins = mm(G[c][:, :], condB[:, k, :], w[:, k, :], start=(k == 0), stop=(k == KD - 1))
                    ins.then_inc(used[(13 + c) % NSLOT].sem, 1)
                pe.wait_ge(poolo_ev.sem, poolo_ev.at(l, 2))
                pe.wait_ge(cacc_ok.sem, l + 1)
                for c in range(KCONV):
                    ins = mm(S[0][:, 0:SEQ], ones, cacc[:, c, :], start=(c == 0), stop=(c == KCONV - 1))
                ins.then_inc(cmean_mm.sem, 1)
                pe.wait_ge(cdev_ok.sem, l + 1)
                for c in range(KCONV):
                    ins = mm(S[1][:, 0:SEQ], ones, csq[:, c, :], start=(c == 0), stop=(c == KCONV - 1))
                ins.then_inc(cvar_mm.sem, 1)
                pe.wait_ge(conv_ok.sem, conv_ok.at(l, 3))
                pe.wait_ge(adaG_ev.sem, l + 1)
                k = 0
                for n, kn in enumerate((3, 3, 2)):
                    w = weights(0, 17 + n, (b2 + (17 + n) // NSLOT + 1) * 16)[:, 0:kn * D].rearrange("p (k n) -> p k n", n=D)
                    for kk in range(kn):
                        for half in range(2):
                            for b in range(NB):
                                ins = mm(G[2 * half + b][:, :], mixT[:, k, b * P:(b + 1) * P], w[:, kk, half * 512:(half + 1) * 512], start=(k == 0), stop=(k == KD - 1))
                        k += 1
                    ins.then_inc(used[(17 + n) % NSLOT].sem, 1)
                turn(v + 1, xn, xn_ok, xn_ok.at(v + 1, 2), xn_turned, hT_act, hT_dve)

                def ffn_step(n, i, count):
                    g, up, dn = (sub(i, piece).rearrange("p (k n) -> p k n", n=(FT * P, FT * P, D)[piece]) for piece in range(3))
                    for piece, w in ((0, g), (1, up)):
                        pe.wait_ge(sub_in[i][piece].sem, count * 16)
                        for f in range(FT):
                            pe.wait_ge(fhid_ok.sem, n * FT + (f + 1))
                            for k in range(KD):
                                ins = mm(H4[2 * f + piece][:, 0:SEQ], w[:, k, f * P:(f + 1) * P], hT[:, k, :], start=(k == 0), stop=(k == KD - 1))
                            ins.then_inc(((fg_mm, fu_mm)[piece] if f == 0 else sub_used[i][piece]).sem, 1)
                    pe.wait_ge(sub_in[i][2].sem, count * 16)
                    for f in range(FT):
                        pe.wait_ge(fhid_ok.sem, n * FT + (f + 1 + FT))
                        for half in range(2):
                            for b in range(NB):
                                ins = mm(G[2 * half + b][:, :], ffhid[:, i, f, b * P:(b + 1) * P], dn[:, f, half * 512:(half + 1) * 512], start=False, stop=False, skip_group_check=True)
                    ins.then_inc(sub_used[i][2].sem, 1)

                if l == 0:
                    open_banks()
                    with pe.Fori(0, 5) as it:
                        for i in range(2):
                            ffn_step(it * 2 + i, i, it + 1)
                    ffn_step(10, 0, 6)
                    close_banks(fdn_done)
                else:
                    for b in range(NB):
                        for k in range(KD):
                            ins = mm(S[0][:, b * EXPERTS:(b + 1) * EXPERTS], hT[:, k, b * P:(b + 1) * P], rw[:, k, :], start=(k == 0), stop=(k == KD - 1))
                    ins.then_inc(rt_mm.sem, 1)
                    pe.wait_ge(chosen_ok.sem, 1)
                    mm(S[0][:, 16:24], tri, chosen[:, 0, :], start=True, stop=True)
                    mm(S[0][:, 24:32], ones, chosen[:, 0, :], start=True, stop=False)
                    mm(S[0][:, 24:32], tri, chosen[:, 1, :], start=False, stop=True)
                    mm(S[0][:, 32:40], ones, chosen[:, 0, :], start=True, stop=False)
                    mm(S[0][:, 32:40], ones, chosen[:, 1, :], start=False, stop=True).then_inc(rank_mm.sem, 1)

                    def gate_up(e, it, i, w):
                        pe.wait_ge(ehid_ok.sem, e * ESTEPS + it * 2 + (i + 1))
                        for piece in range(2):
                            wt = sub(i, piece).rearrange("p (k n) -> p k n", n=FT * P)
                            pe.wait_ge(sub_in[i][piece].sem, (e * (ESTEPS // 2) + it + (7 - i)) * 16)
                            for f in range(FT):
                                for k in range(KD):
                                    ins = mm(H4[2 * i + piece][:, f * w:(f + 1) * w], wt[:, k, f * P:(f + 1) * P], hTe[:, k, 0:w], start=(k == 0), stop=(k == KD - 1))
                            ins.then_inc(sub_used[i][piece].sem, 1)

                    def down(e, it, i, w):
                        wt = sub(i, 2).rearrange("p (k n) -> p k n", n=D)
                        pe.wait_ge(sub_in[i][2].sem, (e * (ESTEPS // 2) + it + (7 - i)) * 16)
                        pe.wait_ge(ehid_ok.sem, e * ESTEPS + it * 2 + (i + 3))
                        for f in range(FT):
                            for half in range(2):
                                for j, s0, n in blocks(w):
                                    ins = mm(G[2 * half + j][0:n, :], ehid[:, i, f * w + s0:f * w + s0 + n], wt[:, f, half * 512:(half + 1) * 512], start=False, stop=False, skip_group_check=True)
                        ins.then_inc(sub_used[i][2].sem, 1)

                    def expert(e, w):
                        pe.wait_ge(sel_ok.sem, e + 1)
                        pe.wait_ge(ehid_ok.sem, e * ESTEPS + 2)
                        for k in range(KD):
                            bank, c0 = gather_bank(k, w)
                            for b in range(NB):
                                ins = mm(H4[bank][:, c0:c0 + w], xn[:, b, k * P:(k + 1) * P], sel[:, b, 0:w], start=(b == 0), stop=(b == NB - 1))
                        ins.then_inc(gath_mm.sem, 1)
                        pe.wait_ge(scat_ev.sem, e * 4 + 1)
                        for half in range(2):
                            for j, s0, n in blocks(w):
                                mm(G[2 * half + j][:, 0:2], ident[:], zcol[:], start=True, stop=False, skip_group_check=True)
                        pe.wait_ge(hTe_act.sem, e + 1)
                        pe.wait_ge(hTe_dve.sem, e + 1)
                        gate_up(e, 0, 0, w)
                        with pe.Fori(0, ESTEPS // 2 - 1) as it:
                            gate_up(e, it, 1, w)
                            down(e, it, 0, w)
                            gate_up(e, it + 1, 0, w)
                            down(e, it, 1, w)
                        last = ESTEPS // 2 - 1
                        gate_up(e, last, 1, w)
                        down(e, last, 0, w)
                        down(e, last, 1, w)
                        for half in range(2):
                            for j, s0, n in blocks(w):
                                ins = mm(G[2 * half + j][:, 0:2], ident[:], zcol[:], start=False, stop=True, skip_group_check=True)
                        ins.then_inc(edn_done.sem, 1)
                        pe.wait_ge(selw_ok.sem, e + 1)
                        for j, s0, n in blocks(w):
                            for b in range(NB):
                                ins = pe.transpose(H4[0][:, j * SEQ + b * P:j * SEQ + (b + 1) * P], selw[:, b, s0:s0 + P], ident[:])
                        ins.then_inc(selT_mm.sem, 1)
                        pe.wait_ge(selT_ok.sem, e + 1)
                        pe.wait_ge(ye_dve.sem, e + 1)
                        pe.wait_ge(ye_act.sem, e + 1)
                        nb = blocks(w)
                        for half in range(2):
                            for b in range(NB):
                                for j, s0, n in nb:
                                    ins = mm(G[2 * half + b][:, :], selT[0:n, j, b * P:(b + 1) * P], ye[0:n, j, half * 512:(half + 1) * 512], start=(j == 0), stop=(j == len(nb) - 1))
                                ins.then_inc(scat_mm.sem, 1)

                    pe.wait_ge(counts_ok.sem, 1)
                    each_expert(pe, expert)


def constants():
    def angles(pos, dim, theta):
        inv = np.float32(theta) ** (-np.arange(0, dim, 2, dtype=np.float32) / np.float32(dim))
        return pos.astype(np.float32)[:, None] * inv.astype(np.float32)[None, :]

    def tables(*angs):
        cos = np.concatenate([np.concatenate([np.cos(a), np.cos(a)], 1) for a in angs], 1)
        sin = np.concatenate([np.concatenate([-np.sin(a), np.sin(a)], 1) for a in angs], 1)
        return np.stack([cos, sin], 1).astype(np.float32)

    pos = np.arange(SEQ)
    band = np.zeros((SEQ, 4, SEQ), np.float32)
    for g, w in enumerate(WINDOWS):
        for s in range(SEQ):
            lo, hi = max(s - w // 2, 0), min(s + w // 2, SEQ)
            band[lo:hi, g, s] = 1.0 / (hi - lo)
            band[s, g, s] -= 1.0
    init = [0.8 - 0.6 * math.exp(-0.3 * l) for l in range(DEPTH)]
    return {
        "rope_a": tables(angles(pos // GRID_W, A_DIM // 2, 10000.0), angles(pos % GRID_W, A_DIM // 2, 10000.0)),
        "rope_b": tables(angles(pos, B_ROT, 500000.0)),
        "rope_c": tables(angles(pos, C_ROPE, 10000.0)),
        "lam_init": np.array([[i, 1.0 - i] for i in init], np.float32),
        "band": band,
        "iota8": np.arange(EXPERTS, dtype=np.float32),
        "slots": np.arange(SEQ, dtype=np.float32),
        "before": np.triu(np.ones((P, P), np.float32), 1),
    }


INPUTS = ["x", "ln1_g", "w_in", "a_q_norm", "a_k_norm", "b_lambda", "b_subln", "c_q_norm", "c_kv_norm", "c_w_uq", "c_w_ukv",
          "w_branch", "w_out", "ln2_g", "w_ff1", "w_ff2", "final_g", "c_2", "ada_w_2", "ada_b_2", "mix_norm_g_2",
          "ffn_norm_g_2", "w_in_2", "pool_w_2", "pool_scale_2", "conv_w_2", "conv_b_2", "conv_ln_g_2", "conv_ln_b_2",
          "sgu_ln_g_2", "sgu_ln_b_2", "sgu_w_2", "sgu_b_2", "w_out_2", "ffn_w_gate_2", "ffn_w_up_2", "ffn_w_down_2",
          "router_w_2", "router_b_2", "moe_w_gate_2", "moe_w_up_2", "moe_w_down_2", "final_norm_g_2"]


def kernel(**inputs):
    import concourse.bacc as bacc
    from concourse.bass_utils import run_bass_kernel_spmd as run

    nc = bacc.Bacc("TRN2", target_bir_lowering=False, num_devices=1)
    arrays, t = {}, {}
    given = {name: inputs[name] for name in INPUTS}
    given.update(constants())
    for name, value in given.items():
        a = np.ascontiguousarray(value)
        arrays[f"in_{name}"] = a
        t[name] = nc.dram_tensor(f"in_{name}", a.shape, mybir.dt.from_np(a.dtype), kind="ExternalInput").ap()
    t["out"] = nc.dram_tensor("out_0", (1, SEQ, D), F32, kind="ExternalOutput").ap()
    build(nc, t)
    r = run(nc, [arrays], core_ids=[0])
    return r.results[0]["out_0"]
```

```python
import math
from contextlib import ExitStack

import numpy as np
import concourse.bass as bass
from concourse import mybir

F32 = mybir.dt.float32
U32 = mybir.dt.uint32
ALU = mybir.AluOpType
ACT = mybir.ActivationFunctionType
AX = mybir.AxisListType.X

P = 128
SEQ = 256
NB = SEQ // P
D = 1024
KD = D // P
DEPTH = 2
EPS = 1e-6
GRID_W = 64

A_HEADS, A_KV, A_DIM = 8, 2, 64
B_HEADS, B_DIM, B_ROT = 8, 32, 8
C_HEADS, C_NOPE, C_ROPE, C_V = 8, 64, 32, 64
C_QK = C_NOPE + C_ROPE
CQ_RANK, CKV_RANK = 384, 256
KCQ, KCKV = CQ_RANK // P, CKV_RANK // P
BR_W = 512
FF = 4 * D
O_AK = A_HEADS * A_DIM
O_AV = O_AK + A_KV * A_DIM
O_BQ = O_AV + A_KV * A_DIM
O_BK = O_BQ + B_HEADS * 2 * B_DIM
O_BV = O_BK + B_HEADS * 2 * B_DIM
O_CQ = O_BV + B_HEADS * 2 * B_DIM
O_CKV = O_CQ + CQ_RANK
O_KR = O_CKV + CKV_RANK
PROJ_W = O_KR + C_ROPE
GATE_W = 3 * D
PROJ_N = PROJ_W // 8
GATE_N = GATE_W // 8

POOL_W, CONV_W, SGU_W = 256, 384, 384
KCONV = CONV_W // P
TAPS = 31
HALO = TAPS // 2
PE_TAPS = 50
SGU_HEADS, SGU_D = 6, 64
WINDOWS = (2, 4, 8, 16)
FF2 = 2816
EXPERTS = 8
FFE = 3584
MODS = 6
ADA_CHUNKS = MODS * D // 512
WIDTHS = (P // 2, P, 160, SEQ)
ESTEPS = FFE // 256

NPROBS = 5
BR_ORDER = (0, 2, 1)
UNITS = ([(0, i, (i,)) for i in range(A_HEADS)]
         + [(1, i, (A_HEADS + 2 * i, A_HEADS + 2 * i + 1)) for i in range(B_HEADS)]
         + [(2, i, (A_HEADS + 2 * B_HEADS + i,)) for i in range(C_HEADS)])
NSLOT = 4
SLOT = 4096
SUB = 2048
L1_CHUNKS = 40
L2_CHUNKS = 8
FT = 2

ROW_L1 = 2 * KD + KCQ + KCKV
R_C = DEPTH * ROW_L1
R2_MIXG, R2_FFNG = 0, DEPTH * KD
R2_PS = 2 * DEPTH * KD
R2_CB = R2_PS + DEPTH * 2
R2_CG = R2_CB + DEPTH * KCONV
R2_CLB = R2_CG + DEPTH * KCONV
R2_SB = R2_CLB + DEPTH * KCONV
R2_N = R2_SB + DEPTH * SGU_HEADS
B_AQ, B_AK, B_SUB, B_LAM, B_INIT = 0, 64, 128, 192, 320
B_N = 322


class Signal:

    def __init__(self, sem, per):
        self.sem, self.per = sem, per

    def at(self, u, k):
        return u * self.per + k


class Steps:

    def __init__(self, eng, sem):
        self.eng, self.sem, self.base, self.n = eng, sem, 0, 0

    def did(self, ins):
        ins.then_inc(self.sem, 1)
        self.n += 1

    def settle(self):
        self.eng.wait_ge(self.sem, self.base + self.n)

    def do(self, ins):
        self.did(ins)
        self.settle()


DVE_STEPS, POOL_STEPS = 93, 12
N_CONST = 3 + 5 * DEPTH
N_ROWS = 4 * DEPTH + 2 + 6 + 2
N_MIX = 7
N_MIXL = 5


def build(nc, t):
    ctx = ExitStack()
    with ctx:
        def sb(name, shape, dt=F32):
            return ctx.enter_context(nc.sbuf_tensor(name, shape, dt))

        def sig(name, per=0):
            return Signal(ctx.enter_context(nc.semaphore(name)), per)

        ring = sb("ring", [P, NSLOT * SLOT])
        x = sb("x", [P, NB, D])
        hT = sb("hT", [P, KD, SEQ])
        rot = sb("rot", [P, 4096])
        arena = sb("arena", [P, 12288])
        qk = sb("qk", [P, 4096])
        yT = sb("yT", [P, 13, SEQ])
        probs = sb("probs", [P, NPROBS, NB * SEQ])
        diag = sb("diag", [P, 2, 2, NB * P])
        pT = sb("pT", [P, 2, 2 * SEQ])
        o = sb("o", [P, NB, BR_W])
        ident = sb("ident", [P, P])
        cols = sb("cols", [P, 3, P])
        bc = sb("bc", [P, DEPTH, B_N])
        cur = sb("cur", [P, ROW_L1])
        curb = sb("curb", [P, B_N])
        cwc = sb("cwc", [P, DEPTH, KCONV, TAPS])
        ropeA = sb("ropeA", [P, NB, 2, A_DIM])
        ropeB = sb("ropeB", [P, NB, 2, B_ROT])
        ropeC = sb("ropeC", [P, NB, 2, C_ROPE])
        small = sb("small", [P, 512])
        mhalf = sb("mhalf", [P, 20])
        epsc = sb("epsc", [P, 20])
        inverse = {n: sb(f"inverse{n}", [P, 20]) for n in (D, A_DIM, CQ_RANK, CKV_RANK)}
        zcol = sb("zcol", [P, 2])
        onec = sb("onec", [P, 2])
        mods = sb("mods", [P, DEPTH, MODS * KD])
        idx = sb("idx", [P, NB, 8], U32)
        counts = sb("counts", [P, EXPERTS], mybir.dt.int32)

        xn = rot[:, 0:NB * D].rearrange("p (b d) -> p b d", b=NB)
        aqr = rot[:, 0:NB * 512].rearrange("p (b d) -> p b d", b=NB)
        akr = rot[:, 1024:1280].rearrange("p (b d) -> p b d", b=NB)
        t1 = rot[:, 1280:2560].rearrange("p (b d) -> p b d", b=NB)
        t2 = rot[:, 2560:3840].rearrange("p (b d) -> p b d", b=NB)
        qC = rot[:, 0:1536].rearrange("p (b d) -> p b d", b=NB)
        kC = rot[:, 1536:3072].rearrange("p (b d) -> p b d", b=NB)
        vC = rot[:, 3072:4096].rearrange("p (b d) -> p b d", b=NB)
        proj = arena[:, 0:NB * PROJ_W].rearrange("p (b n) -> p b n", b=NB)
        lamd = arena[:, NB * PROJ_W:NB * PROJ_W + P]
        rows = arena[:, 6144:6144 + 3 * P].rearrange("p (i c) -> p i c", i=3)
        cwr = arena[0:TAPS, 7168:7168 + DEPTH * CONV_W].rearrange("p (l c) -> p l c", l=DEPTH)
        merged = arena[:, 0:NB * D].rearrange("p (b d) -> p b d", b=NB)
        gated = arena[:, 2048:3072].rearrange("p (i d) -> p i d", i=2)
        gates = arena[:, 6144:12288].rearrange("p (b n) -> p b n", b=NB)
        hid = arena[:, 0:2048].rearrange("p (i f s) -> p i f s", i=2, f=4)
        aqT = qk[:, 0:1024].rearrange("p (k s) -> p k s", s=SEQ)
        akT = qk[:, 1024:1280]
        bqT = qk[:, 1280:2304].rearrange("p (k s) -> p k s", s=SEQ)
        bkT = qk[:, 2304:3328].rearrange("p (k s) -> p k s", s=SEQ)
        cqT = qk[0:C_QK, 0:2048].rearrange("p (k s) -> p k s", s=SEQ)
        ckT = qk[0:C_QK, 2048:4096].rearrange("p (k s) -> p k s", s=SEQ)
        cnT = yT[:, 8:13, :]

        ada_in = [qk[:, :].rearrange("p (k n) -> p k n", k=KD), arena[:, 8192:12288].rearrange("p (k n) -> p k n", k=KD)]
        ada_sum = arena[:, 2048:8192].rearrange("p (c n) -> p c n", c=ADA_CHUNKS)
        condc = small[:, 330:338]

        gateB = arena[:, 0:2048].rearrange("p (g d) -> p g d", g=2)
        band = arena[:, 2048:4096].rearrange("p (k g s) -> p k g s", k=NB, g=4)
        poolA = arena[:, 4096:4608].rearrange("p (b c) -> p b c", b=NB)
        diffT = arena[:, 4608:5120].rearrange("p (j s) -> p j s", j=2)
        glu = arena[:, 5120:5120 + KCONV * (SEQ + 2 * HALO)].rearrange("p (c s) -> p c s", c=KCONV)
        sg = arena[:, 6144:6912].rearrange("p (c s) -> p c s", c=KCONV)
        cacc = arena[:, 6912:7680].rearrange("p (c s) -> p c s", c=KCONV)
        csq = arena[:, 7680:8448].rearrange("p (c s) -> p c s", c=KCONV)
        crdiag = arena[:, 8704:8960]
        us = arena[:, 8960:9728].rearrange("p (b c) -> p b c", b=NB)
        vs = arena[:, 9728:10496].rearrange("p (b c) -> p b c", b=NB)
        swr = arena[:, 10496:11264].rearrange("p (h q) -> p h q", h=SGU_HEADS)
        swT = arena[:, 11264:12032].rearrange("p (h q) -> p h q", h=SGU_HEADS)
        gateD = [qk[:, 0:D], rot[:, 2560:2560 + D]]
        finB = qk[:, 1024:2048]
        sguG = qk[:, 2048:2432]
        sguB = qk[:, 2432:2816]
        outc = qk[:, 2816:3584].rearrange("p (b c) -> p b c", b=NB)
        pw = qk[:, 3584:3712].rearrange("p (j d) -> p j d", j=2)
        rw = qk[:, 3712:3776].rearrange("p (k e) -> p k e", k=KD)
        rb = qk[:, 3776:3784]
        io8 = qk[:, 3784:3792]
        ones = probs[:, 0, 0:P]
        mixT = yT[:, 0:8, :]
        cdiag = (o[:, :, :].rearrange("p b (t q) -> p (b t) q", q=P), diag[:, :, :, :].rearrange("p i j (t q) -> p (i j t) q", q=P),
                 pT[:, :, :].rearrange("p i (t q) -> p (i t) q", q=P), probs[:, 2:5, :].rearrange("p i (t q) -> p (i t) q", q=P),
                 yT[:, 8:13, :].rearrange("p k (t q) -> p (k t) q", q=P), rot[:, 3584:4096].rearrange("p (t q) -> p t q", q=P))
        assert sum(d.shape[1] for d in cdiag) == PE_TAPS
        mulc = probs[:, 1, 32:48]
        ffsg = probs[:, 2, :].rearrange("p (f s) -> p f s", f=FT)
        ffhid = pT[:, :, :].rearrange("p i (f s) -> p i f s", f=FT)
        yacc = arena[:, 4096:6144].rearrange("p (b d) -> p b d", b=NB)
        sel = arena[:, 6144:6656].rearrange("p (b c) -> p b c", b=NB)
        selw = arena[:, 6656:7168].rearrange("p (b c) -> p b c", b=NB)
        selT = arena[:, 7168:7680].rearrange("p (i s) -> p i s", i=2)
        ye = arena[:, 7680:7680 + 2 * D].rearrange("p (i d) -> p i d", i=2)
        hTe = hT
        yeT = hT
        tri = rot[:, 2048:2048 + P]
        slots = rot[:, 2176:2176 + SEQ]
        place = small[:, 240:240 + NB * (EXPERTS + 1)].rearrange("p (b e) -> p b e", b=NB)
        weight = small[:, 260:260 + NB * (EXPERTS + 1)].rearrange("p (b e) -> p b e", b=NB)
        chosen = small[:, 280:296].rearrange("p (b e) -> p b e", b=NB)
        curp, curw = small[:, 300:302], small[:, 302:304]
        emsg = probs[:, 2:4, :]
        ehid = pT[:, :, :]

        negmax = small[:, 344:344 + 2 * NPROBS].rearrange("p (i b) -> p i b", b=NB)
        recips = small[:, 384:384 + 2 * NPROBS].rearrange("p (i b) -> p i b", b=NB)
        sums = small[:, 364:364 + 2 * NPROBS].rearrange("p (i b) -> p i b", b=NB)

        G = [ctx.enter_context(nc.psum_tensor(f"G{i}", [P, 512], F32)) for i in range(4)]
        T = [ctx.enter_context(nc.psum_tensor(f"T{i}", [P, 512], F32)) for i in range(2)]
        S = [ctx.enter_context(nc.psum_tensor(f"S{i}", [P, 512], F32)) for i in range(2)]
        H4 = [S[0], S[1], T[0], T[1]]
        SB = [S[0], S[1], G[2], G[3]]

        loaded = [sig(f"loaded{i}", 16 * L1_CHUNKS // NSLOT) for i in range(NSLOT)]
        used = [sig(f"used{i}", L1_CHUNKS // NSLOT) for i in range(NSLOT)]
        x_in = sig("x_in")
        consts_in = sig("consts_in")
        rows_in = sig("rows_in")
        mix_in = sig("mix_in")
        ident_ok = sig("ident_ok")
        half_ok = sig("half_ok")
        rows_turned = sig("rows_turned")
        cols_ok = sig("cols_ok")
        cur_ok = sig("cur_ok", 1)
        dve_step = sig("dve_step")
        pool_step = sig("pool_step")
        x_new = sig("x_new", 4)
        ss_ok = sig("ss_ok", 2)
        rstd_ok = sig("rstd_ok", 1)
        xn_ok = sig("xn_ok", 2)
        xn_turned = sig("xn_turned", 4)
        hT_act = sig("hT_act", 2)
        hT_dve = sig("hT_dve", 2)
        proj_mm = sig("proj_mm", 8)
        proj_act = sig("proj_act", 8)
        proj_dve = sig("proj_dve", 8)
        gate_mm = sig("gate_mm", 8)
        gate_ev = sig("gate_ev", 16)
        asq_ok = sig("asq_ok", 1)
        ars_ok = sig("ars_ok", 1)
        csq_ok = sig("csq_ok", 4)
        crs_ok = sig("crs_ok", 1)
        lam_in = sig("lam_in", 1)
        lam_exp = sig("lam_exp", 1)
        cn_ok = sig("cn_ok", 1)
        rope_ok = sig("rope_ok", 1)
        cn_turned = sig("cn_turned", 3)
        cn_ev = sig("cn_ev", 3)
        up_mm = sig("up_mm", 6)
        up_ev = sig("up_ev", 8)
        qk_turned = sig("qk_turned", 15)
        qk_act = sig("qk_act", 8)
        qk_dve = sig("qk_dve", 7)
        ropeC_ok = sig("ropeC_ok", 1)
        sc_mm = sig("sc_mm", 32)
        negmax_ok = sig("negmax_ok", 32)
        exp_ok = sig("exp_ok", 32)
        diag_ok = sig("diag_ok", 24)
        p_turned = sig("p_turned", 24)
        pT_ok = sig("pT_ok", 24)
        pv_mm = sig("pv_mm", 24)
        o_ev = sig("o_ev", 16)
        subsq_ok = sig("subsq_ok", 1)
        subrs_ok = sig("subrs_ok", 1)
        o_ok = sig("o_ok", 1)
        o_turned = sig("o_turned", 2)
        y_act = sig("y_act", 1)
        y_dve = sig("y_dve", 1)
        br_mm = sig("br_mm", 9)
        br_ev = sig("br_ev", 12)
        mg_turned = sig("mg_turned", 4)
        mg_act = sig("mg_act", 2)
        mg_dve = sig("mg_dve", 2)
        ff_mm = sig("ff_mm", 24)
        ff_ev = sig("ff_ev", 32)
        ff2_mm = sig("ff2_mm", 1)
        blk1_done = sig("blk1_done")
        cond_ok = sig("cond_ok")
        ada_loaded = [sig(f"ada_loaded{i}", 16 * ADA_CHUNKS // 2) for i in range(2)]
        ada_step = sig("ada_step", ADA_CHUNKS * KD)
        ada_mm = sig("ada_mm", 1)
        adac_ok = sig("adac_ok", 1)
        gateB_mm = sig("gateB_mm", 4)
        mods_ok = sig("mods_ok", 2)
        w2_mm = sig("w2_mm", 7)
        pool_ev = sig("pool_ev", 1)
        conv_sg = sig("conv_sg", 3)
        glu_ok = sig("glu_ok", 3)
        uv_ev = sig("uv_ev", 4)
        diff_mm = sig("diff_mm", 2)
        diff_ev = sig("diff_ev", 2)
        poolo_mm = sig("poolo_mm", 2)
        poolo_ev = sig("poolo_ev", 2)
        cacc_ok = sig("cacc_ok", 1)
        cmean_mm = sig("cmean_mm", 1)
        cdev_ok = sig("cdev_ok", 1)
        cvar_mm = sig("cvar_mm", 1)
        cdiag_ok = sig("cdiag_ok", 1)
        ctaps_mm = sig("ctaps_mm", 2)
        crdiag_ok = sig("crdiag_ok", 1)
        crb_mm = sig("crb_mm", 1)
        cln_ok = sig("cln_ok", 3)
        csig_ok = sig("csig_ok", 3)
        conv_ok = sig("conv_ok", 3)
        sw_turned = sig("sw_turned", 2)
        sw_ev = sig("sw_ev", 2)
        var_ok = sig("var_ok", 2)
        varroot_ok = sig("varroot_ok", 2)
        vn_ok = sig("vn_ok", 1)
        sgu_mm = sig("sgu_mm", 2)
        outc_ok = sig("outc_ok", 1)
        outc_turned = sig("outc_turned", 2)
        outc_ev = sig("outc_ev", 2)
        sub_in = [[sig(f"sub_in{i}{n}") for n in "gud"] for i in range(2)]
        sub_used = [[sig(f"sub_used{i}{n}") for n in "gud"] for i in range(2)]
        fg_mm = sig("fg_mm")
        fu_mm = sig("fu_mm")
        fsg_ok = sig("fsg_ok")
        fhid_ok = sig("fhid_ok")
        chosen_ok = sig("chosen_ok")
        rank_mm = sig("rank_mm")
        counts_ok = sig("counts_ok")
        cur_loaded = sig("cur_loaded")
        sel_ok = sig("sel_ok")
        selw_ok = sig("selw_ok")
        gath_mm = sig("gath_mm")
        hTe_act = sig("hTe_act")
        hTe_dve = sig("hTe_dve")
        esg_ok = sig("esg_ok")
        et_ok = sig("et_ok")
        ehid_ok = sig("ehid_ok")
        eh_turned = sig("eh_turned")
        eh_ok = sig("eh_ok")
        edn_done = sig("edn_done")
        selT_mm = sig("selT_mm")
        selT_ok = sig("selT_ok")
        yeT_act = sig("yeT_act")
        yeT_dve = sig("yeT_dve")
        ye_mm = sig("ye_mm")
        ye_act = sig("ye_act")
        ye_dve = sig("ye_dve")
        scat_mm = sig("scat_mm")
        scat_ev = sig("scat_ev")
        rt_mm = sig("rt_mm")
        rt_max = sig("rt_max")
        rt_exp = sig("rt_exp")
        stored = sig("stored")
        out_ok = sig("out_ok")
        merged_ok = sig("merged_ok", 1)
        ff_relu = sig("ff_relu", 32)
        ft_ok = sig("ft_ok")
        fdn_done = sig("fdn_done")
        adaG_ev = sig("adaG_ev", 1)

        block = ctx.enter_context(nc.Block())

        def slot(pos):
            return ring[:, (pos % NSLOT) * SLOT:(pos % NSLOT + 1) * SLOT]

        def sub(i, piece):
            at = (i * 3 + piece) * SUB
            return ring[:, at:at + SUB]

        U_FIN1, U_MIX, U_FFN, U_FIN2 = 4, 5, 6, 9

        def used_at(l, pos):
            return l * (L1_CHUNKS // NSLOT) + pos // NSLOT + 2

        def used2_at(l, pos):
            return DEPTH * L1_CHUNKS // NSLOT + l * L2_CHUNKS // NSLOT + pos // NSLOT + 2
        X1 = DEPTH * 4 * 2

        def each_expert(eng, body):
            with eng.Fori(0, EXPERTS) as e:
                n = eng.value_load(counts[0:1, bass.ds(e, 1)], min_val=0, max_val=SEQ)
                for lo, w in zip((-1, *WIDTHS), WIDTHS):
                    with eng.If(n > lo):
                        with eng.If(n <= w):
                            body(e, w)

        FEW = P // 2

        def few(w):
            return w == FEW

        def blocks(w):
            return [(i, i * P, min(P, w - i * P)) for i in range(-(-w // P))]

        def result_at(u):
            br, i, _ = UNITS[u]
            return (i // 2, i % 2 == 1) if br == 0 else (4 + i, True) if br == 1 else (12 + i // 2, i % 2 == 1)

        def tile_at(k, w):
            per = min(4, 512 // w)
            return k // per, k % per * w

        def tile_banks(w):
            per = min(4, 512 // w)
            return [(k // per, k, min(k + per, KD)) for k in range(0, KD, per)]

        def ye_bank(j, half):
            return H4[(2 + half, 1 - half)[j]]

        @block.sync
        def _(sp):
            sp.dma_start(x[:], t["x"][0].rearrange("(b p) d -> p b d", p=P)).then_inc(x_in.sem, 16)

            def load(l, pos, dst, src, per=L1_CHUNKS, first=0):
                i = pos % NSLOT
                sp.wait_ge(used[i].sem, first + l * (per // NSLOT) + pos // NSLOT + 1)
                sp.dma_start(dst, src).then_inc(loaded[i].sem, 16)

            with sp.Fori(0, DEPTH) as l:
                w_in = t["w_in"][l].rearrange("(k p) n -> p k n", p=P)
                for part, n, c0 in ((0, PROJ_N, 0), (1, GATE_N, PROJ_W)):
                    with sp.Fori(0, 2) as it:
                        for c in range(NSLOT):
                            i = c
                            sp.wait_ge(used[i].sem, l * (L1_CHUNKS // NSLOT) + (2 * part) + it + 1)
                            sp.dma_start(slot(c)[:, 0:KD * n].rearrange("p (k n) -> p k n", k=KD),
                                         w_in[:, :, bass.ds(it * (NSLOT * n) + c0 + c * n, n)]).then_inc(loaded[i].sem, 16)
                load(l, 16, slot(16)[:, 0:KCQ * 768].rearrange("p (k n) -> p k n", k=KCQ),
                     t["c_w_uq"][l].rearrange("(k p) n -> p k n", p=P))
                load(l, 17, slot(17)[:, 0:KCKV * 1024].rearrange("p (k n) -> p k n", k=KCKV),
                     t["c_w_ukv"][l].rearrange("(k p) n -> p k n", p=P))
                for n in range(3):
                    load(l, 18 + n, slot(18 + n).rearrange("p (k n) -> p k n", k=4),
                         t["w_branch"][l, BR_ORDER[n]].rearrange("(k p) n -> p k n", p=P))
                for n, (k0, k1) in enumerate(((0, 3), (3, 6), (6, 8))):
                    load(l, 21 + n, slot(21 + n)[:, 0:(k1 - k0) * D].rearrange("p (k n) -> p k n", n=D),
                         t["w_out"][l].rearrange("(k p) n -> p k n", p=P)[:, k0:k1, :])
                f1 = t["w_ff1"][l].rearrange("(k p) n -> p k n", p=P)
                f2 = t["w_ff2"][l].rearrange("(k p) n -> p k n", p=P)
                with sp.Fori(0, 4) as it:
                    for c in range(NSLOT):
                        sp.wait_ge(used[c].sem, l * (L1_CHUNKS // NSLOT) + it + 6 + 1)
                        if c % 2 == 0:
                            sp.dma_start(slot(c).rearrange("p (k n) -> p k n", k=KD),
                                         f1[:, :, bass.ds(it * 1024 + (c // 2) * 512, 512)]).then_inc(loaded[c].sem, 16)
                        else:
                            sp.dma_start(slot(c).rearrange("p (k n) -> p k n", k=4),
                                         f2[:, bass.ds(it * 8 + (c // 2) * 4, 4), :]).then_inc(loaded[c].sem, 16)
            base = DEPTH * L1_CHUNKS // NSLOT
            subn = [0, 0]

            def load_sub(i, g, u, d, wait):
                for piece, src in enumerate((g, u, d)):
                    sp.wait_ge(sub_used[i][piece].sem, wait)
                    dst = sub(i, piece).rearrange("p (k n) -> p k n", n=src.shape[2])
                    sp.dma_start(dst, src).then_inc(sub_in[i][piece].sem, 16)

            for l in range(DEPTH):
                b2 = base + l * L2_CHUNKS // NSLOT
                if l > 0:
                    for i in range(2):
                        for piece in range(3):
                            sp.wait_ge(sub_used[i][piece].sem, 1 + subn[i])
                w2 = t["w_in_2"][l].rearrange("(k p) n -> p k n", p=P)
                at = 0
                for c, n in enumerate((POOL_W, CONV_W, CONV_W, SGU_W, SGU_W)):
                    load(0, c, slot(c)[:, 0:KD * n].rearrange("p (k n) -> p k n", k=KD),
                         w2[:, :, at:at + n], first=b2)
                    at += n
                for n, (k0, k1) in enumerate(((0, 3), (3, 6), (6, 8))):
                    load(0, 5 + n, slot(5 + n)[:, 0:(k1 - k0) * D].rearrange("p (k n) -> p k n", n=D),
                         t["w_out_2"][l].rearrange("(k p) n -> p k n", p=P)[:, k0:k1, :], first=b2)
                for i in range(NSLOT):
                    sp.wait_ge(used[i].sem, b2 + L2_CHUNKS // NSLOT + 1)
                if l == 0:
                    g = t["ffn_w_gate_2"][0].rearrange("(k p) n -> p k n", p=P)
                    u = t["ffn_w_up_2"][0].rearrange("(k p) n -> p k n", p=P)
                    d = t["ffn_w_down_2"][0].rearrange("(k p) n -> p k n", p=P)
                    with sp.Fori(0, 5) as it:
                        for i in range(2):
                            n0 = it * (2 * FT * P) + i * FT * P
                            load_sub(i, g[:, :, bass.ds(n0, FT * P)], u[:, :, bass.ds(n0, FT * P)],
                                     d[:, bass.ds(it * (2 * FT) + i * FT, FT), :], it + 1)
                    load_sub(0, g[:, :, 10 * FT * P:], u[:, :, 10 * FT * P:], d[:, 10 * FT:, :], 6)
                    subn = [6, 5]
                else:
                    with sp.Fori(0, EXPERTS) as e:
                        g = t["moe_w_gate_2"][0, e].rearrange("(k p) n -> p k n", p=P)
                        u = t["moe_w_up_2"][0, e].rearrange("(k p) n -> p k n", p=P)
                        d = t["moe_w_down_2"][0, e].rearrange("(k p) n -> p k n", p=P)
                        with sp.Fori(0, 7) as it:
                            for i in range(2):
                                n0 = it * (2 * FT * P) + i * FT * P
                                load_sub(i, g[:, :, bass.ds(n0, FT * P)], u[:, :, bass.ds(n0, FT * P)],
                                         d[:, bass.ds(it * (2 * FT) + i * FT, FT), :],
                                         e * 7 + it + subn[i] + 1)
            sp.wait_ge(out_ok.sem, NB)
            sp.dma_start(t["out"][0].rearrange("(b p) d -> p b d", p=P), x[:]).then_inc(stored.sem, 16)
            sp.wait_ge(stored.sem, 16)

        @block.gpsimd
        def _(pool):
            step = Steps(pool, pool_step.sem)
            pool.memset(ident[:], 0.0).then_inc(ident_ok.sem, 1)
            pool.memset(mhalf[:], -0.5)
            pool.memset(epsc[:], EPS)
            for n, tile in inverse.items():
                last = pool.memset(tile[:], 1.0 / n)
            last.then_inc(half_ok.sem, 1)
            pool.memset(onec[:], 1.0)
            pool.memset(zcol[:], 0.0)
            for i in range(2):
                for piece in range(3):
                    pool.sem_inc(sub_used[i][piece].sem, 1)
            for i in range(NSLOT):
                pool.sem_inc(used[i].sem, 1)
            n = 0
            for l in range(DEPTH):
                at = l * ROW_L1
                for name, r in (("ln1_g", KD), ("ln2_g", KD), ("c_q_norm", KCQ), ("c_kv_norm", KCKV)):
                    pool.dma_start(rows[at:at + r, 0, :], t[name][l].rearrange("(r p) -> r p", p=P)).then_inc(rows_in.sem, 16)
                    at += r
                    n += 1
            pool.dma_start(rows[R_C:R_C + KD, 0, :], t["c_2"][0].rearrange("(r p) -> r p", p=P)).then_inc(rows_in.sem, 16)
            pool.dma_start(rows[0:DEPTH * MODS * KD, 1, :], t["ada_b_2"].rearrange("l (r p) -> (l r) p", p=P)).then_inc(rows_in.sem, 16)
            for at, name in ((R2_MIXG, "mix_norm_g_2"), (R2_FFNG, "ffn_norm_g_2"), (R2_PS, "pool_scale_2"),
                             (R2_CB, "conv_b_2"), (R2_CG, "conv_ln_g_2"), (R2_CLB, "conv_ln_b_2")):
                v = t[name].rearrange("l (r p) -> (l r) p", p=P)
                pool.dma_start(rows[at:at + v.shape[0], 2, :], v).then_inc(rows_in.sem, 16)
            pool.dma_start(rows[R2_SB:R2_SB + DEPTH * SGU_HEADS, 2, :], t["sgu_b_2"].rearrange("l h p -> (l h) p")).then_inc(rows_in.sem, 16)
            pool.dma_start(cwr, t["conv_w_2"].rearrange("l t c -> t l c")).then_inc(rows_in.sem, 16)
            pool.wait_ge(ident_ok.sem, 1)
            pool.affine_select(out=ident[:], in_=ident[:], compare_op=ALU.not_equal, fill=1.0, base=0,
                               pattern=[[-1, P]], channel_multiplier=1).then_inc(ident_ok.sem, 1)
            pool.wait_ge(half_ok.sem, 1)

            def inv_root(v, out, count, done):
                n = v.shape[1]
                step.do(pool.tensor_tensor(v, v, inverse[count][:, 0:n], ALU.mult))
                step.do(pool.tensor_tensor(v, v, epsc[:, 0:n], ALU.add))
                pool.tensor_tensor(out, v, mhalf[:, 0:n], ALU.pow).then_inc(done.sem, 1)

            def norm_root(u):
                pool.wait_ge(ss_ok.sem, ss_ok.at(u, 2))
                inv_root(small[:, 0:2], small[:, 2:4], D, rstd_ok)

            pool.wait_ge(cols_ok.sem, 1)
            pool.wait_ge(consts_in.sem, 16 * N_CONST)
            with pool.Fori(0, DEPTH) as l:
                step.base, step.n = l * POOL_STEPS, 0
                step.do(pool.tensor_copy(cur[:], cols[:, 0, bass.ds(l * ROW_L1, ROW_L1)]))
                pool.tensor_copy(curb[:], bc[:, bass.ds(l, 1), :].rearrange("p a n -> p (a n)")).then_inc(cur_ok.sem, 1)
                norm_root(l * 2)
                pool.wait_ge(asq_ok.sem, asq_ok.at(l, 1))
                inv_root(small[:, 8:28], small[:, 32:52], A_DIM, ars_ok)
                pool.wait_ge(csq_ok.sem, csq_ok.at(l, 4))
                step.did(pool.tensor_tensor(small[:, 56:58], small[:, 56:58], inverse[CQ_RANK][:, 0:2], ALU.mult))
                step.do(pool.tensor_tensor(small[:, 58:60], small[:, 58:60], inverse[CKV_RANK][:, 0:2], ALU.mult))
                step.do(pool.tensor_tensor(small[:, 56:60], small[:, 56:60], epsc[:, 0:4], ALU.add))
                pool.tensor_tensor(small[:, 60:64], small[:, 56:60], mhalf[:, 0:4], ALU.pow).then_inc(crs_ok.sem, 1)
                pool.wait_ge(subsq_ok.sem, subsq_ok.at(l, 1))
                inv_root(small[:, 64:80], small[:, 80:96], 2 * B_DIM, subrs_ok)
                norm_root(l * 2 + 1)
                ada = t["ada_w_2"][l].rearrange("(k p) n -> p k n", p=P)
                for c in range(ADA_CHUNKS):
                    if c >= 2:
                        pool.wait_ge(ada_step.sem, ada_step.at(l, (c - 1) * KD))
                    pool.dma_start(ada_in[c % 2], ada[:, :, c * 512:(c + 1) * 512]).then_inc(ada_loaded[c % 2].sem, 16)
                pool.wait_ge(x_new.sem, l * 8 + 8 + 1)
            assert step.n == POOL_STEPS, step.n
            step.base, step.n = DEPTH * POOL_STEPS, 0
            norm_root(U_FIN1)
            pool.wait_ge(blk1_done.sem, 1)
            pool.dma_start(finB, t["final_norm_g_2"].partition_broadcast(P)).then_inc(mix_in.sem, 16)
            pool.dma_start(rw, t["router_w_2"][0].rearrange("(k p) e -> p k e", p=P)).then_inc(mix_in.sem, 16)
            pool.dma_start(rb, t["router_b_2"][0].partition_broadcast(P)).then_inc(mix_in.sem, 16)
            pool.dma_start(tri, t["before"]).then_inc(mix_in.sem, 16)
            pool.dma_start(slots, t["slots"].partition_broadcast(P)).then_inc(mix_in.sem, 16)
            pool.dma_start(io8, t["iota8"].partition_broadcast(P)).then_inc(mix_in.sem, 16)
            pool.dma_start(band.rearrange("p k g s -> p k (g s)"), t["band"].rearrange("(k p) g s -> p k (g s)", p=P)).then_inc(mix_in.sem, 16)
            pool.memset(ones, 1.0).then_inc(half_ok.sem, 1)
            for c in range(KCONV):
                pool.memset(glu[:, c, 0:HALO], 0.0)
                pool.memset(glu[:, c, HALO + SEQ:], 0.0).then_inc(half_ok.sem, 1)
            for l in range(DEPTH):
                if l:
                    pool.wait_ge(x_new.sem, X1 + 1 + 8)
                q = mix_in.sem
                pool.dma_start(sguG, t["sgu_ln_g_2"][l].partition_broadcast(P)).then_inc(q, 16)
                pool.dma_start(sguB, t["sgu_ln_b_2"][l].partition_broadcast(P)).then_inc(q, 16)
                pool.dma_start(swr, t["sgu_w_2"][l].rearrange("h p q -> p h q")).then_inc(q, 16)
                pw_v = t["pool_w_2"][l].rearrange("(j i) c d -> i c j d", i=2)
                for i in range(2):
                    pool.dma_start(pw[64 * i:64 * i + 64], pw_v[i]).then_inc(q, 16)
                norm_root(U_MIX + 2 * l)
                at = 0
                for d in cdiag:
                    n = d.shape[1]
                    w = cwc[:, l].rearrange("p c t -> p (c t)")[:, at:at + n].unsqueeze(2)
                    ins = pool.tensor_tensor(d, ident[:].unsqueeze(1).broadcast_to([P, n, P]), w.broadcast_to([P, n, P]), ALU.mult)
                    at += n
                ins.then_inc(cdiag_ok.sem, 1)
                pool.wait_ge(var_ok.sem, var_ok.at(l, 1))
                pool.tensor_tensor(small[:, 100:102], small[:, 98:100], mhalf[:, 0:2], ALU.pow).then_inc(varroot_ok.sem, 1)
                pool.wait_ge(var_ok.sem, var_ok.at(l, 2))
                pool.tensor_tensor(small[:, 402:404], small[:, 400:402], mhalf[:, 0:2], ALU.pow).then_inc(varroot_ok.sem, 1)
                norm_root(U_FFN + 2 * l)
            norm_root(U_FIN2)

        @block.scalar
        def _(act):
            q = consts_in.sem
            act.dma_start(ropeA[:], t["rope_a"].rearrange("(b p) c d -> p b c d", p=P)).then_inc(q, 16)
            act.dma_start(ropeB[:], t["rope_b"].rearrange("(b p) c d -> p b c d", p=P)).then_inc(q, 16)
            act.dma_start(ropeC[:], t["rope_c"].rearrange("(b p) c d -> p b c d", p=P)).then_inc(q, 16)
            for l in range(DEPTH):
                for at, name in ((B_AQ, "a_q_norm"), (B_AK, "a_k_norm"), (B_SUB, "b_subln")):
                    act.dma_start(bc[:, l, at:at + 64], t[name][l].partition_broadcast(P)).then_inc(q, 16)
                act.dma_start(bc[:, l, B_LAM:B_LAM + 128], t["b_lambda"][l].rearrange("a d -> (a d)").partition_broadcast(P)).then_inc(q, 16)
                act.dma_start(bc[:, l, B_INIT:B_INIT + 2], t["lam_init"][l].partition_broadcast(P)).then_inc(q, 16)
            act.wait_ge(x_in.sem, 16)
            act.sem_inc(proj_act.sem, 2)
            act.sem_inc(gate_ev.sem, 4)
            act.sem_inc(ff_relu.sem, 4)

            def norm_squares(u):
                for b in range(NB):
                    act.activation(xn[:, b, :], x[:, b, :], ACT.Square, accum_out=small[:, b:b + 1]).then_inc(ss_ok.sem, 1)

            def turned_evac(u, turned, done, mul, add=None):
                for i in (0, 2):
                    act.wait_ge(turned.sem, turned.at(u, i + 1))
                    for kk in range(2):
                        k = 2 * i + kk
                        src = T[0][:, kk * SEQ:(kk + 1) * SEQ]
                        if mul is None:
                            ins = act.activation(hT[:, k, :], src, ACT.Copy)
                        elif add is None:
                            ins = act.activation(hT[:, k, :], src, ACT.Copy, scale=mul[:, k:k + 1])
                        else:
                            ins = act.activation(hT[:, k, :], src, ACT.Identity, scale=mul[:, k:k + 1], bias=add[:, k:k + 1])
                    ins.then_inc(done.sem, 1)

            act.wait_ge(rows_turned.sem, 1)
            for i, n in enumerate((R_C + KD, DEPTH * MODS * KD, R2_N)):
                ins = act.activation(cols[:, i, 0:n], T[0][:, i * P:i * P + n], ACT.Copy)
            ins.then_inc(cols_ok.sem, 1)
            act.wait_ge(rows_turned.sem, 2)
            for l in range(DEPTH):
                ins = act.activation(cwc[:, l], T[1][:, l * 128:l * 128 + KCONV * TAPS].rearrange("p (c t) -> p c t", c=KCONV), ACT.Copy)
            ins.then_inc(cols_ok.sem, 1)

            act.wait_ge(cols_ok.sem, 1)
            act.activation(condc, cols[:, 0, R_C:R_C + KD], ACT.Sigmoid).then_inc(cond_ok.sem, 1)
            with act.Fori(0, DEPTH) as l:
                act.wait_ge(x_new.sem, l * 8 + 1)
                norm_squares(l * 2)
                act.wait_ge(cur_ok.sem, cur_ok.at(l, 1))
                turned_evac(l * 2, xn_turned, hT_act, cur[:, 0:KD])
                with act.Fori(0, 2) as it:
                    for c in range(NSLOT):
                        act.wait_ge(proj_mm.sem, l * 8 + it * 4 + (c + 1))
                        act.activation(proj[:, 0, bass.ds(it * (NSLOT * PROJ_N) + c * PROJ_N, PROJ_N)],
                                       G[2 * (c % 2)][:, 0:PROJ_N], ACT.Copy).then_inc(proj_act.sem, 1)
                act.wait_ge(proj_act.sem, proj_act.at(l, 8) + 2)
                act.wait_ge(proj_dve.sem, proj_dve.at(l, 8) + 2)
                for i, (c0, w) in enumerate(((O_CQ, CQ_RANK), (O_CKV, CKV_RANK))):
                    for b in range(NB):
                        act.activation(probs[:, 2 * i + b, 0:w], proj[:, b, c0:c0 + w], ACT.Square,
                                       accum_out=small[:, 56 + 2 * i + b:57 + 2 * i + b]).then_inc(csq_ok.sem, 1)
                act.wait_ge(lam_in.sem, lam_in.at(l, 1))
                act.activation(small[:, 104:106], small[:, 102:104], ACT.Exp).then_inc(lam_exp.sem, 1)
                with act.Fori(0, 2) as it:
                    for c in range(NSLOT):
                        for b in range(NB):
                            if b == 0:
                                act.wait_ge(gate_mm.sem, l * 8 + it * 4 + (c + 1))
                            else:
                                act.wait_ge(used[c].sem, used_at(l, 8) + it)
                            act.activation(gates[:, b, bass.ds(it * (NSLOT * GATE_N) + c * GATE_N, GATE_N)],
                                           G[2 * (c % 2) + b][:, 0:GATE_N], ACT.Sigmoid).then_inc(gate_ev.sem, 1)
                for i in range(3):
                    act.wait_ge(cn_turned.sem, cn_turned.at(l, i + 1))
                    for kk in range(2 if i < 2 else 1):
                        k = 2 * i + kk
                        ins = act.activation(cnT[:, k, :], T[i % 2][:, kk * SEQ:(kk + 1) * SEQ], ACT.Copy,
                                             scale=cur[:, 2 * KD + k:2 * KD + k + 1])
                    ins.then_inc(cn_ev.sem, 1)
                for i in range(0, 7, 2):
                    act.wait_ge(qk_turned.sem, qk_turned.at(l, i + 1))
                    dst = (qk[:, 0:512], None, akT, None, qk[:, 1280 + 512:1280 + 1024], None, qk[:, 2304 + 512:2304 + 1024])[i]
                    act.activation(dst, T[0][:, 0:dst.shape[1]], ACT.Copy,
                                   scale={0: A_DIM ** -0.5, 4: B_DIM ** -0.5}.get(i, 1.0)).then_inc(qk_act.sem, 1)

                def exps(u):
                    for s in UNITS[u][2]:
                        act.wait_ge(negmax_ok.sem, negmax_ok.at(l, s + 1))
                        if s >= NPROBS:
                            past = next(v for v in range(len(UNITS)) if s - NPROBS in UNITS[v][2])
                            act.wait_ge(p_turned.sem, p_turned.at(l, past + 1))
                        for b in range(NB):
                            ins = act.activation(probs[:, s % NPROBS, b * SEQ:(b + 1) * SEQ], SB[s % 4][:, b * SEQ:(b + 1) * SEQ], ACT.Exp,
                                                 bias=negmax[:, s % NPROBS, b:b + 1], accum_out=sums[:, s % NPROBS, b:b + 1])
                        ins.then_inc(exp_ok.sem, 1)

                def attend(u0, u1):
                    exps(u0)
                    for u in range(u0, u1):
                        if u + 1 < u1:
                            exps(u + 1)
                        act.wait_ge(p_turned.sem, p_turned.at(l, u + 1))
                        act.activation(pT[:, u % 2, :], T[u % 2][:, :], ACT.Copy).then_inc(pT_ok.sem, 1)

                attend(0, 16)
                for i in range(0, 8, 2):
                    act.wait_ge(qk_turned.sem, qk_turned.at(l, 7 + i + 1))
                    dst = (cqT if i < 4 else ckT)[:, 2 * (i % 4):2 * (i % 4) + 2, :]
                    act.activation(dst, T[(7 + i) % 2][0:C_QK, :].rearrange("p (k s) -> p k s", k=2), ACT.Copy,
                                   scale=C_QK ** -0.5 if i < 4 else 1.0).then_inc(qk_act.sem, 1)
                attend(16, 24)
                act.wait_ge(o_turned.sem, o_turned.at(l, 1))
                act.activation(yT[:, 4:6, :], T[0][:, :].rearrange("p (k s) -> p k s", k=2), ACT.Copy).then_inc(y_act.sem, 1)
                turned_evac(l, mg_turned, mg_act, None)
                act.wait_ge(x_new.sem, l * 8 + 4 + 1)
                norm_squares(l * 2 + 1)
                turned_evac(l * 2 + 1, xn_turned, hT_act, cur[:, KD:2 * KD])
                with act.Fori(0, 4) as it:
                    for j in range(2):
                        for f in range(4):
                            if f < 3:
                                act.wait_ge(ff_mm.sem, l * 24 + it * 6 + (3 * j + f + 1))
                            else:
                                act.wait_ge(used[2 * j].sem, used_at(l, 24) + it)
                            act.activation(hid[:, j, f, :], H4[f][:, 0:SEQ], ACT.Relu).then_inc(ff_relu.sem, 1)
            act.wait_ge(x_new.sem, X1 + 1)
            act.dma_start(arena[:, 0:D], t["final_g"].partition_broadcast(P)).then_inc(consts_in.sem, 16)
            norm_squares(U_FIN1)
            act.wait_ge(blk1_done.sem, 1)
            for l in range(DEPTH):
                u = U_MIX + 2 * l
                if l:
                    act.wait_ge(x_new.sem, X1 + 1 + 8 * l)
                norm_squares(u)
                act.wait_ge(mods_ok.sem, mods_ok.at(l, 1))
                turned_evac(u - 1, xn_turned, hT_act, mulc[:, 0:KD], mods[:, l, 0:KD])
                for c in range(KCONV):
                    if c < 2:
                        act.wait_ge(w2_mm.sem, w2_mm.at(l, 4 + c))
                    else:
                        act.wait_ge(used[2].sem, used2_at(l, 2))
                    act.activation(sg[:, c, :], H4[1 + c][:, 0:SEQ], ACT.Sigmoid).then_inc(conv_sg.sem, 1)
                for i, dst in enumerate((us, vs)):
                    for b in range(NB):
                        if b == 0:
                            act.wait_ge(w2_mm.sem, w2_mm.at(l, 6 + i))
                        else:
                            act.wait_ge(used[(3 + i) % NSLOT].sem, used2_at(l, 3 + i))
                        act.activation(dst[:, b, :], G[2 * i + b][:, 0:SGU_W], ACT.Copy).then_inc(uv_ev.sem, 1)
                for i in range(2):
                    act.wait_ge(outc_turned.sem, outc_turned.at(l, i + 1))
                    k = 2 - i
                    act.activation(mixT[:, 5 + 2 * i:5 + 2 * i + k, :], G[2 + i][:, 0:k * SEQ].rearrange("p (k s) -> p k s", k=k),
                                   ACT.Copy).then_inc(outc_ev.sem, 1)
                for c in range(4):
                    act.wait_ge(gateB_mm.sem, gateB_mm.at(l, c + 1))
                    ins = act.activation(gateB[:, c // 2, (c % 2) * 512:(c % 2 + 1) * 512], G[c][:, :], ACT.Copy)
                ins.then_inc(adaG_ev.sem, 1)
                for c in range(KCONV):
                    act.wait_ge(cln_ok.sem, cln_ok.at(l, c + 1))
                    act.activation(sg[:, c, :], cacc[:, c, :], ACT.Sigmoid).then_inc(csig_ok.sem, 1)
                act.wait_ge(x_new.sem, X1 + 1 + 8 * l + 4)
                norm_squares(u + 1)
                turned_evac(u, xn_turned, hT_act, mulc[:, KD:2 * KD], mods[:, l, 3 * KD:4 * KD])

                def silu_gate(n, i, count):
                    for f in range(FT):
                        act.wait_ge(fhid_ok.sem, n * FT + (f + 1))
                        if f == 0:
                            act.wait_ge(fg_mm.sem, n + 1)
                        else:
                            act.wait_ge(sub_used[i][0].sem, count)
                        act.activation(ffsg[:, f, :], H4[2 * f][:, 0:SEQ], ACT.Sigmoid).then_inc(fsg_ok.sem, 1)

                if l == 0:
                    with act.Fori(0, 5) as it:
                        for i in range(2):
                            silu_gate(it * 2 + i, i, it + 2)
                    silu_gate(10, 0, 7)
                else:
                    act.wait_ge(rt_max.sem, 1)
                    act.activation(small[:, 200:202], small[:, 196:198], ACT.Exp).then_inc(rt_exp.sem, 1)

                    def inputs(e, w):
                        act.wait_ge(gath_mm.sem, e + 1)
                        for k in range(KD):
                            bank, c0 = tile_at(k, w)
                            if bank % 2 == 0:
                                ins = act.activation(hTe[:, k, 0:w], H4[bank][:, c0:c0 + w], ACT.Identity, scale=mulc[:, KD + k:KD + k + 1], bias=mods[:, l, 3 * KD + k:3 * KD + k + 1])
                        ins.then_inc(hTe_act.sem, 1)

                    def sigmoids(e, it, i, n):
                        act.wait_ge(ehid_ok.sem, e * ESTEPS + it * 2 + (i + 1))
                        act.wait_ge(sub_used[i][0].sem, e * (ESTEPS // 2) + it + (8 - i))
                        act.activation(emsg[:, i, 0:n], H4[2 * i][:, 0:n], ACT.Sigmoid).then_inc(esg_ok.sem, 1)

                    def hidden_turned(e, it, i):
                        act.wait_ge(eh_turned.sem, e * ESTEPS + it * 2 + (i + 1))
                        act.activation(ehid[:, i, 0:P], G[2 + i][:, 0:P], ACT.Copy).then_inc(eh_ok.sem, 1)

                    def by_slot(e, w):
                        act.wait_ge(selT_mm.sem, e + 1)
                        for i, s0, n in blocks(max(w, P)):
                            ins = act.activation(selT[0:n, i, :], H4[0][0:n, i * SEQ:(i + 1) * SEQ], ACT.Copy)
                        ins.then_inc(selT_ok.sem, 1)

                    def expert_few(e):
                        inputs(e, P)
                        last = ESTEPS // 2 - 1
                        sigmoids(e, 0, 0, P)
                        with act.Fori(0, last) as it:
                            sigmoids(e, it, 1, P)
                            hidden_turned(e, it, 0)
                            sigmoids(e, it + 1, 0, P)
                            hidden_turned(e, it, 1)
                        sigmoids(e, last, 1, P)
                        hidden_turned(e, last, 0)
                        hidden_turned(e, last, 1)
                        by_slot(e, P)
                        act.sem_inc(yeT_act.sem, 1)
                        act.sem_inc(ye_act.sem, 1)

                    def expert(e, w):
                        if few(w):
                            return expert_few(e)
                        inputs(e, w)
                        with act.Fori(0, ESTEPS // 2) as it:
                            for i in range(2):
                                sigmoids(e, it, i, FT * w)
                        act.sem_inc(eh_ok.sem, ESTEPS)
                        by_slot(e, w)
                        act.wait_ge(edn_done.sem, e + 1)
                        for bank, k0, k1 in tile_banks(w):
                            if bank % 2 == 0:
                                ins = act.activation(yeT[:, k0:k1, 0:w], G[bank][:, 0:(k1 - k0) * w].rearrange("p (k s) -> p k s", s=w), ACT.Copy)
                        ins.then_inc(yeT_act.sem, 1)
                        act.wait_ge(ye_mm.sem, e + 1)
                        for i, s0, n in blocks(w):
                            ins = act.activation(ye[0:n, i, 512:1024], ye_bank(i, 1)[0:n, :], ACT.Copy)
                        ins.then_inc(ye_act.sem, 1)

                    act.wait_ge(counts_ok.sem, 1)
                    each_expert(act, expert)
            act.wait_ge(x_new.sem, X1 + 1 + 16)
            norm_squares(U_FIN2)

        @block.vector
        def _(dve):
            step = Steps(dve, dve_step.sem)
            dve.sem_inc(x_new.sem, 1)
            dve.sem_inc(proj_dve.sem, 2)
            dve.sem_inc(fhid_ok.sem, FT)
            dve.sem_inc(scat_ev.sem, 1)
            dve.sem_inc(ehid_ok.sem, 2)
            dve.wait_ge(x_in.sem, 16)
            dve.wait_ge(ident_ok.sem, 2)
            dve.wait_ge(consts_in.sem, 16 * N_CONST)

            def normalise(u, v):
                dve.wait_ge(rstd_ok.sem, rstd_ok.at(u, 1))
                for b in range(NB):
                    dve.tensor_scalar(xn[:, b, :], x[:, b, :], small[:, 2 + b:3 + b], None, ALU.mult).then_inc(xn_ok.sem, 1)

            def turned_evac(v, turned, done, mul, add=None):
                for i in (1, 3):
                    dve.wait_ge(turned.sem, turned.at(v, i + 1))
                    for kk in range(2):
                        k = 2 * i + kk
                        src = T[1][:, kk * SEQ:(kk + 1) * SEQ]
                        if mul is None:
                            ins = dve.tensor_copy(hT[:, k, :], src)
                        elif add is None:
                            ins = dve.tensor_scalar(hT[:, k, :], src, mul[:, k:k + 1], None, ALU.mult)
                        else:
                            ins = dve.tensor_scalar(hT[:, k, :], src, mul[:, k:k + 1], add[:, k:k + 1], ALU.mult, ALU.add)
                    ins.then_inc(done.sem, 1)

            def add_to_x(g=None, count=0):
                for half in range(2):
                    for b in range(NB):
                        xs = x[:, b, half * 512:(half + 1) * 512]
                        if g is None:
                            dve.tensor_tensor(xs, G[2 * half + b][:, :], xs, ALU.add).then_inc(x_new.sem, 1)
                        else:
                            tmp = csq.rearrange("p c s -> p (c s)")[:, 0:512]
                            dve.wait_ge(x_new.sem, count + 2 * half + b)
                            step.do(dve.tensor_tensor(tmp, G[2 * half + b][:, :], gateB[:, g, half * 512:(half + 1) * 512], ALU.mult))
                            dve.tensor_tensor(xs, xs, tmp, ALU.add).then_inc(x_new.sem, 1)

            def bcast(ap, shape):
                return ap.broadcast_to(shape)

            dve.wait_ge(cond_ok.sem, 1)
            dve.tensor_tensor(condc, condc, cols[:, 0, R_C:R_C + KD], ALU.mult).then_inc(cond_ok.sem, 1)
            dve.wait_ge(cond_ok.sem, 2)
            with dve.Fori(0, DEPTH) as l:
                step.base, step.n = l * DVE_STEPS, 0
                dve.wait_ge(cur_ok.sem, cur_ok.at(l, 1))
                normalise(l * 2, l * 2)
                turned_evac(l * 2, xn_turned, hT_dve, cur[:, 0:KD])
                lp = curb[:, B_LAM:B_LAM + 128].rearrange("p (a c d) -> p a c d", a=2, c=2)
                lt = small[:, 400:464].rearrange("p (a d) -> p a d", a=2)
                step.do(dve.tensor_tensor(lt, lp[:, :, 0, :], lp[:, :, 1, :], ALU.mult))
                dve.tensor_reduce(small[:, 102:104], lt, AX, ALU.add).then_inc(lam_in.sem, 1)
                step.did(dve.tensor_scalar(curb[:, B_SUB:B_SUB + 64], curb[:, B_SUB:B_SUB + 64], curb[:, B_INIT + 1:B_INIT + 2], None, ALU.mult))
                with dve.Fori(0, 2) as it:
                    for c in range(NSLOT):
                        dve.wait_ge(used[c].sem, used_at(l, 0) + it)
                        dve.tensor_copy(proj[:, 1, bass.ds(it * (NSLOT * PROJ_N) + c * PROJ_N, PROJ_N)],
                                        G[2 * (c % 2) + 1][:, 0:PROJ_N]).then_inc(proj_dve.sem, 1)
                dve.wait_ge(proj_act.sem, proj_act.at(l, 8) + 2)
                dve.wait_ge(proj_dve.sem, proj_dve.at(l, 8) + 2)
                nqk = A_HEADS + A_KV
                for b in range(NB):
                    step.did(dve.tensor_tensor(t1[:, b, :], proj[:, b, 0:nqk * A_DIM], proj[:, b, 0:nqk * A_DIM], ALU.mult))
                step.settle()
                dve.tensor_reduce(small[:, 8:28], rot[:, 1280:2560].rearrange("p (h d) -> p h d", d=A_DIM), AX, ALU.add).then_inc(asq_ok.sem, 1)
                dve.wait_ge(crs_ok.sem, crs_ok.at(l, 1))
                for i, (c0, w) in enumerate(((O_CQ, CQ_RANK), (O_CKV, CKV_RANK))):
                    for b in range(NB):
                        r = small[:, 60 + 2 * i + b:61 + 2 * i + b]
                        ins = dve.tensor_scalar(proj[:, b, c0:c0 + w], proj[:, b, c0:c0 + w], r, None, ALU.mult)
                        if (i, b) == (1, 1):
                            ins.then_inc(cn_ok.sem, 1)
                        else:
                            step.did(ins)
                dve.wait_ge(ars_ok.sem, ars_ok.at(l, 1))
                for b in range(NB):
                    v = proj[:, b, 0:nqk * A_DIM].rearrange("p (h d) -> p h d", d=A_DIM)
                    r = small[:, 32 + 10 * b:42 + 10 * b].unsqueeze(2)
                    step.did(dve.tensor_tensor(t1[:, b].rearrange("p (h d) -> p h d", d=A_DIM), v, bcast(r, [P, nqk, A_DIM]), ALU.mult))
                step.settle()
                for b in range(NB):
                    v = t1[:, b].rearrange("p (h d) -> p h d", d=A_DIM)
                    for h0, h1, at in ((0, A_HEADS, B_AQ), (A_HEADS, nqk, B_AK)):
                        gn = curb[:, at:at + A_DIM].unsqueeze(1)
                        step.did(dve.tensor_tensor(v[:, h0:h1], v[:, h0:h1], bcast(gn, [P, h1 - h0, A_DIM]), ALU.mult))
                step.settle()
                for b in range(NB):
                    v = t1[:, b].rearrange("p (h d) -> p h d", d=A_DIM)
                    w = t2[:, b].rearrange("p (h d) -> p h d", d=A_DIM)
                    for e in range(2):
                        vo = t1[:, b].rearrange("p (h a e d) -> p h a e d", h=nqk, a=2, e=2)[:, :, :, 1 - e, :]
                        wo = t2[:, b].rearrange("p (h a e d) -> p h a e d", h=nqk, a=2, e=2)[:, :, :, e, :]
                        sn = ropeA[:, b, 1, :].rearrange("p (a e d) -> p a e d", a=2, e=2)[:, :, e, :].unsqueeze(1)
                        step.did(dve.tensor_tensor(wo, vo, bcast(sn, [P, nqk, 2, 16]), ALU.mult))
                step.settle()
                for b in range(NB):
                    v = t1[:, b].rearrange("p (h d) -> p h d", d=A_DIM)
                    cs = ropeA[:, b, 0, :].unsqueeze(1)
                    step.did(dve.tensor_tensor(v, v, bcast(cs, [P, nqk, A_DIM]), ALU.mult))
                step.settle()
                for b in range(NB):
                    v = t1[:, b].rearrange("p (h d) -> p h d", d=A_DIM)
                    w = t2[:, b].rearrange("p (h d) -> p h d", d=A_DIM)
                    q_out = aqr[:, b].rearrange("p (i g d) -> p g i d", i=4, g=2)
                    for g in range(A_KV):
                        step.did(dve.tensor_tensor(q_out[:, g], v[:, 4 * g:4 * g + 4], w[:, 4 * g:4 * g + 4], ALU.add))
                    step.did(dve.tensor_tensor(akr[:, b].rearrange("p (h d) -> p h d", d=A_DIM), v[:, A_HEADS:], w[:, A_HEADS:], ALU.add))
                for b in range(NB):
                    v = proj[:, b, O_BQ:O_BV].rearrange("p (u d) -> p u d", d=B_DIM)
                    a = probs[:, b, 0:256].rearrange("p (u d) -> p u d", d=B_ROT)
                    c = probs[:, b, 256:512].rearrange("p (u d) -> p u d", d=B_ROT)
                    step.did(dve.tensor_tensor(a, v[:, :, 0:B_ROT], bcast(ropeB[:, b, 0, :].unsqueeze(1), [P, 32, B_ROT]), ALU.mult))
                    for e in range(2):
                        sn = ropeB[:, b, 1, 4 * e:4 * e + 4].unsqueeze(1)
                        step.did(dve.tensor_tensor(c[:, :, 4 * e:4 * e + 4], v[:, :, 4 - 4 * e:8 - 4 * e], bcast(sn, [P, 32, 4]), ALU.mult))
                for b in range(NB):
                    v = proj[:, b, O_KR:O_KR + C_ROPE]
                    a, c = probs[:, 2 + b, 0:C_ROPE], probs[:, 2 + b, C_ROPE:2 * C_ROPE]
                    step.did(dve.tensor_tensor(a, v, ropeC[:, b, 0, :], ALU.mult))
                    for e in range(2):
                        step.did(dve.tensor_tensor(c[:, 16 * e:16 * e + 16], v[:, 16 - 16 * e:32 - 16 * e], ropeC[:, b, 1, 16 * e:16 * e + 16], ALU.mult))
                step.settle()
                for b in range(NB):
                    a, c = probs[:, 2 + b, 0:C_ROPE], probs[:, 2 + b, C_ROPE:2 * C_ROPE]
                    step.did(dve.tensor_tensor(proj[:, b, O_KR:O_KR + C_ROPE], a, c, ALU.add))
                for b in range(NB):
                    v = proj[:, b, O_BQ:O_BV].rearrange("p (u d) -> p u d", d=B_DIM)
                    a = probs[:, b, 0:256].rearrange("p (u d) -> p u d", d=B_ROT)
                    c = probs[:, b, 256:512].rearrange("p (u d) -> p u d", d=B_ROT)
                    ins = dve.tensor_tensor(v[:, :, 0:B_ROT], a, c, ALU.add)
                    if b == 0:
                        step.did(ins)
                    else:
                        ins.then_inc(rope_ok.sem, 1)
                dve.wait_ge(lam_exp.sem, lam_exp.at(l, 1))
                step.do(dve.tensor_tensor(small[:, 107:108], small[:, 105:106], small[:, 104:105], ALU.subtract))
                step.do(dve.tensor_tensor(small[:, 106:107], small[:, 107:108], curb[:, B_INIT:B_INIT + 1], ALU.subtract))
                step.did(dve.tensor_scalar(lamd, ident[:], small[:, 106:107], None, ALU.mult))
                for i in (1, 3, 5):
                    dve.wait_ge(qk_turned.sem, qk_turned.at(l, i + 1))
                    dst = {1: qk[:, 512:1024], 3: qk[:, 1280:1792], 5: qk[:, 2304:2816]}[i]
                    if i < 5:
                        ins = dve.tensor_scalar(dst, T[1][:, :], (A_DIM if i == 1 else B_DIM) ** -0.5, None, ALU.mult)
                    else:
                        ins = dve.tensor_copy(dst, T[1][:, :])
                    ins.then_inc(qk_dve.sem, 1)
                for half in range(2):
                    for b in range(NB):
                        j = 2 * half + b
                        if j < 3:
                            dve.wait_ge(up_mm.sem, up_mm.at(l, j + 1))
                        else:
                            dve.wait_ge(used[0].sem, used_at(l, 16))
                        dve.tensor_copy(qC[:, b, half * 384:(half + 1) * 384], G[j][:, 0:384]).then_inc(up_ev.sem, 1)
                for half in range(2):
                    for b in range(NB):
                        j = 2 * half + b
                        if j < 3:
                            dve.wait_ge(up_mm.sem, up_mm.at(l, 3 + j + 1))
                        else:
                            dve.wait_ge(used[1].sem, used_at(l, 17))
                        kv = G[j][:, :].rearrange("p (h d) -> p h d", d=C_NOPE + C_V)
                        kh = kC[:, b, half * 384:(half + 1) * 384].rearrange("p (h d) -> p h d", d=C_QK)
                        vh = vC[:, b, half * 256:(half + 1) * 256].rearrange("p (h d) -> p h d", d=C_V)
                        dve.tensor_copy(kh[:, :, 0:C_NOPE], kv[:, :, 0:C_NOPE])
                        dve.tensor_copy(vh, kv[:, :, C_NOPE:]).then_inc(up_ev.sem, 1)
                dve.wait_ge(up_ev.sem, up_ev.at(l, 8))
                for b in range(NB):
                    kh = kC[:, b].rearrange("p (h d) -> p h d", d=C_QK)[:, :, C_NOPE:]
                    step.did(dve.tensor_copy(kh, bcast(proj[:, b, O_KR:O_KR + C_ROPE].unsqueeze(1), [P, C_HEADS, C_ROPE])))
                    v = qC[:, b].rearrange("p (h d) -> p h d", d=C_QK)[:, :, C_NOPE:]
                    a = pT[:, b, 0:256].rearrange("p (h d) -> p h d", d=C_ROPE)
                    c = pT[:, b, 256:512].rearrange("p (h d) -> p h d", d=C_ROPE)
                    step.did(dve.tensor_tensor(a, v, bcast(ropeC[:, b, 0, :].unsqueeze(1), [P, C_HEADS, C_ROPE]), ALU.mult))
                    for e in range(2):
                        sn = ropeC[:, b, 1, 16 * e:16 * e + 16].unsqueeze(1)
                        step.did(dve.tensor_tensor(c[:, :, 16 * e:16 * e + 16], v[:, :, 16 - 16 * e:32 - 16 * e], bcast(sn, [P, C_HEADS, 16]), ALU.mult))
                step.settle()
                for b in range(NB):
                    v = qC[:, b].rearrange("p (h d) -> p h d", d=C_QK)[:, :, C_NOPE:]
                    a = pT[:, b, 0:256].rearrange("p (h d) -> p h d", d=C_ROPE)
                    c = pT[:, b, 256:512].rearrange("p (h d) -> p h d", d=C_ROPE)
                    ins = dve.tensor_tensor(v, a, c, ALU.add)
                    if b == 0:
                        step.did(ins)
                    else:
                        ins.then_inc(ropeC_ok.sem, 1)

                def maxima(u):
                    for s in UNITS[u][2]:
                        dve.wait_ge(sc_mm.sem, sc_mm.at(l, s + 1))
                        dve.tensor_reduce(negmax[:, s % NPROBS, :], SB[s % 4][:, :].rearrange("p (b k) -> p b k", b=NB), AX, ALU.max, negate=True).then_inc(negmax_ok.sem, 1)

                def diagonals(u):
                    if u >= 2:
                        dve.wait_ge(p_turned.sem, p_turned.at(l, u - 1))
                    ss = UNITS[u][2]
                    dve.wait_ge(exp_ok.sem, exp_ok.at(l, ss[-1] + 1))
                    for s in ss:
                        step.did(dve.reciprocal(recips[:, s % NPROBS, :], sums[:, s % NPROBS, :]))
                    step.settle()
                    for j, s in enumerate(ss):
                        ins = dve.tensor_tensor(diag[:, u % 2, j, :].rearrange("p (b q) -> p b q", b=NB), bcast((lamd if j else ident)[:, :].unsqueeze(1), [P, NB, P]),
                                                bcast(recips[:, s % NPROBS, :].unsqueeze(2), [P, NB, P]), ALU.mult)
                    ins.then_inc(diag_ok.sem, 1)

                def result(u):
                    g, last = result_at(u)
                    br, i, _ = UNITS[u]
                    if last:
                        dve.wait_ge(pv_mm.sem, pv_mm.at(l, u + 1))
                        if br == 1:
                            ins = dve.tensor_copy(o[:, :, 64 * i:64 * i + 64], G[g % 2][:, 0:NB * 64].rearrange("p (b d) -> p b d", b=NB))
                        else:
                            ins = dve.tensor_copy(yT[:, 4 * br + i // 2, :], G[g % 2][:, 0:SEQ])
                        ins.then_inc(o_ev.sem, 1)

                def attend(u0, u1):
                    maxima(u0)
                    for u in range(u0, u1):
                        if u + 1 < u1:
                            maxima(u + 1)
                        diagonals(u)
                        if u - 2 >= u0:
                            result(u - 2)
                    for u in (u1 - 2, u1 - 1):
                        result(u)

                step.settle()
                attend(0, 16)
                for i in range(1, 8, 2):
                    dve.wait_ge(qk_turned.sem, qk_turned.at(l, 7 + i + 1))
                    dst = (cqT if i < 4 else ckT)[:, 2 * (i % 4):2 * (i % 4) + 2, :]
                    src = T[(7 + i) % 2][0:C_QK, :].rearrange("p (k s) -> p k s", k=2)
                    if i < 4:
                        ins = dve.tensor_scalar(dst, src, C_QK ** -0.5, None, ALU.mult)
                    else:
                        ins = dve.tensor_copy(dst, src)
                    ins.then_inc(qk_dve.sem, 1)
                attend(16, 24)
                dve.wait_ge(o_ev.sem, o_ev.at(l, 12))
                of = o[:, :, :].rearrange("p b (h d) -> p (b h) d", d=64)
                tf = qk[:, 0:1024].rearrange("p (h d) -> p h d", d=64)
                dve.wait_ge(sc_mm.sem, sc_mm.at(l, 32))
                step.do(dve.tensor_tensor(tf, of, of, ALU.mult))
                dve.tensor_reduce(small[:, 64:80], tf, AX, ALU.add).then_inc(subsq_ok.sem, 1)
                dve.wait_ge(subrs_ok.sem, subrs_ok.at(l, 1))
                step.do(dve.tensor_tensor(of, of, bcast(small[:, 80:96].unsqueeze(2), [P, 16, 64]), ALU.mult))
                dve.tensor_tensor(of, of, bcast(curb[:, B_SUB:B_SUB + 64].unsqueeze(1), [P, 16, 64]), ALU.mult).then_inc(o_ok.sem, 1)
                dve.wait_ge(gate_ev.sem, gate_ev.at(l, 16) + 4)
                for n, br in enumerate(BR_ORDER):
                    if n == 2:
                        dve.wait_ge(o_turned.sem, o_turned.at(l, 2))
                        dve.tensor_copy(yT[:, 6:8, :], T[1][:, :].rearrange("p (k s) -> p k s", k=2)).then_inc(y_dve.sem, 1)
                    for half in range(2):
                        for b in range(NB):
                            j = 2 * half + b
                            if j < 3:
                                dve.wait_ge(br_mm.sem, br_mm.at(l, 3 * n + j + 1))
                            else:
                                dve.wait_ge(used[(18 + n) % NSLOT].sem, used_at(l, 18 + n))
                            gt = gates[:, b, br * D + half * 512:br * D + (half + 1) * 512]
                            m = merged[:, b, half * 512:(half + 1) * 512]
                            if n == 0:
                                dve.tensor_tensor(m, G[j][:, :], gt, ALU.mult).then_inc(br_ev.sem, 1)
                            else:
                                dve.tensor_tensor(gated[:, j % 2], G[j][:, :], gt, ALU.mult).then_inc(br_ev.sem, 1)
                                dve.wait_ge(br_ev.sem, br_ev.at(l, 4 * n + j + 1))
                                ins = dve.tensor_tensor(m, m, gated[:, j % 2], ALU.add)
                                if (n, j) == (2, 3):
                                    ins.then_inc(merged_ok.sem, 1)
                                else:
                                    step.did(ins)
                    if n:
                        step.settle()
                turned_evac(l, mg_turned, mg_dve, None)
                dve.wait_ge(used[23 % NSLOT].sem, used_at(l, 23))
                add_to_x()
                normalise(l * 2 + 1, l * 2 + 1)
                turned_evac(l * 2 + 1, xn_turned, hT_dve, cur[:, KD:2 * KD])
                def ada(it, c):
                    dve.wait_ge(ada_loaded[c % 2].sem, l * (8 * ADA_CHUNKS) + it * 48 + (c // 2 + 1) * 16)
                    out, w = ada_sum[:, bass.ds(it * 6 + c, 1), :].rearrange("p a n -> p (a n)"), ada_in[c % 2]
                    for k in range(KD):
                        if k == 0:
                            ins = dve.tensor_scalar(out, w[:, k, :], condc[:, k:k + 1], None, ALU.mult)
                        else:
                            dve.wait_ge(ada_step.sem, l * (ADA_CHUNKS * KD) + it * (6 * KD) + (c * KD + k))
                            ins = dve.scalar_tensor_tensor(out=out, in0=w[:, k, :], scalar=condc[:, k:k + 1], in1=out, op0=ALU.mult, op1=ALU.add)
                        ins.then_inc(ada_step.sem, 1)

                with dve.Fori(0, 2) as it:
                    for j in range(4):
                        for f in range(4):
                            dve.wait_ge(ff_relu.sem, l * 32 + it * 16 + (j * 4 + f + 1 + 4))
                            dve.tensor_tensor(hid[:, j % 2, f, :], hid[:, j % 2, f, :], hid[:, j % 2, f, :], ALU.mult).then_inc(ff_ev.sem, 1)
                        for c in ((0, 1), (2,), (3, 4), (5,))[j]:
                            ada(it, c)
                dve.wait_ge(ff2_mm.sem, ff2_mm.at(l, 1))
                add_to_x()
                dve.wait_ge(ada_mm.sem, l + 1)
                dve.tensor_tensor(mods[:, bass.ds(l, 1), :].rearrange("p a n -> p (a n)"), S[0][:, 0:MODS * KD],
                                  cols[:, 1, bass.ds(l * (MODS * KD), MODS * KD)], ALU.add).then_inc(adac_ok.sem, 1)
            assert step.n == DVE_STEPS, step.n
            step.base, step.n = DEPTH * DVE_STEPS, 0

            gF = arena[:, 0:D]
            dve.wait_ge(consts_in.sem, 16 * (N_CONST + 1))
            dve.wait_ge(rstd_ok.sem, rstd_ok.at(U_FIN1, 1))
            for b in range(NB):
                ins = dve.scalar_tensor_tensor(out=x[:, b, :], in0=x[:, b, :], scalar=small[:, 2 + b:3 + b], in1=gF, op0=ALU.mult, op1=ALU.mult)
                if b == 0:
                    step.did(ins)
                else:
                    ins.then_inc(blk1_done.sem, 1)
            dve.wait_ge(adac_ok.sem, DEPTH)
            dve.wait_ge(mix_in.sem, 16 * N_MIX)
            dve.wait_ge(half_ok.sem, 2 + KCONV)
            for l in range(DEPTH):
                u = U_MIX + 2 * l
                dve.wait_ge(mix_in.sem, 16 * (N_MIX + (l + 1) * N_MIXL))
                for i, r in enumerate((R2_MIXG, R2_FFNG)):
                    ins = dve.scalar_tensor_tensor(out=mulc[:, KD * i:KD * i + KD], in0=mods[:, l, (3 * i + 1) * KD:(3 * i + 2) * KD], scalar=1.0,
                                                   in1=cols[:, 2, r + l * KD:r + l * KD + KD], op0=ALU.add, op1=ALU.mult)
                    if i == 0:
                        step.do(ins)
                    else:
                        ins.then_inc(mods_ok.sem, 1)
                for g in range(2):
                    ins = dve.tensor_tensor(gateD[g].rearrange("p (k q) -> p k q", k=KD), bcast(ident[:].unsqueeze(1), [P, KD, P]),
                                            bcast(mods[:, l, (3 * g + 2) * KD:(3 * g + 3) * KD].unsqueeze(2), [P, KD, P]), ALU.mult)
                ins.then_inc(mods_ok.sem, 1)
                normalise(u, u - 1)
                dve.wait_ge(mods_ok.sem, mods_ok.at(l, 1))
                turned_evac(u - 1, xn_turned, hT_dve, mulc[:, 0:KD], mods[:, l, 0:KD])
                for b in range(NB):
                    if b == 0:
                        dve.wait_ge(w2_mm.sem, w2_mm.at(l, 1))
                        step.did(dve.tensor_copy(poolA[:, b, :], G[b][:, 0:POOL_W]))
                    else:
                        dve.wait_ge(used[0].sem, used2_at(l, 0))
                        dve.tensor_copy(poolA[:, b, :], G[b][:, 0:POOL_W]).then_inc(pool_ev.sem, 1)
                dve.wait_ge(used[1].sem, used2_at(l, 1))
                for c in range(KCONV):
                    dve.wait_ge(conv_sg.sem, conv_sg.at(l, c + 1))
                    dve.tensor_tensor(glu[:, c, HALO:HALO + SEQ], (G[2], G[3], S[0])[c][:, 0:SEQ], sg[:, c, :], ALU.mult).then_inc(glu_ok.sem, 1)
                for j in range(2):
                    dve.wait_ge(diff_mm.sem, diff_mm.at(l, j + 1))
                    dve.tensor_copy(diffT[:, j, :], T[j][:, 0:SEQ]).then_inc(diff_ev.sem, 1)
                for j in range(2):
                    dve.wait_ge(sw_turned.sem, sw_turned.at(l, j + 1))
                    dve.tensor_copy(swT[:, 3 * j:3 * j + 3, :], T[j][:, 0:3 * P].rearrange("p (h q) -> p h q", h=3)).then_inc(sw_ev.sem, 1)
                for j in range(2):
                    dve.wait_ge(poolo_mm.sem, poolo_mm.at(l, j + 1))
                    dve.tensor_scalar(mixT[:, j, :], S[j][:, 0:SEQ], cols[:, 2, R2_PS + 2 * l + j:R2_PS + 2 * l + j + 1], None, ALU.mult).then_inc(poolo_ev.sem, 1)
                dve.wait_ge(uv_ev.sem, uv_ev.at(l, 4))
                for b in range(NB):
                    step.did(dve.bn_stats(small[:, 150 + 6 * b:156 + 6 * b], vs[:, b, :]))
                step.settle()
                for b in range(NB):
                    step.did(dve.bn_aggr(small[:, 162 + 2 * b:164 + 2 * b], small[:, 150 + 6 * b:156 + 6 * b]))
                step.settle()
                for b in range(NB):
                    ins = dve.tensor_scalar(small[:, 98 + b:99 + b], small[:, 163 + 2 * b:164 + 2 * b], EPS, None, ALU.add)
                    if b == 0:
                        step.do(ins)
                    else:
                        ins.then_inc(var_ok.sem, 1)
                dve.wait_ge(varroot_ok.sem, varroot_ok.at(l, 1))
                for b in range(NB):
                    step.did(dve.tensor_scalar(vs[:, b, :], vs[:, b, :], small[:, 162 + 2 * b:163 + 2 * b], small[:, 100 + b:101 + b], ALU.subtract, ALU.mult))
                step.settle()
                step.do(dve.tensor_tensor(vs, vs, bcast(sguG.unsqueeze(1), [P, NB, SGU_W]), ALU.mult))
                dve.tensor_tensor(vs, vs, bcast(sguB.unsqueeze(1), [P, NB, SGU_W]), ALU.add).then_inc(vn_ok.sem, 1)
                dve.wait_ge(glu_ok.sem, glu_ok.at(l, 3))
                taps = [(c, tap) for c in range(KCONV) for tap in range(TAPS)][PE_TAPS:]
                c1 = taps[0][0]
                begun = set()
                for _, c, tap in sorted((tap - min(t for b, t in taps if b == c), c, tap) for c, tap in taps):
                    w = cwc[:, l, c, tap:tap + 1]
                    if c not in begun:
                        step.do(dve.tensor_scalar(cacc[:, c, :], glu[:, c, tap:tap + SEQ], w, cols[:, 2, R2_CB + l * KCONV + c:R2_CB + l * KCONV + c + 1], ALU.mult, ALU.add))
                        begun.add(c)
                    else:
                        step.do(dve.scalar_tensor_tensor(out=cacc[:, c, :], in0=glu[:, c, tap:tap + SEQ], scalar=w, in1=cacc[:, c, :], op0=ALU.mult, op1=ALU.add))
                for h in range(SGU_HEADS):
                    dve.wait_ge(sgu_mm.sem, sgu_mm.at(l, h // 4 + 1))
                    src = G[h // 4][:, (h % 4) * P:(h % 4 + 1) * P].rearrange("p (b d) -> p b d", b=NB)
                    ins = dve.scalar_tensor_tensor(out=outc[:, :, h * SGU_D:(h + 1) * SGU_D], in0=src,
                                                   scalar=cols[:, 2, R2_SB + l * SGU_HEADS + h:R2_SB + l * SGU_HEADS + h + 1],
                                                   in1=us[:, :, h * SGU_D:(h + 1) * SGU_D], op0=ALU.add, op1=ALU.mult)
                    if h < SGU_HEADS - 1:
                        step.did(ins)
                    else:
                        ins.then_inc(outc_ok.sem, 1)
                for c in range(c1 + 1):
                    dve.wait_ge(ctaps_mm.sem, ctaps_mm.at(l, c + 1))
                    if c in begun:
                        ins = dve.tensor_tensor(cacc[:, c, :], T[c][:, 0:SEQ], cacc[:, c, :], ALU.add)
                    else:
                        ins = dve.tensor_scalar(cacc[:, c, :], T[c][:, 0:SEQ], cols[:, 2, R2_CB + l * KCONV + c:R2_CB + l * KCONV + c + 1], None, ALU.add)
                    if c < c1:
                        step.do(ins)
                    else:
                        ins.then_inc(cacc_ok.sem, 1)
                dve.wait_ge(cmean_mm.sem, l + 1)
                for c in range(KCONV):
                    step.did(dve.scalar_tensor_tensor(out=cacc[:, c, :], in0=S[0][:, 0:SEQ], scalar=-1.0 / CONV_W, in1=cacc[:, c, :], op0=ALU.mult, op1=ALU.add))
                step.settle()
                for c in range(KCONV):
                    ins = dve.tensor_tensor(csq[:, c, :], cacc[:, c, :], cacc[:, c, :], ALU.mult)
                    if c < KCONV - 1:
                        step.did(ins)
                    else:
                        ins.then_inc(cdev_ok.sem, 1)
                dve.wait_ge(cvar_mm.sem, l + 1)
                dve.tensor_scalar(small[:, 400:402], S[1][:, 0:NB], 1.0 / CONV_W, EPS, ALU.mult, ALU.add).then_inc(var_ok.sem, 1)
                dve.wait_ge(varroot_ok.sem, varroot_ok.at(l, 2))
                dve.tensor_tensor(crdiag.rearrange("p (b q) -> p b q", b=NB), bcast(ident[:].unsqueeze(1), [P, NB, P]),
                                  bcast(small[:, 402:404].unsqueeze(2), [P, NB, P]), ALU.mult).then_inc(crdiag_ok.sem, 1)
                dve.wait_ge(crb_mm.sem, l + 1)
                for c in range(KCONV):
                    step.did(dve.tensor_tensor(cacc[:, c, :], cacc[:, c, :], S[0][:, 0:SEQ], ALU.mult))
                step.settle()
                for c in range(KCONV):
                    gc = cols[:, 2, R2_CG + l * KCONV + c:R2_CG + l * KCONV + c + 1]
                    bcc = cols[:, 2, R2_CLB + l * KCONV + c:R2_CLB + l * KCONV + c + 1]
                    dve.tensor_scalar(cacc[:, c, :], cacc[:, c, :], gc, bcc, ALU.mult, ALU.add).then_inc(cln_ok.sem, 1)
                dve.wait_ge(cln_ok.sem, cln_ok.at(l, 3))
                for c in range(KCONV):
                    dve.wait_ge(csig_ok.sem, csig_ok.at(l, c + 1))
                    dve.tensor_tensor(mixT[:, 2 + c, :], cacc[:, c, :], sg[:, c, :], ALU.mult).then_inc(conv_ok.sem, 1)
                dve.wait_ge(adaG_ev.sem, l + 1)
                dve.wait_ge(used[7 % NSLOT].sem, used2_at(l, 7))
                add_to_x(0, X1 + 1 + 8 * l)
                dve.wait_ge(x_new.sem, X1 + 1 + 8 * l + 4)
                normalise(u + 1, u)
                turned_evac(u, xn_turned, hT_dve, mulc[:, KD:2 * KD], mods[:, l, 3 * KD:4 * KD])

                def hidden(n, i, count):
                    for f in range(FT):
                        dve.wait_ge(fsg_ok.sem, n * FT + (f + 1))
                        dve.tensor_tensor(ffsg[:, f, :], H4[2 * f][:, 0:SEQ], ffsg[:, f, :], ALU.mult).then_inc(ft_ok.sem, 1)
                        if f == 0:
                            dve.wait_ge(fu_mm.sem, n + 1)
                        else:
                            dve.wait_ge(sub_used[i][1].sem, count)
                        dve.wait_ge(ft_ok.sem, n * FT + (f + 1))
                        dve.tensor_tensor(ffhid[:, i, f, :], H4[2 * f + 1][:, 0:SEQ], ffsg[:, f, :], ALU.mult).then_inc(fhid_ok.sem, 1)

                if l == 0:
                    with dve.Fori(0, 5) as it:
                        for i in range(2):
                            hidden(it * 2 + i, i, it + 2)
                    hidden(10, 0, 7)
                    dve.wait_ge(fdn_done.sem, 1)
                    add_to_x(1, X1 + 1 + 8 * l + 4)
                else:
                    dve.wait_ge(rt_mm.sem, 1)
                    lg = small[:, 160:176].rearrange("p (b e) -> p b e", b=NB)
                    step.do(dve.tensor_tensor(lg, S[0][:, 0:NB * EXPERTS].rearrange("p (b e) -> p b e", b=NB), bcast(rb.unsqueeze(1), [P, NB, EXPERTS]), ALU.add))
                    for b in range(NB):
                        step.did(dve.max(small[:, 176 + 8 * b:184 + 8 * b], lg[:, b, :]))
                    step.settle()
                    mx = small[:, 176:192].rearrange("p (b e) -> p b e", b=NB)
                    for b in range(NB):
                        step.did(dve.max_index(idx[:, b, :], mx[:, b, :], lg[:, b, :]))
                    dve.tensor_tensor(small[:, 196:198], mx[:, :, 1], mx[:, :, 0], ALU.subtract).then_inc(rt_max.sem, 1)
                    step.settle()
                    idf = small[:, 208:224].rearrange("p (b e) -> p b e", b=NB)
                    step.do(dve.tensor_copy(idf, idx[:, :, :]))
                    dve.wait_ge(rt_exp.sem, 1)
                    step.do(dve.tensor_scalar(small[:, 202:204], small[:, 200:202], 1.0, None, ALU.add))
                    step.do(dve.reciprocal(small[:, 204:206], small[:, 202:204]))
                    step.do(dve.tensor_tensor(small[:, 206:208], small[:, 200:202], small[:, 204:206], ALU.mult))
                    for b in range(NB):
                        first, second = small[:, 310 + 16 * b:318 + 16 * b], small[:, 318 + 16 * b:326 + 16 * b]
                        step.did(dve.tensor_scalar(first, io8, idf[:, b, 0:1], None, ALU.is_equal))
                        step.did(dve.tensor_scalar(second, io8, idf[:, b, 1:2], None, ALU.is_equal))
                    step.did(dve.memset(place, -1.0))
                    step.did(dve.memset(weight, 0.0))
                    step.did(dve.memset(yacc, 0.0))
                    step.settle()
                    for b in range(NB):
                        first, second = small[:, 310 + 16 * b:318 + 16 * b], small[:, 318 + 16 * b:326 + 16 * b]
                        step.do(dve.tensor_tensor(chosen[:, b, :], first, second, ALU.add))
                        step.did(dve.tensor_scalar(first, first, small[:, 204 + b:205 + b], None, ALU.mult))
                        step.do(dve.tensor_scalar(second, second, small[:, 206 + b:207 + b], None, ALU.mult))
                        ins = dve.tensor_tensor(weight[:, b, 0:EXPERTS], first, second, ALU.add)
                        if b == 0:
                            step.do(ins)
                        else:
                            ins.then_inc(chosen_ok.sem, 1)
                    dve.wait_ge(rank_mm.sem, 1)
                    step.did(dve.tensor_copy(counts[:], S[0][:, 32:40]))
                    step.do(dve.scalar_tensor_tensor(out=place[:, :, 0:EXPERTS], in0=S[0][:, 16:32].rearrange("p (b e) -> p b e", b=NB),
                                                     scalar=1.0, in1=chosen, op0=ALU.add, op1=ALU.mult))
                    dve.tensor_scalar(place[:, :, 0:EXPERTS], place[:, :, 0:EXPERTS], -1.0, None, ALU.add).then_inc(counts_ok.sem, 1)
                    dve.wait_ge(chosen_ok.sem, 1)
                    dve.wait_ge(counts_ok.sem, 1)

                    def select(e):
                        dve.tensor_copy(curp.unsqueeze(2), place[:, :, bass.ds(e, 1)])
                        dve.tensor_copy(curw.unsqueeze(2), weight[:, :, bass.ds(e, 1)]).then_inc(cur_loaded.sem, 1)
                        dve.wait_ge(cur_loaded.sem, e + 1)
                        for b in range(NB):
                            ins = dve.tensor_scalar(sel[:, b, :], slots, curp[:, b:b + 1], None, ALU.is_equal)
                        ins.then_inc(sel_ok.sem, 1)

                    def add_results(e):
                        dve.wait_ge(scat_ev.sem, e * 4 + 1)
                        for half in range(2):
                            for b in range(NB):
                                j = 2 * half + b
                                ys = yacc[:, b, half * 512:(half + 1) * 512]
                                dve.wait_ge(scat_mm.sem, e * 4 + (j + 1))
                                dve.tensor_tensor(ys, G[j][:, :], ys, ALU.add).then_inc(scat_ev.sem, 1)

                    def expert(e, w):
                        wide = max(w, P)
                        dve.wait_ge(gath_mm.sem, e + 1)
                        for k in range(KD):
                            bank, c0 = tile_at(k, wide)
                            if bank % 2 == 1:
                                ins = dve.tensor_scalar(hTe[:, k, 0:wide], H4[bank][:, c0:c0 + wide], mulc[:, KD + k:KD + k + 1], mods[:, l, 3 * KD + k:3 * KD + k + 1], ALU.mult, ALU.add)
                        ins.then_inc(hTe_dve.sem, 1)
                        n = FEW if few(w) else P * len(blocks(w))
                        for b in range(NB):
                            for c0 in range(0, max(n, P), n):
                                ins = dve.tensor_scalar(selw[:, b, c0:c0 + n], slots[:, 0:n], curp[:, b:b + 1], curw[:, b:b + 1], ALU.is_equal, ALU.mult)
                        ins.then_inc(selw_ok.sem, 1)
                        dve.wait_ge(sel_ok.sem, e + 1)
                        dve.wait_ge(selw_ok.sem, e + 1)
                        select(e + 1)
                        with dve.Fori(0, ESTEPS // 2) as it:
                            for i in range(2):
                                n = e * ESTEPS + it * 2
                                cols_n = P if few(w) else FT * w
                                hidden_to = emsg[:, i, P:2 * P] if few(w) else ehid[:, i, 0:FT * w]
                                dve.wait_ge(esg_ok.sem, n + (i + 1))
                                dve.tensor_tensor(emsg[:, i, 0:cols_n], H4[2 * i][:, 0:cols_n], emsg[:, i, 0:cols_n], ALU.mult).then_inc(et_ok.sem, 1)
                                dve.wait_ge(sub_used[i][1].sem, e * (ESTEPS // 2) + it + (8 - i))
                                dve.wait_ge(et_ok.sem, n + (i + 1))
                                dve.tensor_tensor(hidden_to, H4[2 * i + 1][:, 0:cols_n], emsg[:, i, 0:cols_n], ALU.mult).then_inc(ehid_ok.sem, 1)
                        dve.wait_ge(edn_done.sem, e + 1)
                        if few(w):
                            dve.tensor_copy(ye[:, 0, 0:512], G[0][:, :]).then_inc(ye_dve.sem, 1)
                            dve.sem_inc(yeT_dve.sem, 1)
                            return add_results(e)
                        for bank, k0, k1 in tile_banks(w):
                            if bank % 2 == 1:
                                ins = dve.tensor_copy(yeT[:, k0:k1, 0:w], G[bank][:, 0:(k1 - k0) * w].rearrange("p (k s) -> p k s", s=w))
                        ins.then_inc(yeT_dve.sem, 1)
                        dve.wait_ge(ye_mm.sem, e + 1)
                        for i, s0, n in blocks(w):
                            ins = dve.tensor_copy(ye[0:n, i, 0:512], ye_bank(i, 0)[0:n, :])
                        ins.then_inc(ye_dve.sem, 1)
                        add_results(e)

                    select(0)
                    each_expert(dve, expert)
                    dve.wait_ge(scat_ev.sem, EXPERTS * 4 + 1)
                    for half in range(2):
                        for b in range(NB):
                            hs = slice(half * 512, (half + 1) * 512)
                            step.do(dve.tensor_tensor(yacc[:, b, hs], yacc[:, b, hs], gateB[:, 1, hs], ALU.mult))
                            dve.tensor_tensor(x[:, b, hs], x[:, b, hs], yacc[:, b, hs], ALU.add).then_inc(x_new.sem, 1)
            dve.wait_ge(rstd_ok.sem, rstd_ok.at(U_FIN2, 1))
            for b in range(NB):
                dve.scalar_tensor_tensor(out=x[:, b, :], in0=x[:, b, :], scalar=small[:, 2 + b:3 + b], in1=finB, op0=ALU.mult, op1=ALU.mult).then_inc(out_ok.sem, 1)

        @block.tensor
        def _(pe):
            mm = pe.matmul

            def weights(l, pos, at=None):
                i = pos % NSLOT
                pe.wait_ge(loaded[i].sem, (l * (L1_CHUNKS // NSLOT) + pos // NSLOT + 1) * 16 if at is None else at)
                return slot(pos)

            def turn(v, src, ready, count, turned, done_a, done_d, whole=True):
                pe.wait_ge(ready.sem, count)
                for i in range(4):
                    if i == 2:
                        pe.wait_ge(done_a.sem, done_a.at(v, 1))
                    if i == 3:
                        pe.wait_ge(done_d.sem, done_d.at(v, 1))
                    for kk in range(2):
                        for b in range(NB):
                            k = 2 * i + kk
                            ins = pe.transpose(T[i % 2][:, kk * SEQ + b * P:kk * SEQ + (b + 1) * P], src[:, b, k * P:(k + 1) * P], ident[:])
                    ins.then_inc(turned.sem, 1)
                if whole:
                    pe.wait_ge(done_a.sem, done_a.at(v, 2))
                    pe.wait_ge(done_d.sem, done_d.at(v, 2))

            def open_banks():
                for j in range(4):
                    mm(G[j][:, 0:2], ident[:], zcol[:], start=True, stop=False, skip_group_check=True)

            def close_banks(done):
                for j in range(4):
                    ins = mm(G[j][:, 0:2], ident[:], zcol[:], start=False, stop=True, skip_group_check=True)
                ins.then_inc(done.sem, 1)

            pe.wait_ge(ident_ok.sem, 2)
            pe.wait_ge(rows_in.sem, 16 * N_ROWS)
            for i, n in enumerate((R_C + KD, DEPTH * MODS * KD, R2_N)):
                ins = pe.transpose(T[0][:, i * P:i * P + n], rows[0:n, i, :], ident[0:n, 0:n])
            ins.then_inc(rows_turned.sem, 1)
            for l in range(DEPTH):
                for c in range(KCONV):
                    ins = pe.transpose(T[1][:, l * 128 + c * TAPS:l * 128 + (c + 1) * TAPS], cwr[:, l, c * P:(c + 1) * P], ident[0:TAPS, 0:TAPS])
            ins.then_inc(rows_turned.sem, 1)
            pe.wait_ge(cols_ok.sem, 2)

            with pe.Fori(0, DEPTH) as l:
                turn(l * 2, xn, xn_ok, xn_ok.at(l * 2, 2), xn_turned, hT_act, hT_dve, whole=False)
                for part, n in ((0, PROJ_N), (1, GATE_N)):
                    with pe.Fori(0, 2) as it:
                        if part == 0:
                            pe.wait_ge(hT_act.sem, hT_act.at(l * 2, 2))
                            pe.wait_ge(hT_dve.sem, hT_dve.at(l * 2, 2))
                        else:
                            pe.wait_ge(proj_act.sem, proj_act.at(l, 8) + 2)
                            pe.wait_ge(proj_dve.sem, proj_dve.at(l, 8) + 2)
                        for c in range(NSLOT):
                            w = weights(l, 8 * part + c, (l * 10 + it + (2 * part + 1)) * 16)[:, 0:KD * n].rearrange("p (k n) -> p k n", k=KD)
                            for b in range(NB):
                                if part == 0:
                                    pe.wait_ge((proj_act if b == 0 else proj_dve).sem, l * 8 + it * 4 + (c + 1))
                                else:
                                    pe.wait_ge(gate_ev.sem, l * 16 + it * 8 + (2 * c + b + 1))
                                for k in range(KD):
                                    ins = mm(G[2 * (c % 2) + b][:, 0:n], hT[:, k, b * P:(b + 1) * P], w[:, k, :], start=(k == 0), stop=(k == KD - 1))
                                ins.then_inc(((proj_mm, gate_mm)[part] if b == 0 else used[c]).sem, 1)
                pe.wait_ge(cn_ok.sem, cn_ok.at(l, 1))
                for i in range(3):
                    if i == 2:
                        pe.wait_ge(cn_ev.sem, cn_ev.at(l, 1))
                    for kk in range(2 if i < 2 else 1):
                        for b in range(NB):
                            c0 = O_CQ + (2 * i + kk) * P
                            ins = pe.transpose(T[i % 2][:, kk * SEQ + b * P:kk * SEQ + (b + 1) * P], proj[:, b, c0:c0 + P], ident[:])
                    ins.then_inc(cn_turned.sem, 1)
                pe.wait_ge(rope_ok.sem, rope_ok.at(l, 1))
                pe.wait_ge(cn_ev.sem, cn_ev.at(l, 3))
                src = ([(aqr, 256 * i) for i in range(2)] + [(akr, 0)] + [(proj, O_BQ + 256 * i) for i in range(4)])
                for i, (s, c0) in enumerate(src):
                    if i >= 2:
                        (pe.wait_ge(qk_act.sem, qk_act.at(l, i // 2)) if i % 2 == 0 else pe.wait_ge(qk_dve.sem, qk_dve.at(l, i // 2)))
                    for kk in range(1 if i == 2 else 2):
                        for b in range(NB):
                            ins = pe.transpose(T[i % 2][:, kk * SEQ + b * P:kk * SEQ + (b + 1) * P], s[:, b, c0 + kk * P:c0 + (kk + 1) * P], ident[:])
                    ins.then_inc(qk_turned.sem, 1)
                pe.wait_ge(gate_ev.sem, gate_ev.at(l, 16) + 4)
                w = weights(l, 16)[:, 0:KCQ * 768].rearrange("p (k n) -> p k n", k=KCQ)
                for half in range(2):
                    for b in range(NB):
                        j = 2 * half + b
                        for k in range(KCQ):
                            ins = mm(G[j][:, 0:384], cnT[:, k, b * P:(b + 1) * P], w[:, k, half * 384:(half + 1) * 384], start=(k == 0), stop=(k == KCQ - 1))
                        ins.then_inc((up_mm if j < 3 else used[0]).sem, 1)
                w = weights(l, 17)[:, 0:KCKV * 1024].rearrange("p (k n) -> p k n", k=KCKV)
                for half in range(2):
                    for b in range(NB):
                        j = 2 * half + b
                        pe.wait_ge(up_ev.sem, up_ev.at(l, j + 1))
                        for k in range(KCKV):
                            ins = mm(G[j][:, :], cnT[:, KCQ + k, b * P:(b + 1) * P], w[:, k, half * 512:(half + 1) * 512], start=(k == 0), stop=(k == KCKV - 1))
                        ins.then_inc((up_mm if j < 3 else used[1]).sem, 1)

                def operands(u, j):
                    br, i, _ = UNITS[u]
                    if br == 0:
                        r = slice(64 * (i // 4), 64 * (i // 4) + 64)
                        return aqT[r, i % 4, :], akT[r, :], lambda kb: proj[:, kb, O_AV + 64 * (i // 4):O_AV + 64 * (i // 4) + 64]
                    if br == 1:
                        h = 2 * i + j
                        r = slice(32 * (h % 4), 32 * (h % 4) + 32)
                        return bqT[r, h // 4, :], bkT[r, h // 4, :], lambda kb: proj[:, kb, O_BV + 64 * i:O_BV + 64 * i + 64]
                    return cqT[:, i, :], ckT[:, i, :], lambda kb: vC[:, kb, 64 * i:64 * i + 64]

                def scores(u):
                    for j, s in enumerate(UNITS[u][2]):
                        q, k, _ = operands(u, j)
                        if s >= 4:
                            pe.wait_ge(exp_ok.sem, exp_ok.at(l, s - 3))
                        for b in range(NB):
                            ins = mm(SB[s % 4][:, b * SEQ:(b + 1) * SEQ], q[:, b * P:(b + 1) * P], k, start=True, stop=True)
                        ins.then_inc(sc_mm.sem, 1)

                def turn_probs(u):
                    pe.wait_ge(diag_ok.sem, diag_ok.at(l, u + 1))
                    if u >= 2:
                        pe.wait_ge(pT_ok.sem, pT_ok.at(l, u - 1))
                    ss = UNITS[u][2]
                    for kb in range(NB):
                        for b in range(NB):
                            for j, s in enumerate(ss):
                                ins = mm(T[u % 2][:, kb * SEQ + b * P:kb * SEQ + (b + 1) * P], probs[:, s % NPROBS, b * SEQ + kb * P:b * SEQ + (kb + 1) * P],
                                         diag[:, u % 2, j, b * P:(b + 1) * P], start=(j == 0), stop=(j == len(ss) - 1))
                    ins.then_inc(p_turned.sem, 1)

                def values(u):
                    br, i, _ = UNITS[u]
                    g, last = result_at(u)
                    v = operands(u, 0)[2]
                    pe.wait_ge(pT_ok.sem, pT_ok.at(l, u + 1))
                    if g >= 2:
                        pe.wait_ge(o_ev.sem, o_ev.at(l, g - 1))
                    if br == 1:
                        for b in range(NB):
                            for kb in range(NB):
                                ins = mm(G[g % 2][:, b * 64:(b + 1) * 64], pT[:, u % 2, kb * SEQ + b * P:kb * SEQ + (b + 1) * P], v(kb), start=(kb == 0), stop=(kb == NB - 1))
                    else:
                        r = 64 * (i % 2)
                        for kb in range(NB):
                            ins = mm(G[g % 2][r:r + 64, 0:SEQ], v(kb), pT[:, u % 2, kb * SEQ:(kb + 1) * SEQ], start=(kb == 0), stop=(kb == NB - 1))
                    ins.then_inc(pv_mm.sem, 1)

                def attend(u0, u1):
                    scores(u0)
                    scores(u0 + 1)
                    for u in range(u0, u1):
                        turn_probs(u)
                        if u + 2 < u1:
                            scores(u + 2)
                        if u > u0:
                            values(u - 1)
                    values(u1 - 1)

                pe.wait_ge(up_ev.sem, up_ev.at(l, 8))
                pe.wait_ge(qk_act.sem, qk_act.at(l, 4))
                pe.wait_ge(qk_dve.sem, qk_dve.at(l, 3))
                attend(0, 16)
                pe.wait_ge(ropeC_ok.sem, ropeC_ok.at(l, 1))
                pe.wait_ge(pT_ok.sem, pT_ok.at(l, 16))
                for i in range(8):
                    if i >= 2:
                        (pe.wait_ge(qk_act.sem, qk_act.at(l, 4 + i // 2)) if i % 2 == 0 else pe.wait_ge(qk_dve.sem, qk_dve.at(l, 3 + i // 2)))
                    for kk in range(2):
                        for b in range(NB):
                            h = 2 * (i % 4) + kk
                            s = qC if i < 4 else kC
                            ins = pe.transpose(T[(7 + i) % 2][0:C_QK, kk * SEQ + b * P:kk * SEQ + (b + 1) * P], s[:, b, h * C_QK:(h + 1) * C_QK], ident[:])
                    ins.then_inc(qk_turned.sem, 1)
                pe.wait_ge(qk_act.sem, qk_act.at(l, 8))
                pe.wait_ge(qk_dve.sem, qk_dve.at(l, 7))
                attend(16, 24)
                pe.wait_ge(o_ev.sem, o_ev.at(l, 16))
                for n, br in enumerate(BR_ORDER):
                    if br == 1:
                        pe.wait_ge(o_ok.sem, o_ok.at(l, 1))
                        for i in range(2):
                            for kk in range(2):
                                for b in range(NB):
                                    ins = pe.transpose(T[i][:, kk * SEQ + b * P:kk * SEQ + (b + 1) * P], o[:, b, (2 * i + kk) * P:(2 * i + kk + 1) * P], ident[:])
                            ins.then_inc(o_turned.sem, 1)
                        pe.wait_ge(y_act.sem, y_act.at(l, 1))
                        pe.wait_ge(y_dve.sem, y_dve.at(l, 1))
                    w = weights(l, 18 + n).rearrange("p (k n) -> p k n", k=4)
                    for half in range(2):
                        for b in range(NB):
                            j = 2 * half + b
                            if n:
                                pe.wait_ge(br_ev.sem, br_ev.at(l, 4 * (n - 1) + j + 1))
                            for k in range(4):
                                ins = mm(G[j][:, :], yT[:, 4 * br + k, b * P:(b + 1) * P], w[:, k, half * 512:(half + 1) * 512], start=(k == 0), stop=(k == 3))
                            ins.then_inc((br_mm if j < 3 else used[(18 + n) % NSLOT]).sem, 1)
                turn(l, merged, merged_ok, merged_ok.at(l, 1), mg_turned, mg_act, mg_dve)
                k = 0
                for n, kn in enumerate((3, 3, 2)):
                    w = weights(l, 21 + n)[:, 0:kn * D].rearrange("p (k n) -> p k n", n=D)
                    for kk in range(kn):
                        for half in range(2):
                            for b in range(NB):
                                ins = mm(G[2 * half + b][:, :], hT[:, k, b * P:(b + 1) * P], w[:, kk, half * 512:(half + 1) * 512], start=(k == 0), stop=(k == KD - 1))
                        k += 1
                    ins.then_inc(used[(21 + n) % NSLOT].sem, 1)
                turn(l * 2 + 1, xn, xn_ok, xn_ok.at(l * 2 + 1, 2), xn_turned, hT_act, hT_dve)
                open_banks()
                with pe.Fori(0, 4) as it:
                    for j in range(2):
                        w = weights(l, 2 * j, (l * 10 + it + 7) * 16).rearrange("p (k n) -> p k n", k=KD)
                        for f in range(4):
                            pe.wait_ge(ff_relu.sem, l * 32 + it * 8 + (4 * j + f + 1))
                            for k in range(KD):
                                ins = mm(H4[f][:, 0:SEQ], w[:, k, f * P:(f + 1) * P], hT[:, k, :], start=(k == 0), stop=(k == KD - 1))
                            ins.then_inc((ff_mm if f < 3 else used[2 * j]).sem, 1)
                        w = weights(l, 2 * j + 1, (l * 10 + it + 7) * 16).rearrange("p (k n) -> p k n", k=4)
                        for f in range(4):
                            pe.wait_ge(ff_ev.sem, l * 32 + it * 8 + (4 * j + f + 1))
                            for half in range(2):
                                for b in range(NB):
                                    ins = mm(G[2 * half + b][:, :], hid[:, j, f, b * P:(b + 1) * P], w[:, f, half * 512:(half + 1) * 512], start=False, stop=False, skip_group_check=True)
                        ins.then_inc(used[2 * j + 1].sem, 1)
                close_banks(ff2_mm)
                pe.wait_ge(ada_step.sem, ada_step.at(l, ADA_CHUNKS * KD))
                for j in range(MODS * KD):
                    ins = mm(S[0][:, j:j + 1], ada_sum[:, j // 4, j % 4 * P:(j % 4 + 1) * P], onec[:, 0:1], start=True, stop=True)
                ins.then_inc(ada_mm.sem, 1)

            pe.wait_ge(mix_in.sem, 16 * N_MIX)
            pe.wait_ge(half_ok.sem, 2 + KCONV)
            for l in range(DEPTH):
                v = U_MIX + 2 * l - 1
                b2 = (DEPTH * L1_CHUNKS + l * L2_CHUNKS) // NSLOT
                pe.wait_ge(mix_in.sem, 16 * (N_MIX + (l + 1) * N_MIXL))
                turn(v, xn, xn_ok, xn_ok.at(v, 2), xn_turned, hT_act, hT_dve)

                def chunk(pos, n=512):
                    return weights(0, pos, (b2 + pos // NSLOT + 1) * 16)[:, 0:KD * n].rearrange("p (k n) -> p k n", k=KD)

                def tokens(pos, n, banks, sem):
                    w = chunk(pos, n)
                    for b in range(NB):
                        for k in range(KD):
                            ins = mm(banks[b][:, 0:n], hT[:, k, b * P:(b + 1) * P], w[:, k, :], start=(k == 0), stop=(k == KD - 1))
                        ins.then_inc((sem if b == 0 else used[pos % NSLOT]).sem, 1)

                def features(pos, n, banks, sem):
                    w = chunk(pos, n)
                    for f in range(n // P):
                        for k in range(KD):
                            ins = mm(banks[f][:, 0:SEQ], w[:, k, f * P:(f + 1) * P], hT[:, k, :], start=(k == 0), stop=(k == KD - 1))
                        ins.then_inc((sem if f < n // P - 1 else used[pos % NSLOT]).sem, 1)

                tokens(0, POOL_W, (G[0], G[1]), w2_mm)
                features(1, CONV_W, (G[2], G[3], S[0]), w2_mm)
                features(2, CONV_W, (S[1], T[0], T[1]), w2_mm)
                pe.wait_ge(pool_ev.sem, l + 1)
                tokens(3, SGU_W, (G[0], G[1]), w2_mm)
                pe.wait_ge(glu_ok.sem, glu_ok.at(l, 3))
                tokens(4, SGU_W, (G[2], G[3]), w2_mm)
                for g in range(4):
                    j, r = g // 2, 64 * (g % 2)
                    for b in range(NB):
                        ins = mm(T[j][r:r + 64, 0:SEQ], poolA[:, b, g * 64:(g + 1) * 64], band[:, b, g, :], start=(b == 0), stop=(b == NB - 1))
                    if g % 2:
                        ins.then_inc(diff_mm.sem, 1)
                for j in range(2):
                    pe.wait_ge(diff_ev.sem, diff_ev.at(l, j + 1))
                    for h in range(3):
                        ins = pe.transpose(T[j][:, h * P:(h + 1) * P], swr[:, 3 * j + h, :], ident[:])
                    ins.then_inc(sw_turned.sem, 1)
                for g in range(4):
                    j, r = g // 2, 64 * (g % 2)
                    ins = mm(S[j][r:r + 64, 0:SEQ], pw[r:r + 64, j, :], diffT[r:r + 64, j, :], start=True, stop=True)
                    if g % 2:
                        ins.then_inc(poolo_mm.sem, 1)
                pe.wait_ge(sw_ev.sem, sw_ev.at(l, 2))
                pe.wait_ge(cdiag_ok.sem, l + 1)
                tiles = [d[:, i, :] for d in cdiag for i in range(d.shape[1])]
                for n, w in enumerate(tiles):
                    c, tap = n // TAPS, n % TAPS
                    last = n == PE_TAPS - 1 or tap == TAPS - 1
                    ins = mm(T[c][:, 0:SEQ], w, glu[:, c, tap:tap + SEQ], start=(tap == 0), stop=last)
                    if last:
                        ins.then_inc(ctaps_mm.sem, 1)
                pe.wait_ge(vn_ok.sem, l + 1)
                for h in range(SGU_HEADS):
                    ins = mm(G[h // 4][:, (h % 4) * P:(h % 4 + 1) * P], swT[:, h, :], vs[:, :, h * SGU_D:(h + 1) * SGU_D], start=True, stop=True)
                    if h in (3, SGU_HEADS - 1):
                        ins.then_inc(sgu_mm.sem, 1)
                pe.wait_ge(poolo_ev.sem, poolo_ev.at(l, 2))
                pe.wait_ge(cacc_ok.sem, l + 1)
                for c in range(KCONV):
                    ins = mm(S[0][:, 0:SEQ], ones, cacc[:, c, :], start=(c == 0), stop=(c == KCONV - 1))
                ins.then_inc(cmean_mm.sem, 1)
                pe.wait_ge(outc_ok.sem, l + 1)
                for i in range(2):
                    for kk in range(2 - i):
                        for b in range(NB):
                            k = 2 * i + kk
                            ins = pe.transpose(G[2 + i][:, kk * SEQ + b * P:kk * SEQ + (b + 1) * P], outc[:, b, k * P:(k + 1) * P], ident[:])
                    ins.then_inc(outc_turned.sem, 1)
                pe.wait_ge(cdev_ok.sem, l + 1)
                for b in range(NB):
                    for c in range(KCONV):
                        ins = mm(S[1][:, b:b + 1], csq[:, c, b * P:(b + 1) * P], onec[:, 0:1], start=(c == 0), stop=(c == KCONV - 1))
                ins.then_inc(cvar_mm.sem, 1)
                pe.wait_ge(outc_ev.sem, outc_ev.at(l, 2))
                pe.wait_ge(mods_ok.sem, mods_ok.at(l, 2))
                for c in range(4):
                    mm(G[c][:, :], ones, gateD[c // 2][:, (c % 2) * 512:(c % 2 + 1) * 512], start=True, stop=True).then_inc(gateB_mm.sem, 1)
                pe.wait_ge(crdiag_ok.sem, l + 1)
                mm(S[0][:, 0:SEQ], ones, crdiag, start=True, stop=True).then_inc(crb_mm.sem, 1)
                pe.wait_ge(conv_ok.sem, conv_ok.at(l, 3))
                pe.wait_ge(adaG_ev.sem, l + 1)
                k = 0
                for n, kn in enumerate((3, 3, 2)):
                    w = weights(0, 5 + n, (b2 + (5 + n) // NSLOT + 1) * 16)[:, 0:kn * D].rearrange("p (k n) -> p k n", n=D)
                    for kk in range(kn):
                        for half in range(2):
                            for b in range(NB):
                                ins = mm(G[2 * half + b][:, :], mixT[:, k, b * P:(b + 1) * P], w[:, kk, half * 512:(half + 1) * 512], start=(k == 0), stop=(k == KD - 1))
                        k += 1
                    ins.then_inc(used[(5 + n) % NSLOT].sem, 1)
                turn(v + 1, xn, xn_ok, xn_ok.at(v + 1, 2), xn_turned, hT_act, hT_dve)

                def ffn_step(n, i, count):
                    g, up, dn = (sub(i, piece).rearrange("p (k n) -> p k n", n=(FT * P, FT * P, D)[piece]) for piece in range(3))
                    for piece, w in ((0, g), (1, up)):
                        pe.wait_ge(sub_in[i][piece].sem, count * 16)
                        for f in range(FT):
                            pe.wait_ge(fhid_ok.sem, n * FT + (f + 1))
                            for k in range(KD):
                                ins = mm(H4[2 * f + piece][:, 0:SEQ], w[:, k, f * P:(f + 1) * P], hT[:, k, :], start=(k == 0), stop=(k == KD - 1))
                            ins.then_inc(((fg_mm, fu_mm)[piece] if f == 0 else sub_used[i][piece]).sem, 1)
                    pe.wait_ge(sub_in[i][2].sem, count * 16)
                    for f in range(FT):
                        pe.wait_ge(fhid_ok.sem, n * FT + (f + 1 + FT))
                        for half in range(2):
                            for b in range(NB):
                                ins = mm(G[2 * half + b][:, :], ffhid[:, i, f, b * P:(b + 1) * P], dn[:, f, half * 512:(half + 1) * 512], start=False, stop=False, skip_group_check=True)
                    ins.then_inc(sub_used[i][2].sem, 1)

                if l == 0:
                    open_banks()
                    with pe.Fori(0, 5) as it:
                        for i in range(2):
                            ffn_step(it * 2 + i, i, it + 1)
                    ffn_step(10, 0, 6)
                    close_banks(fdn_done)
                else:
                    for b in range(NB):
                        for k in range(KD):
                            ins = mm(S[0][:, b * EXPERTS:(b + 1) * EXPERTS], hT[:, k, b * P:(b + 1) * P], rw[:, k, :], start=(k == 0), stop=(k == KD - 1))
                    ins.then_inc(rt_mm.sem, 1)
                    pe.wait_ge(chosen_ok.sem, 1)
                    mm(S[0][:, 16:24], tri, chosen[:, 0, :], start=True, stop=True)
                    mm(S[0][:, 24:32], ones, chosen[:, 0, :], start=True, stop=False)
                    mm(S[0][:, 24:32], tri, chosen[:, 1, :], start=False, stop=True)
                    mm(S[0][:, 32:40], ones, chosen[:, 0, :], start=True, stop=False)
                    mm(S[0][:, 32:40], ones, chosen[:, 1, :], start=False, stop=True).then_inc(rank_mm.sem, 1)

                    def gate_up(e, it, i, w):
                        pe.wait_ge(ehid_ok.sem, e * ESTEPS + it * 2 + (i + 1))
                        for piece in range(2):
                            wt = sub(i, piece).rearrange("p (k n) -> p k n", n=FT * P)
                            pe.wait_ge(sub_in[i][piece].sem, (e * (ESTEPS // 2) + it + (7 - i)) * 16)
                            if few(w):
                                for k in range(KD):
                                    for f in range(FT):
                                        ins = mm(H4[2 * i + piece][f * FEW:(f + 1) * FEW, 0:P], hTe[:, k, 0:FEW], wt[:, k, f * P:(f + 1) * P], start=(k == 0), stop=(k == KD - 1))
                                ins.then_inc(sub_used[i][piece].sem, 1)
                                continue
                            for f in range(FT):
                                for k in range(KD):
                                    ins = mm(H4[2 * i + piece][:, f * w:(f + 1) * w], wt[:, k, f * P:(f + 1) * P], hTe[:, k, 0:w], start=(k == 0), stop=(k == KD - 1))
                            ins.then_inc(sub_used[i][piece].sem, 1)

                    def down(e, it, i, w):
                        wt = sub(i, 2).rearrange("p (k n) -> p k n", n=D)
                        pe.wait_ge(sub_in[i][2].sem, (e * (ESTEPS // 2) + it + (7 - i)) * 16)
                        pe.wait_ge(ehid_ok.sem, e * ESTEPS + it * 2 + (i + 3))
                        if few(w):
                            pe.transpose(G[2 + i][:, 0:P], emsg[:, i, P:2 * P], ident[:]).then_inc(eh_turned.sem, 1)
                            pe.wait_ge(eh_ok.sem, e * ESTEPS + it * 2 + (i + 1))
                            for f in range(FT):
                                for half in range(2):
                                    ins = mm(G[0][half * FEW:(half + 1) * FEW, :], ehid[:, i, f * FEW:(f + 1) * FEW], wt[:, f, half * 512:(half + 1) * 512], start=False, stop=False, skip_group_check=True)
                            ins.then_inc(sub_used[i][2].sem, 1)
                            return
                        for f in range(FT):
                            for k in range(KD):
                                bank, c0 = tile_at(k, w)
                                ins = mm(G[bank][:, c0:c0 + w], wt[:, f, k * P:(k + 1) * P], ehid[:, i, f * w:(f + 1) * w], start=False, stop=False, skip_group_check=True)
                        ins.then_inc(sub_used[i][2].sem, 1)

                    def expert(e, w):
                        wide = max(w, P)
                        banks = [0] if few(w) else [bank for bank, k0, k1 in tile_banks(w)]
                        pe.wait_ge(sel_ok.sem, e + 1)
                        pe.wait_ge(ehid_ok.sem, e * ESTEPS + 2)
                        for k in range(KD):
                            bank, c0 = tile_at(k, wide)
                            for b in range(NB):
                                ins = mm(H4[bank][:, c0:c0 + wide], xn[:, b, k * P:(k + 1) * P], sel[:, b, 0:wide], start=(b == 0), stop=(b == NB - 1))
                        ins.then_inc(gath_mm.sem, 1)
                        pe.wait_ge(scat_ev.sem, e * 4 + 1)
                        for bank in banks:
                            mm(G[bank][:, 0:2], ident[:], zcol[:], start=True, stop=False, skip_group_check=True)
                        pe.wait_ge(hTe_act.sem, e + 1)
                        pe.wait_ge(hTe_dve.sem, e + 1)
                        gate_up(e, 0, 0, w)
                        with pe.Fori(0, ESTEPS // 2 - 1) as it:
                            gate_up(e, it, 1, w)
                            down(e, it, 0, w)
                            gate_up(e, it + 1, 0, w)
                            down(e, it, 1, w)
                        last = ESTEPS // 2 - 1
                        gate_up(e, last, 1, w)
                        down(e, last, 0, w)
                        down(e, last, 1, w)
                        for bank in banks:
                            ins = mm(G[bank][:, 0:2], ident[:], zcol[:], start=False, stop=True, skip_group_check=True)
                        ins.then_inc(edn_done.sem, 1)
                        pe.wait_ge(selw_ok.sem, e + 1)
                        for j, s0, n in blocks(wide):
                            for b in range(NB):
                                ins = pe.transpose(H4[0][:, j * SEQ + b * P:j * SEQ + (b + 1) * P], selw[:, b, s0:s0 + P], ident[:])
                        ins.then_inc(selT_mm.sem, 1)
                        pe.wait_ge(selT_ok.sem, e + 1)
                        if few(w):
                            pe.sem_inc(ye_mm.sem, 1)
                            pe.wait_ge(ye_dve.sem, e + 1)
                            for half in range(2):
                                r = slice(half * FEW, (half + 1) * FEW)
                                for b in range(NB):
                                    mm(G[2 * half + b][:, :], selT[r, 0, b * P:(b + 1) * P], ye[r, 0, 0:512], start=True, stop=True).then_inc(scat_mm.sem, 1)
                            return
                        pe.sem_inc(eh_turned.sem, ESTEPS)
                        pe.wait_ge(yeT_act.sem, e + 1)
                        pe.wait_ge(yeT_dve.sem, e + 1)
                        for j, s0, n in blocks(w):
                            for k in range(KD):
                                ins = pe.transpose(ye_bank(j, k // 4)[:, k % 4 * P:(k % 4 + 1) * P], yeT[:, k, s0:s0 + P], ident[:])
                        ins.then_inc(ye_mm.sem, 1)
                        pe.wait_ge(ye_dve.sem, e + 1)
                        pe.wait_ge(ye_act.sem, e + 1)
                        nb = blocks(w)
                        for half in range(2):
                            for b in range(NB):
                                for j, s0, n in nb:
                                    ins = mm(G[2 * half + b][:, :], selT[0:n, j, b * P:(b + 1) * P], ye[0:n, j, half * 512:(half + 1) * 512], start=(j == 0), stop=(j == len(nb) - 1))
                                ins.then_inc(scat_mm.sem, 1)

                    pe.wait_ge(counts_ok.sem, 1)
                    each_expert(pe, expert)


def constants():
    def angles(pos, dim, theta):
        inv = np.float32(theta) ** (-np.arange(0, dim, 2, dtype=np.float32) / np.float32(dim))
        return pos.astype(np.float32)[:, None] * inv.astype(np.float32)[None, :]

    def tables(*angs):
        cos = np.concatenate([np.concatenate([np.cos(a), np.cos(a)], 1) for a in angs], 1)
        sin = np.concatenate([np.concatenate([-np.sin(a), np.sin(a)], 1) for a in angs], 1)
        return np.stack([cos, sin], 1).astype(np.float32)

    pos = np.arange(SEQ)
    band = np.zeros((SEQ, 4, SEQ), np.float32)
    for g, w in enumerate(WINDOWS):
        for s in range(SEQ):
            lo, hi = max(s - w // 2, 0), min(s + w // 2, SEQ)
            band[lo:hi, g, s] = 1.0 / (hi - lo)
            band[s, g, s] -= 1.0
    init = [0.8 - 0.6 * math.exp(-0.3 * l) for l in range(DEPTH)]
    return {
        "rope_a": tables(angles(pos // GRID_W, A_DIM // 2, 10000.0), angles(pos % GRID_W, A_DIM // 2, 10000.0)),
        "rope_b": tables(angles(pos, B_ROT, 500000.0)),
        "rope_c": tables(angles(pos, C_ROPE, 10000.0)),
        "lam_init": np.array([[i, 1.0 - i] for i in init], np.float32),
        "band": band,
        "iota8": np.arange(EXPERTS, dtype=np.float32),
        "slots": np.arange(SEQ, dtype=np.float32),
        "before": np.triu(np.ones((P, P), np.float32), 1),
    }


INPUTS = ["x", "ln1_g", "w_in", "a_q_norm", "a_k_norm", "b_lambda", "b_subln", "c_q_norm", "c_kv_norm", "c_w_uq", "c_w_ukv",
          "w_branch", "w_out", "ln2_g", "w_ff1", "w_ff2", "final_g", "c_2", "ada_w_2", "ada_b_2", "mix_norm_g_2",
          "ffn_norm_g_2", "w_in_2", "pool_w_2", "pool_scale_2", "conv_w_2", "conv_b_2", "conv_ln_g_2", "conv_ln_b_2",
          "sgu_ln_g_2", "sgu_ln_b_2", "sgu_w_2", "sgu_b_2", "w_out_2", "ffn_w_gate_2", "ffn_w_up_2", "ffn_w_down_2",
          "router_w_2", "router_b_2", "moe_w_gate_2", "moe_w_up_2", "moe_w_down_2", "final_norm_g_2"]


def kernel(**inputs):
    import concourse.bacc as bacc
    from concourse.bass_utils import run_bass_kernel_spmd as run

    nc = bacc.Bacc("TRN2", target_bir_lowering=False, num_devices=1)
    arrays, t = {}, {}
    given = {name: inputs[name] for name in INPUTS}
    given.update(constants())
    for name, value in given.items():
        a = np.ascontiguousarray(value)
        arrays[f"in_{name}"] = a
        t[name] = nc.dram_tensor(f"in_{name}", a.shape, mybir.dt.from_np(a.dtype), kind="ExternalInput").ap()
    t["out"] = nc.dram_tensor("out_0", (1, SEQ, D), F32, kind="ExternalOutput").ap()
    build(nc, t)
    r = run(nc, [arrays], core_ids=[0])
    return r.results[0]["out_0"]
```
